# Optimizing a Trainium2 kernel written in Bass

```python
import jax, jax.numpy as jnp
from jax import lax
import numpy as np

D_MODEL = 1024
BATCH = 1
SEQ = 512
DEPTH = 2
DEC_BATCH = 8
DEC_SEQ = 16
PAST_LEN = 256

CHUNK = 64
N_EVEN = (DEPTH + 1) // 2
N_ODD = DEPTH // 2
POOL_WINDOWS = (2, 4, 8, 16)
N_POOL_GROUPS = len(POOL_WINDOWS)
D_POOL = D_MODEL // 2
POOL_GROUP = D_POOL // N_POOL_GROUPS
POOL_HIST = max(POOL_WINDOWS) - 1
SG_CHUNK = 128
D_SG = D_MODEL // 2
SG_HEADS = 4
SG_HEAD = D_SG // SG_HEADS
D_IN_EVEN = D_POOL + 2 * D_SG
GLA_HEADS = 4
GLA_DK = D_MODEL // 2 // GLA_HEADS
GLA_DV = D_MODEL // GLA_HEADS
GLA_GATE_RANK = 16
GLA_TAU = 16.0
D_QK = GLA_HEADS * GLA_DK
D_V = GLA_HEADS * GLA_DV
D_IN_ODD = 2 * D_QK + 2 * D_V + GLA_GATE_RANK
D_FF = -(-8 * D_MODEL // (3 * 256)) * 256
EPS = 1e-6

kernel_name = "streaming_pool_sgmlp_gla_hybrid_step"

def rms_norm(x, g):
    xf = x.astype(jnp.float32)
    y = xf * lax.rsqrt(jnp.mean(xf * xf, axis=-1, keepdims=True) + EPS)
    return (y * g.astype(jnp.float32)).astype(x.dtype)

def layer_norm(x, g, b):
    xf = x.astype(jnp.float32)
    mu = jnp.mean(xf, axis=-1, keepdims=True)
    var = jnp.mean(jnp.square(xf - mu), axis=-1, keepdims=True)
    y = (xf - mu) * lax.rsqrt(var + EPS) * g.astype(jnp.float32) + b.astype(jnp.float32)
    return y.astype(x.dtype)

def pool_mixer(a, hist, start, w_pool, pool_scale):
    B, L, _ = a.shape
    full = jnp.concatenate([hist.astype(a.dtype), a], axis=1)
    cs = jnp.cumsum(full.astype(jnp.float32), axis=1)
    cs = jnp.concatenate([jnp.zeros_like(cs[:, :1]), cs], axis=1)
    pos = start + jnp.arange(L)
    hi = cs[:, POOL_HIST + 1:]
    outs = []
    for gi, w in enumerate(POOL_WINDOWS):
        sl = slice(gi * POOL_GROUP, (gi + 1) * POOL_GROUP)
        lo = cs[:, POOL_HIST + 1 - w:POOL_HIST + 1 - w + L, sl]
        cnt = jnp.minimum(w, pos + 1).astype(jnp.float32)
        outs.append((hi[..., sl] - lo) / cnt[None, :, None])
    pooled = jnp.concatenate(outs, axis=-1) - a.astype(jnp.float32)
    pooled = pooled.reshape(B, L, N_POOL_GROUPS, POOL_GROUP)
    y = jnp.einsum('blgc,gcd->blgd', pooled, w_pool.astype(jnp.float32)).reshape(B, L, D_POOL)
    y = y * pool_scale.astype(jnp.float32)
    return y.astype(a.dtype), full[:, -POOL_HIST:]

def spatial_gate(u, v, w_s, b_s):
    B, L, _ = u.shape
    n = max(L // SG_CHUNK, 1)
    c = L // n
    mask = jnp.tril(jnp.ones((c, c), dtype=bool))
    w = jnp.where(mask[None], w_s[:, :c, :c], 0.0)
    vh = v.reshape(B, n, c, SG_HEADS, SG_HEAD)
    mixed = jnp.einsum('hts,bnshd->bnthd', w, vh)
    mixed = mixed + jnp.transpose(b_s[:, :c])[None, None, :, :, None]
    return u * mixed.reshape(B, L, D_SG)

def even_mixer(h, hist, start, w_in, w_pool, pool_scale, ln_v_g, ln_v_b, w_s, b_s, w_out):
    z = h @ w_in
    a = z[..., :D_POOL]
    u = jax.nn.gelu(z[..., D_POOL:D_POOL + D_SG])
    v = layer_norm(jax.nn.gelu(z[..., D_POOL + D_SG:]), ln_v_g, ln_v_b)
    ya, new_hist = pool_mixer(a, hist, start, w_pool, pool_scale)
    yb = spatial_gate(u, v, w_s, b_s)
    y = jnp.concatenate([ya, yb], axis=-1) @ w_out
    return y, new_hist, v

def gla_chunked(q, k, v, log_a, s0):
    B, L, H, _ = q.shape
    c = min(CHUNK, L)
    n = L // c

    def to_blocks(t):
        return t.astype(jnp.float32).reshape(B, n, c, H, -1).transpose(1, 0, 3, 2, 4)

    qc, kc, vc, gc = to_blocks(q), to_blocks(k), to_blocks(v), to_blocks(log_a)
    cum = jnp.cumsum(gc, axis=3)
    mask = jnp.tril(jnp.ones((c, c), dtype=bool))

    def step(s, inp):
        qi, ki, vi, bi = inp
        b_last = bi[:, :, -1:, :]
        q_dec = qi * jnp.exp(bi)
        k_inv = ki * jnp.exp(-bi)
        k_to_end = ki * jnp.exp(b_last - bi)
        att = jnp.where(mask, jnp.einsum('bhik,bhjk->bhij', q_dec, k_inv), 0.0)
        o = jnp.einsum('bhik,bhkv->bhiv', q_dec, s) + jnp.einsum('bhij,bhjv->bhiv', att, vi)
        s_new = jnp.exp(b_last[:, :, 0, :])[..., None] * s + jnp.einsum('bhjk,bhjv->bhkv', k_to_end, vi)
        return s_new, o

    s_fin, o = lax.scan(step, s0.astype(jnp.float32), (qc, kc, vc, cum))
    o = o.transpose(1, 0, 3, 2, 4).reshape(B, L, H, GLA_DV)
    return o.astype(q.dtype), s_fin.astype(s0.dtype)

def gla_mixer(h, s0, w_in, w_gate2, b_gate, g_onorm, w_out):
    B, L, _ = h.shape
    z = h @ w_in
    q = z[..., :D_QK].reshape(B, L, GLA_HEADS, GLA_DK) * (GLA_DK ** -0.5)
    k = z[..., D_QK:2 * D_QK].reshape(B, L, GLA_HEADS, GLA_DK)
    v = z[..., 2 * D_QK:2 * D_QK + D_V].reshape(B, L, GLA_HEADS, GLA_DV)
    r = z[..., 2 * D_QK + D_V:2 * D_QK + 2 * D_V]
    g_lr = z[..., 2 * D_QK + 2 * D_V:]
    log_a = jax.nn.log_sigmoid((g_lr @ w_gate2 + b_gate).astype(jnp.float32)) / GLA_TAU
    o, s_new = gla_chunked(q, k, v, log_a.reshape(B, L, GLA_HEADS, GLA_DK), s0)
    o = rms_norm(o, g_onorm.reshape(GLA_HEADS, GLA_DV)).reshape(B, L, D_V)
    y = (o * jax.nn.silu(r)) @ w_out
    return y, s_new

def swiglu(h, w_gate, w_up, w_down):
    return (jax.nn.silu(h @ w_gate) * (h @ w_up)) @ w_down

def trunk(x, start, pool_hist, gla_state, pre_mix_g, post_mix_g, pre_ffn_g, post_ffn_g,
          w_in_even, w_pool, pool_scale, ln_v_g, ln_v_b, w_s, b_s, w_out_even,
          w_in_odd, w_gate2, b_gate, g_onorm, w_out_odd, w_ffn_gate, w_ffn_up, w_ffn_down):
    new_pool, new_v, new_gla = [], [], []
    for l in range(DEPTH):
        h = rms_norm(x, pre_mix_g[l])
        if l % 2 == 0:
            e = l // 2
            y, hist, v = even_mixer(h, pool_hist[e], start, w_in_even[e], w_pool[e], pool_scale[e],
                                    ln_v_g[e], ln_v_b[e], w_s[e], b_s[e], w_out_even[e])
            new_pool.append(hist)
            new_v.append(v)
        else:
            o = l // 2
            y, s = gla_mixer(h, gla_state[o], w_in_odd[o], w_gate2[o], b_gate[o], g_onorm[o], w_out_odd[o])
            new_gla.append(s)
        x = x + rms_norm(y, post_mix_g[l])
        h = rms_norm(x, pre_ffn_g[l])
        x = x + rms_norm(swiglu(h, w_ffn_gate[l], w_ffn_up[l], w_ffn_down[l]), post_ffn_g[l])
    return x, jnp.stack(new_pool), jnp.stack(new_v), jnp.stack(new_gla)

def setup_inputs(seed: int = 0) -> dict:
    key = jax.random.key(seed)
    ks = jax.random.split(key, 32)
    nrm = lambda k, shape, s: jax.random.normal(k, shape, jnp.float32) * s
    gain = lambda k, shape: 1.0 + 0.05 * jax.random.normal(k, shape, jnp.float32)
    return {
        'x_prompt': nrm(ks[0], (BATCH, SEQ, D_MODEL), 1.0),
        'x_sample': nrm(ks[1], (DEC_BATCH, DEC_SEQ, D_MODEL), 1.0),
        'state_pool': nrm(ks[2], (N_EVEN, DEC_BATCH, POOL_HIST, D_POOL), 1.0),
        'state_gla': nrm(ks[3], (N_ODD, DEC_BATCH, GLA_HEADS, GLA_DK, GLA_DV), 1.0),
        'pre_mix_g': gain(ks[4], (DEPTH, D_MODEL)),
        'post_mix_g': gain(ks[5], (DEPTH, D_MODEL)),
        'pre_ffn_g': gain(ks[6], (DEPTH, D_MODEL)),
        'post_ffn_g': gain(ks[7], (DEPTH, D_MODEL)),
        'w_in_even': nrm(ks[8], (N_EVEN, D_MODEL, D_IN_EVEN), D_MODEL ** -0.5),
        'w_pool': nrm(ks[9], (N_EVEN, N_POOL_GROUPS, POOL_GROUP, POOL_GROUP), POOL_GROUP ** -0.5),
        'pool_scale': 1.0 + 0.1 * jax.random.normal(ks[10], (N_EVEN, D_POOL), jnp.float32),
        'ln_v_g': gain(ks[11], (N_EVEN, D_SG)),
        'ln_v_b': nrm(ks[12], (N_EVEN, D_SG), 0.02),
        'w_s': nrm(ks[13], (N_EVEN, SG_HEADS, SG_CHUNK, SG_CHUNK), SG_CHUNK ** -0.5),
        'b_s': 1.0 + 0.1 * jax.random.normal(ks[14], (N_EVEN, SG_HEADS, SG_CHUNK), jnp.float32),
        'w_out_even': nrm(ks[15], (N_EVEN, D_POOL + D_SG, D_MODEL), (D_POOL + D_SG) ** -0.5),
        'w_in_odd': nrm(ks[16], (N_ODD, D_MODEL, D_IN_ODD), D_MODEL ** -0.5),
        'w_gate2': nrm(ks[17], (N_ODD, GLA_GATE_RANK, D_QK), GLA_GATE_RANK ** -0.5),
        'b_gate': 1.0 + 0.1 * jax.random.normal(ks[18], (N_ODD, D_QK), jnp.float32),
        'g_onorm': gain(ks[19], (N_ODD, D_V)),
        'w_out_odd': nrm(ks[20], (N_ODD, D_V, D_MODEL), D_V ** -0.5),
        'w_ffn_gate': nrm(ks[21], (DEPTH, D_MODEL, D_FF), D_MODEL ** -0.5),
        'w_ffn_up': nrm(ks[22], (DEPTH, D_MODEL, D_FF), D_MODEL ** -0.5),
        'w_ffn_down': nrm(ks[23], (DEPTH, D_FF, D_MODEL), D_FF ** -0.5),
    }

def reference(x_prompt, x_sample, state_pool, state_gla, pre_mix_g, post_mix_g, pre_ffn_g, post_ffn_g,
              w_in_even, w_pool, pool_scale, ln_v_g, ln_v_b, w_s, b_s, w_out_even,
              w_in_odd, w_gate2, b_gate, g_onorm, w_out_odd, w_ffn_gate, w_ffn_up, w_ffn_down):
    weights = (pre_mix_g, post_mix_g, pre_ffn_g, post_ffn_g,
               w_in_even, w_pool, pool_scale, ln_v_g, ln_v_b, w_s, b_s, w_out_even,
               w_in_odd, w_gate2, b_gate, g_onorm, w_out_odd, w_ffn_gate, w_ffn_up, w_ffn_down)
    pool0 = jnp.zeros((N_EVEN, x_prompt.shape[0], POOL_HIST, D_POOL), x_prompt.dtype)
    gla0 = jnp.zeros((N_ODD, x_prompt.shape[0], GLA_HEADS, GLA_DK, GLA_DV), x_prompt.dtype)
    y_prompt, pool_prompt, _, gla_prompt = trunk(x_prompt, 0, pool0, gla0, *weights)
    y_sample, pool_sample, sg_v_sample, gla_sample = trunk(x_sample, PAST_LEN, state_pool, state_gla, *weights)
    return (y_prompt, y_sample, pool_prompt, pool_sample, sg_v_sample, gla_prompt, gla_sample)


_drawn_inputs = setup_inputs


def setup_inputs(seed=0):
    import zlib

    import numpy as np

    out = dict(_drawn_inputs(seed))
    spreads = {}
    factors = {'ln_v_b': 2.879}
    for name, (base, spread) in spreads.items():
        noise = np.random.default_rng([zlib.crc32(name.encode()), seed]).standard_normal(out[name].shape)
        drawn = base * np.exp(spread * noise) if base else spread * noise
        out[name] = __import__('jax').numpy.asarray(drawn.astype(out[name].dtype))
    for name, factor in factors.items():
        out[name] = (out[name] * factor).astype(out[name].dtype)
    return out
```

```python
from contextlib import ExitStack

import concourse.bass as bass
import numpy as np
from concourse import mybir

F32 = mybir.dt.float32
F32R = mybir.dt.float32r
U32 = mybir.dt.uint32
ACT = mybir.ActivationFunctionType
ALU = mybir.AluOpType

P = 128
D = 1024
KB = D // P
PROMPT, STREAMS, STEP = 512, 8, 16
T = PROMPT + STREAMS * STEP
TT = T // P
HALF = T // 2
EPS = 1e-6
WINDOWS = (2, 4, 8, 16)
HIST = 15
SG = 512
HEADS, DK, DV = 4, 128, 256
TAU = 16.0
CHUNK = 64
D_FF = 2816
FF_PARTS = ((0, 4), (8, 4), (16, 3))
UW = 2 * P
CONSTS = 4 * P + 66

PRE_MIX, POST_MIX, PRE_FFN, POST_FFN, POOL_SCALE, O_NORM, ROWS = 0, 16, 32, 48, 64, 68, 76

U_AU, U_V, U_OUT0, U_FF0 = 0, 4, 6, 10
FF_UNITS = sum(2 * n + 4 for _, n in FF_PARTS)
U_QK = U_FF0 + FF_UNITS
U_G = U_QK + 4
U_VV = U_G + 1
U_R = U_VV + 4
U_OUT1 = U_R + 4
U_FF1 = U_OUT1 + 4
UNITS = U_FF1 + FF_UNITS

G_AU, G_OUT0, G_FF0 = 0, 4, 8
G_QK = G_FF0 + FF_UNITS
G_G = G_QK + 4
G_R = G_G + 1
G_OUT1 = G_R + 4
G_FF1 = G_OUT1 + 4


def encoder(nc, a):
    with ExitStack() as ctx:
        base, end = nc.sbuf_base, nc.sbuf_usable_end
        base = (base + 63) // 64 * 64

        def at(name, offset, shape, dt=F32, parts=P):
            size = 4 * int(np.prod(shape))
            assert base + offset + size <= end, (name, base + offset + size, end)
            return nc.alloc_sbuf_tensor_at(name, [parts, *shape], dt, offset=base + offset)

        K20, K10, K5 = 20480, 10240, 5120
        o_x, o_xh, o_xl, o_y, o_hh, o_hl = (i * K20 for i in range(6))
        o_stage = 6 * K20
        o_wh, o_wl = o_stage + 16384, o_stage + 2 * 16384
        o_rs = o_wl + 16384
        o_sq = o_rs + 2560
        o_acc = o_sq + K5
        o_gate = o_acc + K5
        o_up = o_gate + K5
        o_diag = o_up + K5
        o_late = o_diag + 2560
        o_const = o_late + K10

        x = at("x", o_x, [KB, T])
        xh = at("xh", o_xh, [KB, T], F32R)
        xl = at("xl", o_xl, [KB, T], F32R)
        y = at("y", o_y, [KB, T])
        hh = at("hh", o_hh, [KB, T], F32R)
        hl = at("hl", o_hl, [KB, T], F32R)
        stage = at("stage", o_stage, [2, KB * UW])
        wh = at("wh", o_wh, [2, KB, UW], F32R)
        wl = at("wl", o_wl, [2, KB, UW], F32R)
        rs = at("rs", o_rs, [T])
        sq = at("sq", o_sq, [2, T])
        acc = at("acc", o_acc, [2, T])
        gate = at("gate", o_gate, [2, T])
        up = at("up", o_up, [2, T])
        diag = at("diag", o_diag, [TT, P])
        cst = at("cst", o_const, [CONSTS])
        ident = cst[:, 0:P]
        tri = cst[:, P:4 * P].rearrange("p (m t) -> p m t", m=3)
        fix = cst[:, 4 * P:4 * P + 64].rearrange("p (g t) -> p g t", g=4)
        par = cst[:, 4 * P + 64:4 * P + 66]
        ones = at("ones", o_const + 2368, [P])
        gains = at("gains", o_const + 2880, [ROWS])
        small = at("small", o_const + 3200, [130])
        elast = at("elast", o_const + 3744, [HEADS, 2 * STREAMS])
        ss, ms, rstd = small[:, 0:20], small[:, 20:40], small[:, 40:60]
        minus_half = small[:, 60:80]
        rpre = small[:, 80:85]
        bn6, mv, vms, vrstd = small[:, 90:96], small[:, 96:98], small[:, 98:99], small[:, 100:105]
        bend = small[:, 110:126]

        uT = at("uT", o_y, [4, T])
        v = at("v", o_y + K10, [TT, SG])
        xin = at("xin", o_y, [TT, D])
        junk = at("junk", o_hl + 6000 // 32 * 32, [D])
        AW = 16 + PROMPT + STREAMS * 32
        winA = at("winA", o_hh, [4, AW])
        winB = at("winB", o_hh + 4 * 4 * AW, [4, AW])
        winC = at("winC", o_hh + 8 * 4 * AW, [4, AW])
        wsT = at("wsT", o_late, [2, 4, P])
        wpool = at("wpool", o_late + 4096, [4, P])
        lng = at("lng", o_late + 6144, [SG])
        lnb = at("lnb", o_late + 8192, [SG])
        gv = at("gv", o_gate, [2, SG])
        bs = at("bs", o_gate + 4096, [2, 4 * P])
        hist = at("hist", o_sq, [SG])
        a_last = at("a_last", o_sq + 2048, [4, P])
        wsn = at("wsn", o_acc, [2, 4, P])
        rows = at("rows", o_diag, [P])

        qk = at("qk", o_hh, [8, T])
        vv = at("vv", o_hl, [TT, D])
        rT = at("rT", o_y, [KB, T])
        la = at("la", o_y, [TT, SG])
        cum = at("cum", o_gate, [HEADS, T])
        zf = at("zf", o_diag, [T])
        w2 = at("w2", o_late, [SG])
        bg = at("bg", o_late + 2048, [SG])
        kend = at("kend", o_late, [TT, SG])
        ga, gb, gc = (at(f"gt{i}", o_sq + 2048 * i, [SG]) for i in range(3))
        eq = at("eq", o_sq, [T])
        ek = at("ek", o_sq + 2560, [T])
        att = at("att", o_sq, [3, 4 * P])
        km = at("km", o_gate, [2, SG])
        S = at("S", o_xh, [2, HEADS, DV])
        Ss = at("Ss", o_xh + 8192, [HEADS, STREAMS, DV])
        out_t = at("out_t", o_hh, [TT, D])

        ps = ctx.enter_context(nc.psum_tensor("ps", [P, 8, 512], F32))
        flat = ps[:].rearrange("p b n -> p (b n)")

        def f32(t):
            return t.bitcast(F32)

        def banks4(g):
            b = 4 * (g % 2)
            return ps[:, b:b + 4, 0:HALF].rearrange("p (m h) n -> p m h n", m=2)

        def pair(b, n=T):
            return flat[:, 512 * b:512 * b + n]

        def halves(t):
            return t.rearrange("p (h n) -> p h n", h=2)

        def blocks(t, k, n=2):
            return t[:, k:k + n, :].rearrange("p m (h n) -> p m h n", h=2)

        def twice(t):
            return halves(t).unsqueeze(1).broadcast_to([P, 2, 2, HALF])

        def sem(name):
            return ctx.enter_context(nc.semaphore(name))

        w_loaded = [sem("w_loaded0"), sem("w_loaded1")]
        w_hi, w_lo, w_used = sem("w_hi"), sem("w_lo"), sem("w_used")
        acc_empty = sem("acc_empty")
        small_loads, x_loads = sem("small_loads"), sem("x_loads")
        consts_set, zeroed = sem("consts_set"), sem("zeroed")
        dve_step, act_step, pool_step = sem("dve_step"), sem("act_step"), sem("pool_step")
        xh_done, xl_done = sem("xh_done"), sem("xl_done")
        squares, squares_added = sem("squares"), sem("squares_added")
        sums_full, ms_done, rstd_done = sem("sums_full"), sem("ms_done"), sem("rstd_done")
        diag_done, r_full, rs_done = sem("diag_done"), sem("r_full"), sem("rs_done")
        y_scaled, x_added = sem("y_scaled"), sem("x_added")
        x_squares, x_squares_added = sem("x_squares"), sem("x_squares_added")
        rows_full, rows_done, x0_full, x0_done = sem("rows_full"), sem("rows_done"), sem("x0_full"), sem("x0_done")
        ws_full, ws_done, hist_full, hist_done = sem("ws_full"), sem("ws_done"), sem("hist_full"), sem("hist_done")
        x0_sums = sem("x0_sums")
        a_last_done, windows_done, pooled_done, ya_full = sem("a_last_done"), sem("windows_done"), sem("pooled_done"), sem("ya_full")
        u_done, v_full, v_gelu, vms_done = sem("u_done"), sem("v_full"), sem("v_gelu"), sem("vms_done")
        vrstd_done, v_normed, v_done = sem("vrstd_done"), sem("v_normed"), sem("v_done")
        yb_full, yb_done, yb_hi, yb_lo = sem("yb_full"), sem("yb_done"), sem("yb_hi"), sem("yb_lo")
        last_a_full, last_a_done, mixer_stores = sem("last_a_full"), sem("last_a_done"), sem("mixer_stores")
        silu_done, hid_done, hid_hi, hid_lo = sem("silu_done"), sem("hid_done"), sem("hid_hi"), sem("hid_lo")
        w2_zeroed, gate_loads = sem("w2_zeroed"), sem("gate_loads")
        vv_full, vv_done = sem("vv_full"), sem("vv_done")
        gate_full, gx_done, gabs_done, gln_done, la_done = (sem(n) for n in ("gate_full", "gx_done", "gabs_done", "gln_done", "la_done"))
        cum_full, cum_done, bend_done, exps_done = sem("cum_full"), sem("cum_done"), sem("bend_done"), sem("exps_done")
        dist_done, dist_exp, head_done, r_silu = sem("dist_done"), sem("dist_exp"), sem("head_done"), sem("r_silu")
        kt_full, kt_done, cleared, km_done, states_in = (sem(n) for n in ("kt_full", "kt_done", "cleared", "km_done", "states_in"))
        att_full, att_done, kv_full, s_done = sem("att_full"), sem("att_done"), sem("kv_full"), sem("s_done")
        o_full, o_copied, skv_full, ss_done = sem("o_full"), sem("o_copied"), sem("skv_full"), sem("ss_done")
        o_sq, o_added, o_sums, o_ms, o_rstd = (sem(n) for n in ("o_sq", "o_added", "o_sums", "o_ms", "o_rstd"))
        o_diag, o_r, o_gated, state_stores = sem("o_diag"), sem("o_r"), sem("o_gated"), sem("state_stores")
        out_full, out_ready, stores = sem("out_full"), sem("out_ready"), sem("stores")

        SMALL_LOADS = 1 + 6 + 2 + STREAMS + 4
        MIXER_STORES = 1 + STREAMS + 1
        NORM = {"pre0": 0, "post0": 1, "preF0": 2, "postF0": 3, "pre1": 4, "post1": 5, "preF1": 6, "postF1": 7}
        X_IN0, X_OUT0, X_FF0, X_IN1, X_OUT1, X_FF1 = 0, 8, 12, 20, 28, 36
        BOUNDS = (
            dict(n=0, post="post0", pre="preF0", gp=POST_MIX, gq=PRE_FFN, g=G_FF0, x=X_FF0),
            dict(n=1, post="postF0", pre="pre1", gp=POST_FFN, gq=PRE_MIX + 8, g=G_QK, x=X_IN1),
            dict(n=2, post="post1", pre="preF1", gp=POST_MIX + 8, gq=PRE_FFN + 8, g=G_FF1, x=X_FF1),
            dict(n=3, post="postF1", pre=None, gp=POST_FFN + 8, gq=None, g=G_FF1 + FF_UNITS, x=None),
        )

        def f32(t):
            return t.bitcast(F32)

        def banks4(g):
            b = 4 * (g % 2)
            return ps[:, b:b + 4, 0:HALF].rearrange("p (m h) n -> p m h n", m=2)

        def span(b, n=T):
            return flat[:, 512 * b:512 * b + n]

        def halved(t):
            return t.rearrange("p (h n) -> p h n", h=2)

        def two(t, k):
            return t[:, bass.ds(k, 2), :].rearrange("p m (h n) -> p m h n", h=2)

        def rs_twice():
            return halved(rs[:]).unsqueeze(1).broadcast_to([P, 2, 2, HALF])

        def tile(t):
            return slice(t * P, (t + 1) * P)

        def norm_banks(g):
            b = 4 * ((g + 1) % 2)
            return b, b + 2, b + 3

        def gain(row):
            return gains[:, row:row + 1]

        block = ctx.enter_context(nc.Block())

        @block.sync
        def _(sp):
            def load(u, src, wait=True):
                if wait:
                    sp.wait_ge(w_lo, u - 1)
                src = src.rearrange("(k p) c -> p k c", p=P)
                nk, width = src.shape[1:]
                dst = stage[:, u % 2, 0:nk * width].rearrange("p (k c) -> p k c", c=width)
                sp.dma_start(dst, src).then_inc(w_loaded[u % 2], 16)

            def load_loop(u0, pairs, src):
                with sp.Fori(0, pairs) as i:
                    for j in range(2):
                        u = u0 + j
                        sp.wait_ge(w_lo, i * 2 + (u - 1))
                        dst = stage[:, u % 2, :].rearrange("p (k c) -> p k c", c=UW)
                        s = src(i, j).rearrange("(k p) c -> p k c", p=P)
                        sp.dma_start(dst[:, 0:s.shape[1], :], s).then_inc(w_loaded[u % 2], 16)

            def load_ffn(layer, u):
                for f, pairs in FF_PARTS:
                    load_loop(u, pairs, lambda i, j: (a["w_ffn_gate"], a["w_ffn_up"])[j][layer, :, bass.ds(i * UW + f * P, UW)])
                    u += 2 * pairs
                    load_loop(u, 2, lambda i, j: a["w_ffn_down"][layer, f * P:(f + 2 * pairs) * P, bass.ds(i * (2 * UW) + j * UW, UW)])
                    u += 4

            for u in range(U_OUT0):
                load(u, a["w_in_even"][0, :, u * UW:(u + 1) * UW], wait=u >= 2)
            for m in range(4):
                load(U_OUT0 + m, a["w_out_even"][0, :, m * UW:(m + 1) * UW])
            load_ffn(0, U_FF0)
            w_in = a["w_in_odd"][0]
            for j in range(4):
                load(U_QK + j, w_in[:, j * UW:(j + 1) * UW])
            load(U_G, w_in[:, w_in.shape[1] - P:])
            for j in range(8):
                load(U_VV + j, w_in[:, D + j * UW:D + (j + 1) * UW])
            for m in range(4):
                load(U_OUT1 + m, a["w_out_odd"][0, :, m * UW:(m + 1) * UW])
            load_ffn(1, U_FF1)

            for t in range(TT):
                sp.wait_ge(out_ready, t + 1)
                dst = a["y_prompt"][0, tile(t), :] if t < 4 else a["y_sample"].rearrange("b s d -> (b s) d")
                sp.dma_start(dst, out_t[:, t, :]).then_inc(stores, 16)
            sp.wait_ge(stores, 16 * TT)
            sp.wait_ge(mixer_stores, 16 * MIXER_STORES)
            sp.wait_ge(state_stores, 16 * (HEADS + 1))

        @block.tensor
        def _(pe):
            def unit(u, g, mh, ml, nk=KB, ready=None, blocks=2, di=0):
                pe.wait_ge(w_lo, di + (u + 1))
                if g >= 2:
                    pe.wait_ge(acc_empty, di + (g - 1))
                out = banks4(g)
                for k in range(nk):
                    if ready is not None:
                        ready(k)
                    for m in range(blocks):
                        for n, (w, mv_) in enumerate(((wh, mh), (wh, ml), (wl, mh))):
                            wt = w[:, u % 2, k, m * P:(m + 1) * P] if blocks == 2 else \
                                w[:, u % 2, k // 2, (k % 2) * P:(k % 2 + 1) * P]
                            for h in range(2):
                                last = pe.matmul(out[:, m, h, :], wt, mv_[:, k, h * HALF:(h + 1) * HALF],
                                                 start=(k == 0 and n == 0), stop=(k == nk - 1 and n == 2))
                last.then_inc(w_used, 1)

            def frames_unit(u, bank, half, wait=None, event=None):
                pe.wait_ge(w_lo, u + 1)
                for t in range(TT):
                    if wait is not None:
                        wait(t)
                    for k in range(KB):
                        for n, (w, mv_) in enumerate(((wh, xh), (wl, xh), (wh, xl))):
                            last = pe.matmul(ps[:, bank[t], half * UW:(half + 1) * UW], mv_[:, k, tile(t)], w[:, u % 2, k, :],
                                             start=(k == 0 and n == 0), stop=(k == KB - 1 and n == 2))
                    if t == TT - 1:
                        last.then_inc(w_used, 1)
                    elif event is not None:
                        last.then_inc(event, 1)

            def sums(name, bank, parts):
                for t in range(TT):
                    for j in range(parts):
                        last = pe.matmul(ps[:, bank, t:t + 1], acc[:, j, tile(t)], ones[:, 0:1], start=(j == 0), stop=(j == parts - 1))
                last.then_inc(sums_full, 1)

            def spread(name, b):
                pe.wait_ge(diag_done, NORM[name] + 1)
                for h in range(2):
                    last = pe.matmul(ps[:, b + h, 0:HALF], ones[:], diag[:].rearrange("p t n -> p (t n)")[:, h * HALF:(h + 1) * HALF],
                                     start=True, stop=True)
                last.then_inc(r_full, 1)

            def boundary(B, first_unit):
                b, behind, ahead = norm_banks(B["g"])
                pe.wait_ge(acc_empty, B["g"])
                pe.wait_ge(squares_added, 4 * (B["n"] + 1))
                sums(B["post"], behind, 2)
                spread(B["post"], b)
                if B["pre"] is None:
                    return
                first_unit(lambda k: pe.wait_ge(xl_done, B["x"] + k + 1))
                pe.wait_ge(x_squares_added, 8 * (B["n"] + 1))
                sums(B["pre"], ahead, 1)
                spread(B["pre"], b)
                pe.wait_ge(rs_done, 2 + B["n"])

            def ffn(u, g, pair):
                for n, (f, pairs) in enumerate(FF_PARTS):
                    if n == 0:
                        unit(u + 1, g + 1, xh, xl)
                    with pe.Fori(1 if n == 0 else 0, pairs) as i:
                        for j in range(2):
                            unit(u + j, g + j, xh, xl, di=i * 2)
                    u, g = u + 2 * pairs, g + 2 * pairs

                    def ready(k):
                        if k % 2 == 0:
                            pe.wait_ge(hid_lo, pair + k // 2 + 1)
                    with pe.Fori(0, 2) as i:
                        for j in range(2):
                            unit(u + j, g + j, hh, hl, nk=2 * pairs, ready=ready, di=i * 2)
                    u, g, pair = u + 4, g + 4, pair + pairs

            pe.wait_ge(small_loads, 16 * SMALL_LOADS)
            pe.wait_ge(consts_set, 2)
            pe.wait_ge(zeroed, 1)
            pe.transpose(ps[:, 7, 0:ROWS], rows[0:ROWS, :], ident[0:ROWS, 0:ROWS]).then_inc(rows_full, 1)
            for n in range(2):
                for h in range(4):
                    last = pe.transpose(ps[:, 5 + n, tile(h)], wsn[:, n, h, :], ident)
                last.then_inc(ws_full, 1)
            for h in range(4):
                last = pe.transpose(ps[:, 4, h * P:h * P + STREAMS * HIST], hist[0:STREAMS * HIST, tile(h)], ident[0:STREAMS * HIST, 0:STREAMS * HIST])
            last.then_inc(hist_full, 1)
            pe.wait_ge(x_loads, 16 * TT)
            for k in range(KB):
                if k >= 2:
                    pe.wait_ge(x0_done, k - 1)
                for t in range(TT):
                    last = pe.transpose(span(2 * (k % 2))[:, tile(t)], xin[:, t, tile(k)], ident)
                last.then_inc(x0_full, 1)
            pe.wait_ge(ws_done, 2)
            spread("pre0", 5)

            pe.wait_ge(x0_done, 8)
            for u in range(4):
                if u == 1:
                    pe.wait_ge(rs_done, 1)
                    pe.wait_ge(hist_done, 1)
                    pe.wait_ge(rows_done, 1)
                unit(u, u, xh, xl, ready=(lambda k: pe.wait_ge(xl_done, k + 1)) if u == 0 else None)
            pe.wait_ge(acc_empty, 3)

            def v_wait(t):
                if t == 4:
                    pe.wait_ge(acc_empty, 4)
            frames_unit(U_V, range(5), 0, wait=v_wait)
            frames_unit(U_V + 1, range(5), 1, event=v_full)
            for gr, b in enumerate((6, 4, 0, 2)):
                pe.wait_ge(pooled_done, 2 * gr + 2)
                pe.wait_ge(v_gelu, (1, 5, 5, 5)[gr])
                res = (winB, winC)[gr % 2]
                pe.matmul(span(b)[:, 0:PROMPT], wpool[:, gr, :], res[:, gr, 16:16 + PROMPT], start=True, stop=True)
                pe.matmul(span(b)[:, PROMPT:T], wpool[:, gr, :],
                          res[:, gr, 16 + PROMPT:].rearrange("p (b s) -> p b s", s=32)[:, :, 16:], start=True, stop=True).then_inc(ya_full, 1)
            for t, b in enumerate((6, 7, 4, 5, 0)):
                pe.wait_ge(v_done, t + 1)
                pe.wait_ge(xl_done, X_OUT0 + (1, 1, 2, 2, 3)[t])
                n = int(t == 4)
                for h in range(4):
                    pe.matmul(ps[:, b, tile(h)], v[:, t, tile(h)], wsT[:, n, h, :], start=True, stop=False)
                    last = pe.matmul(ps[:, b, tile(h)], ones[0:1, :], bs[0:1, n, tile(h)], start=False, stop=True)
                last.then_inc(yb_full, 1)
            pe.wait_ge(xl_done, X_OUT0 + 4)
            pe.wait_ge(a_last_done, 1)
            for gr in range(4):
                pe.transpose(ps[0:HIST, 1, tile(gr)], winA[:, gr, 1 + PROMPT:16 + PROMPT], ident)
                last = pe.transpose(ps[:, 2, tile(gr)], a_last[:, gr, :], ident)
            last.then_inc(last_a_full, 1)
            pe.wait_ge(yb_lo, TT)
            pe.wait_ge(last_a_done, 2)
            for m in range(4):
                unit(U_OUT0 + m, G_OUT0 + m, xh, xl)
            boundary(BOUNDS[0], lambda ready: unit(U_FF0, G_FF0, xh, xl, ready=ready))
            ffn(U_FF0, G_FF0, 0)
            boundary(BOUNDS[1], lambda ready: unit(U_QK, G_QK, xh, xl, ready=ready))

            for j in range(1, 4):
                unit(U_QK + j, G_QK + j, xh, xl)
            unit(U_G, G_G, xh, xl, blocks=1)

            def vv_wait(waits):
                return lambda t: [pe.wait_ge(s, n) for s, n in waits[t]]
            QK_OUT = (acc_empty, G_QK + 4)
            frames_unit(U_VV, (4, 5, 6, 7, 2), 0, wait=vv_wait([[QK_OUT], [], [], [], []]))
            frames_unit(U_VV + 1, (4, 5, 6, 7, 2), 1, event=vv_full)
            pe.wait_ge(acc_empty, G_G + 1)
            pe.wait_ge(gate_loads, 32)
            for t, b in enumerate((0, 1, 3, 4, 5)):
                if t >= 3:
                    pe.wait_ge(vv_done, t - 2)
                pe.matmul(ps[:, b, :], zf[:, tile(t)], w2[:], start=True, stop=True).then_inc(gate_full, 1)
            banks = (6, 7, 2, 0, 1)
            waits = [[(vv_done, 3)], [(vv_done, 4)], [(vv_done, 5)], [(gx_done, 1)], [(gx_done, 2)]]
            frames_unit(U_VV + 2, banks, 0, wait=vv_wait(waits))
            frames_unit(U_VV + 3, banks, 1, event=vv_full)
            pe.wait_ge(la_done, TT)
            for h, (b, s, n) in enumerate(((4, gx_done, 5), (6, vv_done, 7), (2, vv_done, 8), (0, vv_done, 10))):
                pe.wait_ge(s, n)
                for t in range(TT):
                    last = pe.matmul(span(b)[:, tile(t)], la[:, t, tile(h)], tri[:, 1 if t < 4 else 2, :], start=True, stop=True)
                last.then_inc(cum_full, 1)
            for j in range(4):
                pe.wait_ge(cum_done, 2 if j == 0 else 4)
                unit(U_R + j, G_R + j, xh, xl)
            for h in range(HEADS):
                pe.wait_ge(acc_empty, G_R + 4)
                pe.wait_ge(head_done, h + 1)
                for t in range(TT):
                    last = pe.transpose(span(2 * h)[:, tile(t)], cum[:, h, tile(t)], ident)
                last.then_inc(kt_full, 1)
            pe.wait_ge(kt_done, 4)
            pe.wait_ge(cleared, 2)
            for t in range(PROMPT // P):
                if t >= 2:
                    pe.wait_ge(att_done, t - 1)
                for h in range(HEADS):
                    last = pe.matmul(ps[:, t % 2, tile(h)], qk[:, 4 + h, tile(t)], qk[:, h, tile(t)], start=True, stop=True)
                last.then_inc(att_full, 1)
                for odd in range(2):
                    c, r0 = 2 * t + odd, CHUNK * odd
                    if c >= 2:
                        pe.wait_ge(s_done, c - 1)
                    for h in range(HEADS):
                        last = pe.matmul(span(2 + 2 * odd, D)[:, h * DV:(h + 1) * DV], kend[r0:r0 + CHUNK, t, tile(h)],
                                         vv[r0:r0 + CHUNK, t, h * DV:(h + 1) * DV], start=True, stop=True)
                    last.then_inc(kv_full, 1)
                    pe.wait_ge(att_done, t + 1)
                    if c:
                        pe.wait_ge(s_done, c)
                    if c >= 2:
                        pe.wait_ge(o_copied, c - 1)
                    for vb in range(2):
                        for h in range(HEADS):
                            out = ps[:, 6 + odd, (vb * HEADS + h) * CHUNK:(vb * HEADS + h + 1) * CHUNK]
                            pe.matmul(out, S[:, odd, h, tile(vb)], qk[:, h, c * CHUNK:(c + 1) * CHUNK], start=True, stop=False)
                            last = pe.matmul(out, vv[:, t, h * DV + vb * P:h * DV + (vb + 1) * P],
                                             att[:, t % 2, h * P + r0:h * P + r0 + CHUNK], start=False, stop=True)
                    last.then_inc(o_full, 1)
            pe.wait_ge(att_done, 3)
            for h in range(HEADS):
                last = pe.matmul(ps[:, 0, tile(h)], qk[:, 4 + h, tile(4)], qk[:, h, tile(4)], start=True, stop=True)
            last.then_inc(att_full, 1)
            pe.wait_ge(att_done, 5)
            pe.wait_ge(states_in, 16 * HEADS)
            pe.wait_ge(o_copied, 8)
            for vb in range(2):
                for h in range(HEADS):
                    out = span(6, D)[:, tile(vb * HEADS + h)]
                    pe.matmul(out, vv[:, 4, h * DV + vb * P:h * DV + (vb + 1) * P], att[:, 2, tile(h)],
                              start=True, stop=False, skip_group_check=True)
                    for b in range(STREAMS):
                        last = pe.matmul(out[:, b * STEP:(b + 1) * STEP], Ss[:, h, b, tile(vb)],
                                         qk[:, h, PROMPT + b * STEP:PROMPT + (b + 1) * STEP], start=False, stop=(b == STREAMS - 1),
                                         skip_group_check=True)
            last.then_inc(o_full, 1)
            pe.wait_ge(km_done, 2)
            pe.wait_ge(s_done, 8)
            for n in range(4 * HEADS):
                h, q = divmod(n, 4)
                if n >= 4:
                    pe.wait_ge(ss_done, 2 * (n - 3))
                rows_ = slice(32 * q, 32 * q + 32)
                for odd in range(2):
                    last = pe.matmul(ps[:, 2 + n % 4, odd * DV:(odd + 1) * DV], km[rows_, odd, tile(h)],
                                     vv[rows_, 4, h * DV:(h + 1) * DV], start=True, stop=True)
                last.then_inc(skv_full, 1)
            for h in range(HEADS):
                pe.wait_ge(o_added, h + 1)
                for t in range(TT):
                    last = pe.matmul(ps[:, 0, h * TT + t:h * TT + t + 1], acc[:, h % 2, tile(t)], ones[:, 0:1], start=True, stop=True)
                last.then_inc(o_sums, 1)
            pe.wait_ge(ss_done, 8 * HEADS)
            for h in range(HEADS):
                pe.wait_ge(o_diag, h + 1)
                if h >= 2:
                    pe.wait_ge(o_gated, 4 * (h - 1))
                for n in range(2):
                    last = pe.matmul(ps[:, 2 * (h % 2) + n, 0:HALF], ones[:], diag[:].rearrange("p t n -> p (t n)")[:, n * HALF:(n + 1) * HALF],
                                     start=True, stop=True)
                last.then_inc(o_r, 1)
            pe.wait_ge(o_copied, 9)
            for m in range(4):
                if m == 1:
                    pe.wait_ge(o_gated, 4 * HEADS)
                unit(U_OUT1 + m, G_OUT1 + m, xh, xl, ready=(lambda k: pe.wait_ge(xl_done, X_OUT1 + k + 1)) if m == 0 else None)
            boundary(BOUNDS[2], lambda ready: unit(U_FF1, G_FF1, xh, xl, ready=ready))
            ffn(U_FF1, G_FF1, sum(n for _, n in FF_PARTS))
            boundary(BOUNDS[3], None)
            for t in range(TT):
                b = norm_banks(BOUNDS[3]["g"])[0]
                b = (b + 4 + 2 * (t % 2)) % 8
                if t >= 2:
                    pe.wait_ge(out_ready, t - 1)
                for k in range(KB):
                    pe.wait_ge(x_added, 3 * KB + KB)
                    last = pe.transpose(span(b, D)[:, tile(k)], x[:, k, tile(t)], ident)
                last.then_inc(out_full, 1)

        @block.vector
        def _(dve):
            steps = [0]

            def step(ins, n=1):
                steps[0] += n
                ins.then_inc(dve_step, 1)
                dve.wait_ge(dve_step, steps[0])

            def lo(u, di=0):
                dve.wait_ge(w_hi, di + (u + 1))
                s = u % 2
                dve.tensor_tensor(wl[:, s].rearrange("p k c -> p (k c)"), stage[:, s, :],
                                  f32(wh[:, s].rearrange("p k c -> p (k c)")), ALU.subtract).then_inc(w_lo, 1)

            def scaled(dst, u, g, di=0):
                dve.wait_ge(w_used, di + (u + 1))
                dve.tensor_tensor(dst, banks4(g), rs_twice(), ALU.mult).then_inc(acc_empty, 1)

            def norm(name, bank, width=D):
                n = NORM[name]
                if bank is not None:
                    dve.wait_ge(sums_full, (0, 1, 2, 3, 4, 5, 6, 7)[n])
                    src = ps[:, bank, 0:TT]
                else:
                    dve.wait_ge(x0_sums, TT)
                    src = ss[:, 0:TT]
                dve.tensor_scalar(ms[:, 0:TT], src, 1.0 / width, EPS, ALU.mult, ALU.add).then_inc(ms_done, 1)
                dve.wait_ge(rstd_done, n + 1)
                dve.tensor_tensor(diag[:], ident.unsqueeze(1).broadcast_to([P, TT, P]),
                                  rstd_of(name).unsqueeze(2).broadcast_to([P, TT, P]), ALU.mult).then_inc(diag_done, 1)

            def x_lo(k, row, n):
                dve.wait_ge(xh_done, n + 1)
                dve.scalar_tensor_tensor(xl[:, k, :], x[:, k, :], gain(row + k), f32(xh[:, k, :]), ALU.mult, ALU.subtract).then_inc(xl_done, 1)

            def y_out(u, g, m, add, di=0):
                dve.wait_ge(w_used, di + (u + 1))
                if add:
                    dve.tensor_tensor(two(y, m), two(y, m), banks4(g), ALU.add).then_inc(acc_empty, 1)
                else:
                    dve.tensor_copy(two(y, m), banks4(g)).then_inc(acc_empty, 1)

            def square_add(n):
                dve.wait_ge(squares, n + 1)
                if n % 4 == 0:
                    dve.tensor_copy(acc[:], sq[:]).then_inc(squares_added, 1)
                else:
                    dve.wait_ge(squares_added, n)
                    dve.tensor_tensor(acc[:], acc[:], sq[:], ALU.add).then_inc(squares_added, 1)

            def boundary(B):
                b, behind, ahead = norm_banks(B["g"])
                norm(B["post"], behind)
                dve.wait_ge(r_full, NORM[B["post"]] + 1)
                r = ps[:, b:b + 2, 0:HALF]
                for k in range(KB + 1):
                    if k < KB:
                        dve.scalar_tensor_tensor(halved(y[:, k, :]), halved(y[:, k, :]), gain(B["gp"] + k), r, ALU.mult, ALU.mult).then_inc(y_scaled, 1)
                    if k and B["pre"]:
                        x_lo(k - 1, B["gq"], B["x"] + k - 1)
                if B["pre"]:
                    norm(B["pre"], ahead)
                    dve.wait_ge(rs_done, 2 + B["n"])

            def ffn(u, g, pair, b, final):
                for n, (f, pairs) in enumerate(FF_PARTS):
                    with dve.Fori(0, pairs) as i:
                        scaled(two(gate, 0), u, g, di=i * 2)
                        lo(u + 2, di=i * 2)
                        scaled(two(up, 0), u + 1, g + 1, di=i * 2)
                        dve.wait_ge(silu_done, i + (pair + 1))
                        dve.wait_ge(acc_empty, i * 2 + (g + 2))
                        dve.tensor_tensor(up[:], up[:], gate[:], ALU.mult).then_inc(hid_done, 1)
                        lo(u + 3, di=i * 2)
                        dve.wait_ge(hid_hi, i + (pair + 1))
                        dve.tensor_tensor(hl[:, bass.ds(i * 2, 2), :], up[:], f32(hh[:, bass.ds(i * 2, 2), :]), ALU.subtract).then_inc(hid_lo, 1)
                        dve.wait_ge(hid_lo, i + (pair + 1))

                    u, g, pair = u + 2 * pairs, g + 2 * pairs, pair + pairs
                    if n < len(FF_PARTS) - 1:
                        with dve.Fori(0, 2) as i:
                            for j in range(2):
                                if n:
                                    dve.wait_ge(acc_empty, i * 2 + (g + j))
                                y_out(u + j, g + j, i * 4 + 2 * j, n > 0, di=i * 2)
                                lo(u + j + 2, di=i * 2)
                    else:
                        for m in range(4):
                            y_out(u + m, g + m, 2 * m, True)
                            if u + m + 2 < UNITS:
                                lo(u + m + 2)
                            square_add(4 * b + m)
                    u, g = u + 4, g + 4

            def rstd_of(name):
                return (rpre if name.startswith("pre") else rstd[:, 0:TT])

            dve.memset(ones[:], 1.0).then_inc(consts_set, 1)
            dve.memset(minus_half, -0.5).then_inc(consts_set, 1)
            dve.wait_ge(rows_full, 1)
            dve.tensor_copy(gains[:], ps[:, 7, 0:ROWS]).then_inc(rows_done, 1)
            dve.wait_ge(small_loads, 16 * SMALL_LOADS)
            for n in range(2):
                dve.wait_ge(ws_full, n + 1)
                dve.tensor_tensor(wsT[:, n], ps[:, 5 + n, :].rearrange("p (h t) -> p h t", h=4),
                                  tri[:, 2 * n:2 * n + 1, :].broadcast_to([P, 4, P]), ALU.mult).then_inc(ws_done, 1)
            dve.tensor_copy(bs[0:1, 1, :].rearrange("p (h b s) -> p h b s", h=4, s=STEP),
                            bs[0:1, 0, :].rearrange("p (h t) -> p h t", h=4)[:, :, 0:STEP].unsqueeze(2).broadcast_to([1, 4, STREAMS, STEP]))
            dve.wait_ge(hist_full, 1)
            dve.wait_ge(zeroed, 3)
            dve.tensor_copy(winA[:, :, 16 + PROMPT:].rearrange("p g (b s) -> p g b s", s=32)[:, :, :, 1:16],
                            ps[:, 4, :].rearrange("p (g n) -> p g n", g=4)[:, :, 0:STREAMS * HIST].rearrange("p g (b s) -> p g b s", s=HIST)).then_inc(hist_done, 1)
            lo(0)
            for k in range(KB):
                dve.wait_ge(x0_full, k + 1)
                dve.tensor_copy(x[:, k, :], span(2 * (k % 2))).then_inc(x0_done, 1)
                if k == 4:
                    lo(1)
                if k == 6:
                    norm("pre0", None)
                if k:
                    x_lo(k - 1, PRE_MIX, X_IN0 + k - 1)
            x_lo(KB - 1, PRE_MIX, X_IN0 + KB - 1)

            dve.wait_ge(rs_done, 1)
            stream_r = rs[:, PROMPT:].rearrange("p (b s) -> p b s", s=STEP)
            for u in range(4):
                if u < 2:
                    dve.wait_ge(w_used, u + 1)
                    src = banks4(u)
                    dst = winA[:, 2 * u:2 * u + 2, :]
                    n = PROMPT - HALF
                    dve.tensor_tensor(dst[:, :, 16:16 + HALF], src[:, :, 0, :], rs[:, 0:HALF].unsqueeze(1).broadcast_to([P, 2, HALF]), ALU.mult)
                    dve.tensor_tensor(dst[:, :, 16 + HALF:16 + PROMPT], src[:, :, 1, 0:n],
                                      rs[:, HALF:PROMPT].unsqueeze(1).broadcast_to([P, 2, n]), ALU.mult)
                    for m in range(2):
                        last = dve.tensor_tensor(dst[:, m, 16 + PROMPT:].rearrange("p (b s) -> p b s", s=32)[:, :, 16:],
                                                 src[:, m, 1, n:].rearrange("p (b s) -> p b s", s=STEP), stream_r, ALU.mult)
                    last.then_inc(acc_empty, 1)
                else:
                    dve.wait_ge(x0_sums, TT)
                    scaled(two(uT, 2 * (u - 2)), u, u)
                lo(u + 2)
            dve.wait_ge(windows_done, 1)
            for gr, w in enumerate(WINDOWS):
                s = (winB, winC)[gr % 2][:, gr, :]
                own = winA[:, gr, :]
                dve.scalar_tensor_tensor(s[:, 16:16 + PROMPT], s[:, 16:16 + PROMPT], 1.0 / w, own[:, 16:16 + PROMPT], ALU.mult, ALU.subtract).then_inc(pooled_done, 1)
                s, own = (t_[:, 16 + PROMPT:].rearrange("p (b s) -> p b s", s=32)[:, :, 16:] for t_ in (s, own))
                dve.scalar_tensor_tensor(s, s, 1.0 / w, own, ALU.mult, ALU.subtract).then_inc(pooled_done, 1)
            lo(U_OUT0)
            for t in range(TT):
                dve.wait_ge(v_gelu, t + 1)
                step(dve.bn_stats(bn6, gv[:, t % 2, :]))
                step(dve.bn_aggr(mv, bn6))
                dve.tensor_scalar(vms, mv[:, 1:2], EPS, None, ALU.add).then_inc(vms_done, 1)
                dve.wait_ge(vrstd_done, t + 1)
                dve.tensor_scalar(v[:, t, :], gv[:, t % 2, :], mv[:, 0:1], vrstd[:, t:t + 1], ALU.subtract, ALU.mult).then_inc(v_normed, 1)
            lo(U_OUT0 + 1)
            for gr, b in enumerate((6, 4, 0, 2)):
                dve.wait_ge(xh_done, X_OUT0 + gr + 1)
                dve.scalar_tensor_tensor(xl[:, gr, :], span(b), gain(POOL_SCALE + gr), f32(xh[:, gr, :]), ALU.mult, ALU.subtract).then_inc(xl_done, 1)
            dve.wait_ge(u_done, 2)
            for t, b in enumerate((6, 7, 4, 5, 0)):
                dve.wait_ge(yb_full, t + 1)
                dve.tensor_tensor(uT[:, :, tile(t)], ps[:, b, :].rearrange("p (h t) -> p h t", h=4), uT[:, :, tile(t)], ALU.mult).then_inc(yb_done, 1)
                dve.wait_ge(yb_hi, t + 1)
                dve.tensor_tensor(xl[:, 4:8, tile(t)], uT[:, :, tile(t)], f32(xh[:, 4:8, tile(t)]), ALU.subtract).then_inc(yb_lo, 1)
            dve.wait_ge(mixer_stores, 16 * MIXER_STORES)
            for m in range(4):
                y_out(U_OUT0 + m, G_OUT0 + m, 2 * m, False)
                lo(U_OUT0 + m + 2)
                square_add(m)
            boundary(BOUNDS[0])
            ffn(U_FF0, G_FF0, 0, 1, False)
            boundary(BOUNDS[1])

            for j in range(4):
                scaled(two(qk, 2 * j), U_QK + j, G_QK + j)
                lo(U_QK + j + 2)
            dve.wait_ge(w_used, U_G + 1)
            dve.tensor_tensor(halved(zf[:]), banks4(G_G)[:, 0], halved(rs[:]), ALU.mult).then_inc(acc_empty, 1)
            lo(U_G + 2)
            lo(U_VV + 2)
            lo(U_VV + 3)
            for t, b in enumerate((0, 1, 3, 4, 5)):
                dve.wait_ge(gate_full, t + 1)
                dve.tensor_tensor(ga[:], ps[:, b, :], bg[:], ALU.add).then_inc(gx_done, 1)
                dve.wait_ge(gx_done, t + 1)
                step(dve.tensor_scalar(gc[:], ga[:], 0.0, None, ALU.min))
                dve.scalar_tensor_tensor(gb[:], gc[:], -2.0, ga[:], ALU.mult, ALU.add).then_inc(gabs_done, 1)
                dve.wait_ge(gln_done, t + 1)
                dve.tensor_tensor(la[:, t, :], gc[:], gb[:], ALU.subtract).then_inc(la_done, 1)
            lo(U_VV + 4)
            lo(U_VV + 5)
            for h in range(HEADS):
                scaled(two(rT, 2 * h), U_R + h, G_R + h)
                lo(U_R + h + 2)
                dve.wait_ge(cum_done, h + 1)
                ends = bend.rearrange("p (n c) -> p n c", n=2)
                c = cum[:, h, :]
                prompt = c[:, 0:PROMPT].rearrange("p (c s) -> p c s", s=CHUNK)
                streams = c[:, PROMPT:].rearrange("p (b s) -> p b s", s=STEP)
                dve.tensor_copy(ends[:, 0, :].unsqueeze(2), prompt[:, :, CHUNK - 1:])
                dve.tensor_copy(ends[:, 1, :].unsqueeze(2), streams[:, :, STEP - 1:]).then_inc(bend_done, 1)
                dve.wait_ge(bend_done, h + 1)
                dve.wait_ge(exps_done, h + 1)
                dve.tensor_tensor(prompt, ends[:, 0, :].unsqueeze(2).broadcast_to([P, 8, CHUNK]), prompt, ALU.subtract)
                dve.tensor_tensor(streams, ends[:, 1, :].unsqueeze(2).broadcast_to([P, 8, STEP]), streams, ALU.subtract).then_inc(dist_done, 1)
                dve.scalar_tensor_tensor(qk[:, h, :], qk[:, h, :], DK ** -0.5, eq[:], ALU.mult, ALU.mult)
                dve.wait_ge(dist_exp, h + 1)
                dve.tensor_tensor(c, c, qk[:, 4 + h, :], ALU.mult)
                dve.tensor_tensor(qk[:, 4 + h, :], qk[:, 4 + h, :], ek[:], ALU.mult).then_inc(head_done, 1)
            dve.wait_ge(cleared, 2)

            def masked(t, slot, mask):
                dve.wait_ge(att_full, t + 1)
                dve.copy_predicated(att[:, slot, :].rearrange("p (h t) -> p h t", h=HEADS),
                                    tri[:, mask:mask + 1, :].bitcast(U32).broadcast_to([P, HEADS, P]),
                                    ps[:, t % 2, :].rearrange("p (h t) -> p h t", h=HEADS)).then_inc(att_done, 1)
            for t in range(PROMPT // P):
                if t >= 2:
                    dve.wait_ge(o_full, 2 * t - 2)
                masked(t, t % 2, 1)
                for odd in range(2):
                    c = 2 * t + odd
                    dve.wait_ge(kv_full, c + 1)
                    if c:
                        dve.wait_ge(o_full, c)
                        dve.wait_ge(s_done, c)
                    for h in range(HEADS):
                        last = dve.scalar_tensor_tensor(S[:, 1 - odd, h, :], S[:, odd, h, :], elast[:, h, c:c + 1],
                                                        span(2 + 2 * odd, D)[:, h * DV:(h + 1) * DV], ALU.mult, ALU.add)
                    last.then_inc(s_done, 1)
            masked(4, 2, 2)
            dve.wait_ge(o_full, 9)
            for n in range(4 * HEADS):
                h, q = divmod(n, 4)
                dve.wait_ge(skv_full, n + 1)
                for odd in range(2):
                    b = 2 * q + odd
                    dve.scalar_tensor_tensor(Ss[:, h, b, :], Ss[:, h, b, :], elast[:, h, STREAMS + b:STREAMS + b + 1],
                                             ps[:, 2 + n % 4, odd * DV:(odd + 1) * DV], ALU.mult, ALU.add).then_inc(ss_done, 1)
            for h in range(HEADS):
                dve.wait_ge(o_sq, h + 1)
                if h >= 2:
                    dve.wait_ge(o_sums, h - 1)
                dve.tensor_tensor(acc[:, h % 2, :], sq[:, 0, :], sq[:, 1, :], ALU.add).then_inc(o_added, 1)
            dve.wait_ge(o_sums, HEADS)
            dve.tensor_scalar(ms, ps[:, 0, 0:20], 1.0 / DV, EPS, ALU.mult, ALU.add).then_inc(o_ms, 1)
            dve.wait_ge(o_rstd, 1)
            dve.wait_ge(r_silu, 4)
            for h in range(HEADS):
                if h:
                    dve.wait_ge(o_r, h)
                dve.tensor_tensor(diag[:], ident.unsqueeze(1).broadcast_to([P, TT, P]),
                                  rstd[:, h * TT:(h + 1) * TT].unsqueeze(2).broadcast_to([P, TT, P]), ALU.mult).then_inc(o_diag, 1)
                dve.wait_ge(o_r, h + 1)
                b = 2 * (h % 2)
                for vb in range(2):
                    k = 2 * h + vb
                    o = qk[:, vb * HEADS + h, :]
                    dve.tensor_tensor(halved(o), halved(o), ps[:, b:b + 2, 0:HALF], ALU.mult).then_inc(o_gated, 1)
                    dve.wait_ge(o_gated, 2 * k + 1)
                    dve.scalar_tensor_tensor(o, o, gain(O_NORM + k), rT[:, k, :], ALU.mult, ALU.mult).then_inc(o_gated, 1)
                    dve.wait_ge(xh_done, X_OUT1 + k + 1)
                    dve.tensor_tensor(xl[:, k, :], o, f32(xh[:, k, :]), ALU.subtract).then_inc(xl_done, 1)
            for m in range(4):
                y_out(U_OUT1 + m, G_OUT1 + m, 2 * m, False)
                lo(U_OUT1 + m + 2)
                square_add(8 + m)
            boundary(BOUNDS[2])
            ffn(U_FF1, G_FF1, 11, 3, True)
            boundary(BOUNDS[3])
            for t in range(TT):
                dve.wait_ge(out_full, t + 1)
                b = (norm_banks(BOUNDS[3]["g"])[0] + 4 + 2 * (t % 2)) % 8
                dve.tensor_copy(out_t[:, t, :], span(b, D)).then_inc(out_ready, 1)

        @block.scalar
        def _(act):
            def hi(u, di=0):
                s = u % 2
                n = di * 8 if not isinstance(di, int) else 0
                act.wait_ge(w_loaded[s], n + 16 * (u // 2 + 1))
                if u >= 2:
                    act.wait_ge(w_used, di + (u - 1))
                act.activation(wh[:, s].rearrange("p k c -> p (k c)"), stage[:, s, :], ACT.Copy).then_inc(w_hi, 1)

            def x_hi(k, row):
                act.activation(xh[:, k, :], x[:, k, :], ACT.Copy, scale=gain(row + k)).then_inc(xh_done, 1)

            def square(m, n, g):
                act.wait_ge(acc_empty, g + 1)
                if n:
                    act.wait_ge(squares_added, n)
                act.activation(sq[:], y[:, 2 * m:2 * m + 2, :], ACT.Square).then_inc(squares, 1)

            def rs_copy(n, b):
                act.wait_ge(r_full, n + 1)
                act.activation(halved(rs[:]), ps[:, b:b + 2, 0:HALF], ACT.Copy).then_inc(rs_done, 1)

            def boundary(B):
                for k in range(KB):
                    act.wait_ge(x_added, KB * B["n"] + k + 1)
                    if B["pre"] is None:
                        continue
                    if k == 0 and B["x"] == X_IN1:
                        pass
                    x_hi(k, B["gq"])
                    if k >= 2:
                        act.wait_ge(x_squares_added, KB * B["n"] + k - 1)
                    act.activation(sq[:, k % 2, :], x[:, k, :], ACT.Square).then_inc(x_squares, 1)
                if B["pre"]:
                    rs_copy(NORM[B["pre"]], norm_banks(B["g"])[0])

            def ffn(u, g, pair, b):
                for n, (f, pairs) in enumerate(FF_PARTS):
                    with act.Fori(0, pairs) as i:
                        hi(u + 2, di=i * 2)
                        act.wait_ge(acc_empty, i * 2 + (g + 1))
                        act.activation(gate[:], gate[:], ACT.Silu).then_inc(silu_done, 1)
                        hi(u + 3, di=i * 2)
                        act.wait_ge(hid_done, i + (pair + 1))
                        act.activation(hh[:, bass.ds(i * 2, 2), :], up[:], ACT.Copy).then_inc(hid_hi, 1)
                    u, g, pair = u + 2 * pairs, g + 2 * pairs, pair + pairs
                    if n < len(FF_PARTS) - 1:
                        with act.Fori(0, 2) as i:
                            for j in range(2):
                                hi(u + j + 2, di=i * 2)
                    else:
                        for m in range(4):
                            if u + m + 2 < UNITS:
                                hi(u + m + 2)
                            square(m, 4 * b + m, g + m)
                    u, g = u + 4, g + 4

            for t in range(TT):
                src = a["x_prompt"][0, tile(t), :] if t < 4 else a["x_sample"].rearrange("b s d -> (b s) d")
                act.dma_start(xin[:, t, :], src).then_inc(x_loads, 16)
            hi(0)
            hi(1)
            act.wait_ge(x_loads, 16 * TT)
            for t in range(TT):
                if t:
                    act.wait_ge(x0_sums, t)
                act.activation(junk[:], xin[:, t, :], ACT.Square, accum_out=ss[:, t:t + 1]).then_inc(x0_sums, 1)
            act.wait_ge(rows_done, 1)
            for k in range(KB):
                act.wait_ge(x0_done, k + 1)
                x_hi(k, PRE_MIX)
            rs_copy(0, 5)
            for u in range(4):
                hi(u + 2)
                if u >= 2:
                    act.wait_ge(acc_empty, u + 1)
                    act.activation(uT[:, 2 * (u - 2):2 * (u - 1), :], uT[:, 2 * (u - 2):2 * (u - 1), :], ACT.Gelu_apprx_tanh).then_inc(u_done, 1)
            act.activation(a_last[:].rearrange("p g (b s) -> p g b s", s=STEP),
                           winA[:, :, 16 + PROMPT:].rearrange("p g (b s) -> p g b s", s=32)[:, :, :, 16:], ACT.Copy).then_inc(a_last_done, 1)
            hi(U_OUT0)
            for t in range(TT):
                if t < 4:
                    act.wait_ge(v_full, t + 1)
                else:
                    act.wait_ge(w_used, U_V + 2)
                if t >= 2:
                    act.wait_ge(v_normed, t - 1)
                act.activation(gv[:, t % 2, :], ps[:, t, :], ACT.Gelu_apprx_tanh, scale=rpre[:, t:t + 1]).then_inc(v_gelu, 1)
            hi(U_OUT0 + 1)
            for gr, b in enumerate((6, 4, 0, 2)):
                act.wait_ge(ya_full, gr + 1)
                act.activation(xh[:, gr, :], span(b), ACT.Copy, scale=gain(POOL_SCALE + gr)).then_inc(xh_done, 1)
            for t in range(TT):
                act.wait_ge(yb_done, t + 1)
                act.activation(xh[:, 4:8, tile(t)], uT[:, :, tile(t)], ACT.Copy).then_inc(yb_hi, 1)
            act.wait_ge(last_a_full, 1)
            act.wait_ge(v_normed, TT)
            act.activation(gv[0:HIST, 0, :], ps[0:HIST, 1, :], ACT.Copy).then_inc(last_a_done, 1)
            act.activation(gv[:, 1, :], ps[:, 2, :], ACT.Copy).then_inc(last_a_done, 1)
            act.wait_ge(last_a_done, 2)
            act.dma_start(a["pool_prompt"][0, 0], gv[0:HIST, 0, :]).then_inc(mixer_stores, 16)
            for b in range(STREAMS):
                act.dma_start(a["pool_sample"][0, b], gv[b * STEP + 1:(b + 1) * STEP, 1, :]).then_inc(mixer_stores, 16)
            act.wait_ge(v_done, TT)
            act.dma_start(a["sg_v_sample"][0].rearrange("b s d -> (b s) d"), v[:, 4, :]).then_inc(mixer_stores, 16)
            for m in range(4):
                hi(U_OUT0 + m + 2)
                square(m, m, G_OUT0 + m)
            boundary(BOUNDS[0])
            ffn(U_FF0, G_FF0, 0, 1)
            boundary(BOUNDS[1])
            for j in range(4):
                hi(U_QK + j + 2)
            hi(U_G + 2)
            hi(U_VV + 2)

            def v_copy(p, banks):
                for t, b in enumerate(banks):
                    if t < 4:
                        act.wait_ge(vv_full, 4 * p + t + 1)
                    else:
                        act.wait_ge(w_used, U_VV + 2 * p + 2)
                    act.activation(vv[:, t, p * 512:(p + 1) * 512], ps[:, b, :], ACT.Copy, scale=rpre[:, t:t + 1]).then_inc(vv_done, 1)
            v_copy(0, (4, 5, 6, 7, 2))
            hi(U_VV + 3)
            for t in range(TT):
                act.wait_ge(gabs_done, t + 1)
                act.activation(gb[:], gb[:], ACT.Exp, scale=-1.0).then_inc(act_step, 1)
                act.wait_ge(act_step, t + 1)
                act.activation(gb[:], gb[:], ACT.Ln, bias=1.0).then_inc(gln_done, 1)
            hi(U_VV + 4)
            v_copy(1, (6, 7, 2, 0, 1))
            hi(U_VV + 5)
            for h, b in enumerate((4, 6, 2, 0)):
                act.wait_ge(cum_full, h + 1)
                act.activation(cum[:, h, :], span(b), ACT.Copy, scale=1.0 / TAU).then_inc(cum_done, 1)
            for h in range(HEADS):
                hi(U_R + h + 2)
                act.wait_ge(acc_empty, G_R + h + 1)
                act.activation(rT[:, 2 * h:2 * h + 2, :], rT[:, 2 * h:2 * h + 2, :], ACT.Silu).then_inc(r_silu, 1)
                act.wait_ge(cum_done, h + 1)
                if h:
                    act.wait_ge(head_done, h)
                act.activation(eq[:], cum[:, h, :], ACT.Exp)
                act.activation(ek[:], cum[:, h, :], ACT.Exp, scale=-1.0)
                act.wait_ge(bend_done, h + 1)
                act.activation(elast[:, h, :], bend, ACT.Exp).then_inc(exps_done, 1)
                act.wait_ge(dist_done, h + 1)
                act.activation(cum[:, h, :], cum[:, h, :], ACT.Exp).then_inc(dist_exp, 1)
            for h in range(HEADS):
                act.wait_ge(kt_full, h + 1)
                act.activation(kend[:, :, tile(h)], span(2 * h).rearrange("p (t n) -> p t n", n=P), ACT.Copy).then_inc(kt_done, 1)
            for c in range(8):
                act.wait_ge(o_full, c + 1)
                act.activation(qk[:, :, c * CHUNK:(c + 1) * CHUNK], ps[:, 6 + c % 2, :].rearrange("p (n t) -> p n t", n=8), ACT.Copy).then_inc(o_copied, 1)
            act.wait_ge(o_full, 9)
            act.activation(qk[:, :, tile(4)], span(6, D).rearrange("p (n t) -> p n t", n=8), ACT.Copy).then_inc(o_copied, 1)
            act.wait_ge(o_copied, 9)
            for h in range(HEADS):
                if h:
                    act.wait_ge(o_added, h)
                act.activation(sq[:], qk[:].rearrange("p (v h) t -> p v h t", v=2)[:, :, h, :], ACT.Square).then_inc(o_sq, 1)
            act.wait_ge(state_stores, 16 * (HEADS + 1))
            for k in range(KB):
                act.wait_ge(o_gated, 2 * k + 2)
                act.activation(xh[:, k, :], qk[:, (k % 2) * HEADS + k // 2, :], ACT.Copy).then_inc(xh_done, 1)
            for m in range(4):
                hi(U_OUT1 + m + 2)
                square(m, 8 + m, G_OUT1 + m)
            boundary(BOUNDS[2])
            ffn(U_FF1, G_FF1, 11, 3)

        @block.gpsimd
        def _(pool):
            steps = [0]

            def step(ins):
                steps[0] += 1
                ins.then_inc(pool_step, 1)
                pool.wait_ge(pool_step, steps[0])

            def norm(name):
                n = NORM[name]
                pool.wait_ge(ms_done, n + 1)
                dst = rpre if name.startswith("pre") else rstd[:, 0:TT]
                pool.tensor_tensor(dst, ms[:, 0:TT], minus_half[:, 0:TT], ALU.pow).then_inc(rstd_done, 1)

            def boundary(B):
                norm(B["post"])
                for k in range(KB + 1):
                    if k < KB:
                        pool.wait_ge(y_scaled, KB * B["n"] + k + 1)
                        pool.tensor_tensor(x[:, k, :], x[:, k, :], y[:, k, :], ALU.add).then_inc(x_added, 1)
                    if k and B["pre"]:
                        j = k - 1
                        pool.wait_ge(x_squares, KB * B["n"] + j + 1)
                        if j == 0:
                            pool.tensor_copy(acc[:, 0, :], sq[:, 0, :]).then_inc(x_squares_added, 1)
                        else:
                            pool.wait_ge(x_squares_added, KB * B["n"] + j)
                            pool.tensor_tensor(acc[:, 0, :], acc[:, 0, :], sq[:, j % 2, :], ALU.add).then_inc(x_squares_added, 1)
                if B["pre"]:
                    norm(B["pre"])

            pool.memset(wsn[:, 1], 0.0).then_inc(zeroed, 1)
            pool.memset(winA[:, :, 0:16], 0.0).then_inc(zeroed, 1)
            pool.memset(winA[:, :, 16 + PROMPT:].rearrange("p g (b s) -> p g b s", s=32)[:, :, :, 0:1], 0.0).then_inc(zeroed, 1)
            pool.dma_start(cst[:], a["consts"]).then_inc(small_loads, 16)
            r0 = 0
            for name in ("pre_mix_g", "post_mix_g", "pre_ffn_g", "post_ffn_g", "pool_scale", "g_onorm"):
                src = a[name].rearrange("l (k p) -> (l k) p", p=P)
                pool.dma_start(rows[r0:r0 + src.shape[0], :], src).then_inc(small_loads, 16)
                r0 += src.shape[0]
            assert r0 == ROWS
            w_s = a["w_s"][0].rearrange("h t s -> t h s")
            pool.dma_start(wsn[:, 0], w_s).then_inc(small_loads, 16)
            pool.dma_start(hist[0:STREAMS * HIST, :], a["state_pool"][0].rearrange("b s d -> (b s) d")).then_inc(small_loads, 16)
            pool.wait_ge(zeroed, 1)
            for b in range(STREAMS):
                pool.dma_start(wsn[b * STEP:(b + 1) * STEP, 1, :, b * STEP:(b + 1) * STEP], w_s[0:STEP, :, 0:STEP]).then_inc(small_loads, 16)
            pool.dma_start(bs[0:1, 0, :], a["b_s"].rearrange("l h t -> l (h t)")).then_inc(small_loads, 16)
            pool.dma_start(wpool[:], a["w_pool"][0].rearrange("g c d -> c g d")).then_inc(small_loads, 16)
            pool.dma_start(lng[:], a["ln_v_g"][0].partition_broadcast(P)).then_inc(small_loads, 16)
            pool.dma_start(lnb[:], a["ln_v_b"][0].partition_broadcast(P)).then_inc(small_loads, 16)
            pool.wait_ge(consts_set, 2)
            norm("pre0")
            pool.wait_ge(acc_empty, 2)
            pool.wait_ge(hist_done, 1)
            for n, (src, dst) in enumerate(((winA, winB), (winB, winC), (winC, winB), (winB, winC))):
                w, s0 = 1 << n, (2 << n) - 1
                step(pool.tensor_tensor(dst[:, n:4, s0:], src[:, n:4, s0:], src[:, n:4, s0 - w:AW - w], ALU.add))
            for gr in range(4):
                s = (winB, winC)[gr % 2][:, gr, 16:32]
                last = pool.tensor_tensor(s, s, fix[:, gr, :], ALU.mult)
            last.then_inc(windows_done, 1)
            for t in range(TT):
                pool.wait_ge(vms_done, t + 1)
                pool.tensor_tensor(vrstd[:, t:t + 1], vms, minus_half[:, 0:1], ALU.pow).then_inc(vrstd_done, 1)
                pool.wait_ge(v_normed, t + 1)
                step(pool.tensor_tensor(v[:, t, :], v[:, t, :], lng[:], ALU.mult))
                pool.tensor_tensor(v[:, t, :], v[:, t, :], lnb[:], ALU.add).then_inc(v_done, 1)
            pool.wait_ge(yb_full, TT)
            pool.wait_ge(v_done, TT)
            pool.memset(w2[:], 0.0).then_inc(w2_zeroed, 1)
            pool.wait_ge(w2_zeroed, 1)
            pool.dma_start(w2[P - 16:P, :], a["w_gate2"][0]).then_inc(gate_loads, 16)
            pool.dma_start(bg[:], a["b_gate"][0].partition_broadcast(P)).then_inc(gate_loads, 16)
            boundary(BOUNDS[0])
            boundary(BOUNDS[1])
            pool.wait_ge(w_used, U_R + 4)
            for h in range(HEADS):
                pool.dma_start(Ss[:, h], a["state_gla"][0, :, h].rearrange("b k v -> k b v")).then_inc(states_in, 16)
            pool.memset(S[:, 0], 0.0).then_inc(cleared, 1)
            pool.wait_ge(head_done, HEADS)
            pool.memset(att[:], 0.0).then_inc(cleared, 1)
            pool.wait_ge(kt_full, HEADS)
            pool.wait_ge(kt_done, HEADS)
            for n in range(2):
                pool.tensor_scalar(km[:, n, :], kend[:, 4, :], par[:, n:n + 1], None, ALU.mult).then_inc(km_done, 1)
            pool.wait_ge(s_done, 8)
            pool.dma_start(a["gla_prompt"][0, 0].rearrange("h k v -> k h v"), S[:, 0]).then_inc(state_stores, 16)
            for h in range(HEADS):
                pool.wait_ge(ss_done, 8 * (h + 1))
                pool.dma_start(a["gla_sample"][0, :, h].rearrange("b k v -> k b v"), Ss[:, h]).then_inc(state_stores, 16)
            pool.wait_ge(o_ms, 1)
            pool.tensor_tensor(rstd, ms, minus_half, ALU.pow).then_inc(o_rstd, 1)
            boundary(BOUNDS[2])
            boundary(BOUNDS[3])


def constants():
    s, t = np.indices((P, P))
    masks = [(s <= t) & (s // n == t // n) for n in (P, CHUNK, STEP)]
    frames = np.arange(16)
    fix = [w / np.minimum(w, frames + 1) for w in WINDOWS]
    odd = (np.arange(P) // STEP) % 2
    parts = [np.eye(P), *masks, np.broadcast_to(np.concatenate(fix), (P, 64)), np.stack([1 - odd, odd], 1)]
    return np.concatenate([np.asarray(x, np.float32) for x in parts], 1)


_OUTS = {
    "y_prompt": (1, PROMPT, D), "y_sample": (STREAMS, STEP, D),
    "pool_prompt": (1, 1, HIST, SG), "pool_sample": (1, STREAMS, HIST, SG),
    "sg_v_sample": (1, STREAMS, STEP, SG),
    "gla_prompt": (1, 1, HEADS, DK, DV), "gla_sample": (1, STREAMS, HEADS, DK, DV),
}


def kernel(**inputs):
    import concourse.bacc as bacc
    from concourse.bass_utils import run_bass_kernel_spmd

    nc = bacc.Bacc("TRN2", target_bir_lowering=False, num_devices=1)
    arrays = {name: np.ascontiguousarray(x) for name, x in inputs.items()}
    arrays["consts"] = constants()
    aps = {name: nc.dram_tensor(name, x.shape, mybir.dt.from_np(x.dtype), kind="ExternalInput").ap() for name, x in arrays.items()}
    for name, shape in _OUTS.items():
        aps[name] = nc.dram_tensor(name, shape, F32, kind="ExternalOutput").ap()
    encoder(nc, aps)
    r = run_bass_kernel_spmd(nc, [arrays], core_ids=[0])
    return tuple(r.results[0][name] for name in _OUTS)
```

```python
from contextlib import ExitStack

import concourse.bass as bass
import numpy as np
from concourse import mybir

F32 = mybir.dt.float32
F32R = mybir.dt.float32r
U32 = mybir.dt.uint32
ACT = mybir.ActivationFunctionType
ALU = mybir.AluOpType

P = 128
D = 1024
KB = D // P
PROMPT, STREAMS, STEP = 512, 8, 16
T = PROMPT + STREAMS * STEP
TT = T // P
HALF = T // 2
EPS = 1e-6
WINDOWS = (2, 4, 8, 16)
HIST = 15
SG = 512
HEADS, DK, DV = 4, 128, 256
TAU = 16.0
CHUNK = 64
D_FF = 2816
FF_PARTS = ((0, 4), (8, 4), (16, 3))
UW = 2 * P
CONSTS = 4 * P + 66

PRE_MIX, POST_MIX, PRE_FFN, POST_FFN, POOL_SCALE, O_NORM, ROWS = 0, 16, 32, 48, 64, 68, 76

U_AU, U_V, U_OUT0, U_FF0 = 0, 4, 6, 10
FF_UNITS = sum(2 * n + 4 for _, n in FF_PARTS)
U_QK = U_FF0 + FF_UNITS
U_G = U_QK + 1
U_VV = U_QK + 5
U_R = U_VV + 4
U_OUT1 = U_R + 4
U_FF1 = U_OUT1 + 4
UNITS = U_FF1 + FF_UNITS

G_AU, G_OUT0, G_FF0 = 0, 4, 8
G_QK = G_FF0 + FF_UNITS
G_G = G_QK + 1
G_OUT1 = G_QK + 5
G_FF1 = G_OUT1 + 4

CORE = (("streams", 0), ("streams", 1), ("chunk", 0), ("chunk", 1), ("streams", 2), ("streams", 3),
        ("r", 0, 0), ("chunk", 2), ("r", 0, 1), ("chunk", 3), ("r", 0, 2), ("r", 0, 3), ("chunk", 4),
        ("r", 0, 4), ("chunk", 5), ("r", 1, 0), ("chunk", 6), ("r", 1, 1), ("chunk", 7),
        ("r", 1, 2), ("r", 1, 3), ("r", 1, 4))


_NORMS = [(what, n[0]) for what, *n in CORE if what == "streams" or (what == "chunk" and n[0] % 2)]
SO_NORMED = [_NORMS.index(("streams", h)) + 1 for h in range(HEADS)]
O_NORMED = [_NORMS.index(("chunk", 2 * t + 1)) + 1 for t in range(PROMPT // P)]


def encoder(nc, a):
    with ExitStack() as ctx:
        base, end = nc.sbuf_base, nc.sbuf_usable_end
        base = (base + 63) // 64 * 64

        def at(name, offset, shape, dt=F32, parts=P):
            size = 4 * int(np.prod(shape))
            assert base + offset + size <= end, (name, base + offset + size, end)
            return nc.alloc_sbuf_tensor_at(name, [parts, *shape], dt, offset=base + offset)

        K20, K10, K5 = 20480, 10240, 5120
        o_x, o_xh, o_xl, o_y, o_hh, o_hl = (i * K20 for i in range(6))
        o_stage = 6 * K20
        o_wh, o_wl = o_stage + 16384, o_stage + 2 * 16384
        o_rs = o_wl + 16384
        o_sq = o_rs + 2560
        o_acc = o_sq + K5
        o_gate = o_acc + K5
        o_up = o_gate + K5
        o_diag = o_up + K5
        o_late = o_diag + 2560
        o_const = o_late + K10

        x = at("x", o_x, [KB, T])
        xh = at("xh", o_xh, [KB, T], F32R)
        xl = at("xl", o_xl, [KB, T], F32R)
        y = at("y", o_y, [KB, T])
        hh = at("hh", o_hh, [KB, T], F32R)
        hl = at("hl", o_hl, [KB, T], F32R)
        stage = at("stage", o_stage, [2, KB * UW])
        wh = at("wh", o_wh, [2, KB, UW], F32R)
        wl = at("wl", o_wl, [2, KB, UW], F32R)
        rs = at("rs", o_rs, [T])
        sq = at("sq", o_sq, [2, T])
        acc = at("acc", o_acc, [2, T])
        gate = at("gate", o_gate, [2, T])
        up = at("up", o_up, [2, T])
        diag = at("diag", o_diag, [TT, P])
        cst = at("cst", o_const, [CONSTS])
        ident = cst[:, 0:P]
        tri = cst[:, P:4 * P].rearrange("p (m t) -> p m t", m=3)
        fix = cst[:, 4 * P:4 * P + 64].rearrange("p (g t) -> p g t", g=4)
        par = cst[:, 4 * P + 64:4 * P + 66]
        ones = at("ones", o_const + 2368, [P])
        gains = at("gains", o_const + 2880, [ROWS])
        small = at("small", o_const + 3200, [130])
        elast = at("elast", o_const + 3744, [HEADS, 2 * STREAMS])
        ss, ms, rstd = small[:, 0:20], small[:, 20:40], small[:, 40:60]
        minus_half = small[:, 60:80]
        rpre = small[:, 80:85]
        bn6, vms, vrstd, mv = small[:, 90:96], small[:, 96:98], small[:, 100:105], small[:, 105:109]
        bend = small[:, 110:126]

        uT = at("uT", o_y, [4, T])
        v = at("v", o_y + K10, [TT, SG])
        xin = at("xin", o_y, [TT, D])
        junk = at("junk", o_hl + 6016, [D])
        xg = at("xg", o_hl + 6016 + 4 * D, [2, KB, P])
        AW = 16 + PROMPT + STREAMS * 32
        winA = at("winA", o_hh, [4, AW])
        winB = at("winB", o_hh + 4 * 4 * AW, [4, AW])
        winC = at("winC", o_hh + 8 * 4 * AW, [4, AW])
        wsT = at("wsT", o_late, [2, 4, P])
        wpool = at("wpool", o_late + 4096, [4, P])
        lng = at("lng", o_late + 6144, [SG])
        lnb = at("lnb", o_late + 8192, [SG])
        gv = at("gv", o_gate, [2, SG])
        bs = at("bs", o_gate + 4096, [2, 4 * P])
        hist = at("hist", o_sq, [SG])
        a_last = at("a_last", o_sq + 2048, [4, P])
        wsn = at("wsn", o_acc, [2, 4, P])
        a_out = at("a_out", o_acc, [2, SG])
        rows = at("rows", o_diag, [P])

        qk = at("qk", o_hh, [8, T])
        vv = at("vv", o_hl, [TT, D])
        la = at("la", o_y, [TT, SG])
        Ss = at("Ss", o_y, [2, STREAMS, DV])
        rg = at("rg", o_y, [TT, D])
        lmin = at("lmin", o_gate, [TT, SG])
        cum = at("cum", o_gate, [HEADS, T])
        zf = at("zf", o_diag, [T])
        w2 = at("w2", o_late, [SG])
        bg = at("bg", o_late + 2048, [SG])
        kend = at("kend", o_late, [TT, SG])
        eq = at("eq", o_sq, [T])
        ek = at("ek", o_sq + 2560, [T])
        att = at("att", o_sq, [3, 4 * P])
        qm = at("qm", o_sq + 6144, [HEADS, 2, P])
        S = at("S", o_gate, [2, HEADS, DV])
        km = at("km", o_gate + 8192, [2, SG])

        yF = at("yF", o_y, [TT, D])
        xF = at("xF", o_xh, [TT, D])
        gF = at("gF", o_late, [D])
        yg = at("yg", o_late + 4 * D, [TT, UW])

        ps = ctx.enter_context(nc.psum_tensor("ps", [P, 8, 512], F32))
        flat = ps[:].rearrange("p b n -> p (b n)")

        def sem(name):
            return ctx.enter_context(nc.semaphore(name))

        w_loaded = [sem("w_loaded0"), sem("w_loaded1")]
        w_hi, w_lo, w_used = sem("w_hi"), sem("w_lo"), sem("w_used")
        acc_empty = sem("acc_empty")
        ident_load, rows_loads, small_loads = sem("ident_load"), sem("rows_loads"), sem("small_loads")
        x_load = [sem(f"x_load{t}") for t in range(TT)]
        consts_set, zeroed = sem("consts_set"), sem("zeroed")
        dve_step, act_step, pool_step = sem("dve_step"), sem("act_step"), sem("pool_step")
        xh_done, xl_done = sem("xh_done"), sem("xl_done")
        squares, squares_added = sem("squares"), sem("squares_added")
        sums_full, ms_done, rstd_done = sem("sums_full"), sem("ms_done"), sem("rstd_done")
        diag_done, r_full, rs_done = sem("diag_done"), sem("r_full"), sem("rs_done")
        y_blocks_full, y_stands, y_scaled = sem("y_blocks_full"), sem("y_stands"), sem("y_scaled")
        x_added_dve, x_added_pool = sem("x_added_dve"), sem("x_added_pool")
        x_squares, x_squares_added = sem("x_squares"), sem("x_squares_added")
        rows_full, rows_done, x0_full, x0_done = sem("rows_full"), sem("rows_done"), sem("x0_full"), sem("x0_done")
        xg_done, x0_hi, x0_lo = sem("xg_done"), sem("x0_hi"), sem("x0_lo")
        ws_full, ws_done, hist_full, hist_done = sem("ws_full"), sem("ws_done"), sem("hist_full"), sem("hist_done")
        x0_sums = sem("x0_sums")
        a_last_done, windows_done, pooled_done, ya_full = sem("a_last_done"), sem("windows_done"), sem("pooled_done"), sem("ya_full")
        u_done, v_full, v_gelu, vms_done = sem("u_done"), sem("v_full"), sem("v_gelu"), sem("vms_done")
        vrstd_done, v_normed, v_gained, v_done = sem("vrstd_done"), sem("v_normed"), sem("v_gained"), sem("v_done")
        yb_full, yb_done, yb_hi, yb_lo = sem("yb_full"), sem("yb_done"), sem("yb_hi"), sem("yb_lo")
        last_a_full, last_a_done, mixer_stores = sem("last_a_full"), sem("last_a_done"), sem("mixer_stores")
        silu_done, hid_done, hid_hi, hid_lo = sem("silu_done"), sem("hid_done"), sem("hid_hi"), sem("hid_lo")
        w2_zeroed, gate_loads = sem("w2_zeroed"), sem("gate_loads")
        vv_full, vv_done = sem("vv_full"), sem("vv_done")
        gate_full, gx_done, gabs_done, gln_done, la_done = (sem(n) for n in ("gate_full", "gx_done", "gabs_done", "gln_done", "la_done"))
        states_in = [sem("states_in0"), sem("states_in1")]
        states_out = [sem("states_out0"), sem("states_out1")]
        cum_full, cum_done, bend_done, exps_done = sem("cum_full"), sem("cum_done"), sem("bend_done"), sem("exps_done")
        dist_done, dist_exp, head_done = sem("dist_done"), sem("dist_exp"), sem("head_done")
        kt_full, kt_done, cleared, km_done = (sem(n) for n in ("kt_full", "kt_done", "cleared", "km_done"))
        att_full, att_done, kv_full, s_done = sem("att_full"), sem("att_done"), sem("kv_full"), sem("s_done")
        o_full, skv_full, ss_done = sem("o_full"), sem("skv_full"), sem("ss_done")
        so_full, o_squared, o_ms, o_rstd, o_normed = (sem(n) for n in ("so_full", "o_squared", "o_ms", "o_rstd", "o_normed"))
        r_tile_full, r_done, gated, gated_full = (sem(n) for n in ("r_tile_full", "r_done", "gated", "gated_full"))
        prompt_out = sem("prompt_out")
        gain_load, xF_full, xF_done = sem("gain_load"), sem("xF_full"), sem("xF_done")
        y_tile_full, y_tile_out, y_tile_sq = sem("y_tile_full"), sem("y_tile_out"), sem("y_tile_sq")
        y_gained, tile_ms, tile_rstd = sem("y_gained"), sem("tile_ms"), sem("tile_rstd")
        out_ready, stores = sem("out_ready"), sem("stores")

        SMALL_LOADS = 1 + 2 + STREAMS + 4
        MIXER_STORES = 1 + STREAMS + 1
        U_QKS = (U_QK, U_QK + 2, U_QK + 3, U_QK + 4)
        G_QKS = (G_QK, G_QK + 2, G_QK + 3, G_QK + 4)
        SO_BANK = (7, 3)
        KV_RING = (1, 2, 5, 6)

        NORM = {"pre0": 0, "post0": 1, "preF0": 2, "postF0": 3, "pre1": 4, "post1": 5, "preF1": 6}
        X_OUT0, X_FF0, X_IN1, X_OUT1, X_FF1 = 0, 4, 12, 20, 28
        BOUNDS = (
            dict(n=0, post="post0", pre="preF0", gp=POST_MIX, gq=PRE_FFN, g=G_FF0, x=X_FF0),
            dict(n=1, post="postF0", pre="pre1", gp=POST_FFN, gq=PRE_MIX + 8, g=G_QK, x=X_IN1),
            dict(n=2, post="post1", pre="preF1", gp=POST_MIX + 8, gq=PRE_FFN + 8, g=G_FF1, x=X_FF1),
        )

        def f32(t):
            return t.bitcast(F32)

        def banks4(g):
            b = 4 * (g % 2)
            return ps[:, b:b + 4, 0:HALF].rearrange("p (m h) n -> p m h n", m=2)

        def span(b, n=T):
            return flat[:, 512 * b:512 * b + n]

        def halved(t):
            return t.rearrange("p (h n) -> p h n", h=2)

        def two(t, k):
            return t[:, bass.ds(k, 2), :].rearrange("p m (h n) -> p m h n", h=2)

        def rs_twice():
            return halved(rs[:]).unsqueeze(1).broadcast_to([P, 2, 2, HALF])

        def tile(t):
            return slice(t * P, (t + 1) * P)

        def norm_banks(g):
            b = 4 * ((g + 1) % 2)
            return b, b + 2, b + 3

        def tile_bank(odd, t):
            return (4 * (G_FF1 % 2) + (5 + t % 3 if odd else t)) % 8

        def xF_bank(t):
            return (4 * (G_FF1 % 2) + 2 * t) % 8

        ADDED_BY_DVE = (0, 4)

        def wait_x_added(engine, n, k):
            if k in ADDED_BY_DVE:
                engine.wait_ge(x_added_dve, len(ADDED_BY_DVE) * n + ADDED_BY_DVE.index(k) + 1)
            else:
                done = sum(j not in ADDED_BY_DVE for j in range(k + 1))
                engine.wait_ge(x_added_pool, (KB - len(ADDED_BY_DVE)) * n + done)

        def gain(row):
            return gains[:, row:row + 1]

        block = ctx.enter_context(nc.Block())

        @block.sync
        def _(sp):
            def load(u, src, wait=True):
                if wait:
                    sp.wait_ge(w_lo, u - 1)
                src = src.rearrange("(k p) c -> p k c", p=P)
                nk, width = src.shape[1:]
                dst = stage[:, u % 2, 0:nk * width].rearrange("p (k c) -> p k c", c=width)
                sp.dma_start(dst, src).then_inc(w_loaded[u % 2], 16)

            def load_loop(u0, pairs, src):
                with sp.Fori(0, pairs) as i:
                    for j in range(2):
                        u = u0 + j
                        sp.wait_ge(w_lo, i * 2 + (u - 1))
                        dst = stage[:, u % 2, :].rearrange("p (k c) -> p k c", c=UW)
                        s = src(i, j).rearrange("(k p) c -> p k c", p=P)
                        sp.dma_start(dst[:, 0:s.shape[1], :], s).then_inc(w_loaded[u % 2], 16)

            def load_ffn(layer, u):
                for f, pairs in FF_PARTS:
                    load_loop(u, pairs, lambda i, j: (a["w_ffn_gate"], a["w_ffn_up"])[j][layer, :, bass.ds(i * UW + f * P, UW)])
                    u += 2 * pairs
                    load_loop(u, 2, lambda i, j: a["w_ffn_down"][layer, f * P:(f + 2 * pairs) * P, bass.ds(i * (2 * UW) + j * UW, UW)])
                    u += 4

            sp.dma_start(ident, a["consts"][:, 0:P]).then_inc(ident_load, 16)
            r0 = 0
            for name in ("pre_mix_g", "post_mix_g", "pre_ffn_g", "post_ffn_g", "pool_scale", "g_onorm"):
                src = a[name].rearrange("l (k p) -> (l k) p", p=P)
                sp.dma_start(rows[r0:r0 + src.shape[0], :], src).then_inc(rows_loads, 16)
                r0 += src.shape[0]
            assert r0 == ROWS
            for t in range(TT):
                src = a["x_prompt"][0, tile(t), :] if t < 4 else a["x_sample"].rearrange("b s d -> (b s) d")
                sp.dma_start(xin[:, t, :], src).then_inc(x_load[t], 16)
                if t == 0:
                    load(0, a["w_in_even"][0, :, 0:UW], wait=False)
            for u in range(1, U_OUT0):
                load(u, a["w_in_even"][0, :, u * UW:(u + 1) * UW], wait=u >= 2)
            for m in range(4):
                load(U_OUT0 + m, a["w_out_even"][0, :, m * UW:(m + 1) * UW])
            load_ffn(0, U_FF0)
            w_in = a["w_in_odd"][0]
            for j, u in enumerate(U_QKS):
                load(u, w_in[:, j * UW:(j + 1) * UW])
                if j == 0:
                    load(U_G, w_in[:, w_in.shape[1] - P:])
            for j in range(8):
                load(U_VV + j, w_in[:, D + j * UW:D + (j + 1) * UW])
            for m in range(4):
                load(U_OUT1 + m, a["w_out_odd"][0, :, m * UW:(m + 1) * UW])
            load_ffn(1, U_FF1)

            for t in range(TT):
                dst = a["y_prompt"][0, tile(t), :] if t < 4 else a["y_sample"].rearrange("b s d -> (b s) d")
                for n, cols in enumerate((slice(0, D - UW), slice(D - UW, D))):
                    sp.wait_ge(out_ready, 2 * t + n + 1)
                    sp.dma_start(dst[:, cols], yF[:, t, cols]).then_inc(stores, 16)
            sp.wait_ge(stores, 16 * 2 * TT)
            sp.wait_ge(mixer_stores, 16 * MIXER_STORES)
            for sem_ in states_out:
                sp.wait_ge(sem_, 16 * HEADS // 2)
            sp.wait_ge(prompt_out, 16)

        @block.tensor
        def _(pe):
            def unit(u, g, mh, ml, nk=KB, ready=None, di=0):
                pe.wait_ge(w_lo, di + (u + 1))
                if g >= 2:
                    pe.wait_ge(acc_empty, di + (g - 1))
                out = banks4(g)
                for k in range(nk):
                    if ready is not None:
                        ready(k)
                    for m in range(2):
                        for n, (w, mv_) in enumerate(((wh, mh), (wh, ml), (wl, mh))):
                            wt = w[:, u % 2, k, m * P:(m + 1) * P]
                            for h in range(2):
                                last = pe.matmul(out[:, m, h, :], wt, mv_[:, k, h * HALF:(h + 1) * HALF],
                                                 start=(k == 0 and n == 0), stop=(k == nk - 1 and n == 2))
                last.then_inc(w_used, 1)

            def frames_unit(u, bank, half, wait=None, event=None):
                pe.wait_ge(w_lo, u + 1)
                for t in range(TT):
                    if wait is not None:
                        wait(t)
                    for k in range(KB):
                        for n, (w, mv_) in enumerate(((wh, xh), (wl, xh), (wh, xl))):
                            last = pe.matmul(ps[:, bank[t], half * UW:(half + 1) * UW], mv_[:, k, tile(t)], w[:, u % 2, k, :],
                                             start=(k == 0 and n == 0), stop=(k == KB - 1 and n == 2))
                    if t == TT - 1:
                        last.then_inc(w_used, 1)
                    elif event is not None:
                        last.then_inc(event, 1)

            def sum_tiles(bank, src, tiles, first=False):
                for t in tiles:
                    last = pe.matmul(ps[:, bank, t:t + 1], src[:, tile(t)], ones[:, 0:1], start=(first and t == 0), stop=True,
                                     skip_group_check=True)
                return last

            def spread(name, b):
                pe.wait_ge(diag_done, NORM[name] + 1)
                for h in range(2):
                    last = pe.matmul(ps[:, b + h, 0:HALF], ones[:], diag[:].rearrange("p t n -> p (t n)")[:, h * HALF:(h + 1) * HALF],
                                     start=True, stop=True)
                last.then_inc(r_full, 1)

            def part(u, out, mh, ml, m, h, ks, nk):
                for k in ks:
                    for n, (w, mv_) in enumerate(((wh, mh), (wh, ml), (wl, mh))):
                        last = pe.matmul(out[:, m, h, :], w[:, u % 2, k, m * P:(m + 1) * P], mv_[:, k, h * HALF:(h + 1) * HALF],
                                         start=(k == 0 and n == 0), stop=(k == nk - 1 and n == 2))
                return last

            def last_y_unit(u, B, mh, ml, nk):
                g, out = B["g"] - 1, banks4(B["g"] - 1)
                pe.wait_ge(w_lo, u + 1)
                pe.wait_ge(acc_empty, g - 1)
                for h in range(2):
                    last = part(u, out, mh, ml, 0, h, range(nk), nk)
                last.then_inc(y_blocks_full, 1)
                part(u, out, mh, ml, 1, 0, range(nk), nk).then_inc(y_blocks_full, 1)
                part(u, out, mh, ml, 1, 1, range(nk), nk).then_inc(w_used, 1)

            def boundary(B, u, blocks=2):
                behind, ahead, bank = norm_banks(B["g"])
                sq_n, g = 6 * B["n"], B["g"]
                pe.wait_ge(acc_empty, g)
                pe.wait_ge(squares_added, 4 * (B["n"] + 1))
                sum_tiles(bank, acc[:, 0], range(TT), first=True)
                pe.wait_ge(squares, sq_n + 5)
                sum_tiles(bank, sq[:, 1], range(2))
                pe.wait_ge(squares, sq_n + 6)
                sum_tiles(bank, sq[:, 1], range(2, TT)).then_inc(sums_full, 1)
                spread(B["post"], behind)
                out = banks4(g)
                pe.wait_ge(w_lo, u + 1)
                for k in range(KB):
                    for n, (w, mv_, ready) in enumerate(((wh, xh, xh_done), (wl, xh, None), (wh, xl, xl_done))):
                        if ready is not None:
                            pe.wait_ge(ready, B["x"] + k + 1)
                        for m in range(2):
                            for h in range(2):
                                last = pe.matmul(out[:, m, h, :], w[:, u % 2, k, m * P:(m + 1) * P], mv_[:, k, h * HALF:(h + 1) * HALF],
                                                 start=(k == 0 and n == 0), stop=(k == KB - 1 and n == 2))
                last.then_inc(w_used, 1)
                out = banks4(g + 1)
                pe.wait_ge(w_lo, u + 2)
                pe.wait_ge(y_scaled, KB * (B["n"] + 1))
                v = u + 1

                def first(ks):
                    for k in ks:
                        for n, (w, mv_) in enumerate(((wh, xh), (wh, xl), (wl, xh))):
                            wt = w[:, v % 2, k, 0:P] if blocks == 2 else w[:, v % 2, k // 2, (k % 2) * P:(k % 2 + 1) * P]
                            for h in range(2):
                                last = pe.matmul(out[:, 0, h, :], wt, mv_[:, k, h * HALF:(h + 1) * HALF],
                                                 start=(k == 0 and n == 0), stop=(k == KB - 1 and n == 2))
                    return last
                first(range(5))
                pe.wait_ge(x_squares_added, 4 * (B["n"] + 1))
                sum_tiles(bank, acc[:, 0], range(TT), first=True).then_inc(sums_full, 1)
                last = first(range(5, KB))
                if blocks == 1:
                    last.then_inc(w_used, 1)
                spread(B["pre"], ahead)
                pe.wait_ge(rs_done, 2 + B["n"])
                if blocks == 2:
                    part(v, out, xh, xl, 1, 0, range(KB), KB)
                    part(v, out, xh, xl, 1, 1, range(KB), KB).then_inc(w_used, 1)

            def gate_up(u, g, pairs, first):
                with pe.Fori(first, pairs) as i:
                    for j in range(2):
                        unit(u + j, g + j, xh, xl, di=i * 2)

            def hid_ready(pair, k):
                if k % 2 == 0:
                    pe.wait_ge(hid_lo, pair + k // 2 + 1)

            def ffn(u, g, pair, B):
                for n, (f, pairs) in enumerate(FF_PARTS):
                    gate_up(u, g, pairs, int(n == 0))
                    u, g = u + 2 * pairs, g + 2 * pairs
                    ready = lambda k: hid_ready(pair, k)
                    if n < len(FF_PARTS) - 1:
                        with pe.Fori(0, 2) as i:
                            for j in range(2):
                                unit(u + j, g + j, hh, hl, nk=2 * pairs, ready=ready, di=i * 2)
                    else:
                        for m in range(3):
                            unit(u + m, g + m, hh, hl, nk=2 * pairs, ready=ready)
                        last_y_unit(u + 3, B, hh, hl, 2 * pairs)
                    u, g, pair = u + 4, g + 4, pair + pairs

            def last_ffn(u, g, pair):
                for n, (f, pairs) in enumerate(FF_PARTS):
                    gate_up(u, g, pairs, int(n == 0))
                    u, g = u + 2 * pairs, g + 2 * pairs
                    if n == len(FF_PARTS) - 1:
                        for t in range(TT):
                            b = xF_bank(t)
                            if t < 4:
                                pe.wait_ge(acc_empty, g - 1 + t // 2)
                            else:
                                pe.wait_ge(xF_done, 1)
                            for k in range(KB):
                                last = pe.transpose(span(b, D)[:, tile(k)], x[:, k, tile(t)], ident)
                            last.then_inc(xF_full, 1)
                        pe.wait_ge(xF_done, TT)
                    nk = 2 * pairs
                    with pe.Fori(0, 2) as i:
                        pe.wait_ge(w_lo, i * 2 + (u + 1))
                        for k in range(nk):
                            hid_ready(pair, k)
                            for t in range(TT):
                                if k == 0 and t == 4:
                                    pe.wait_ge(acc_empty, g)
                                for j, (w, mv_) in enumerate(((wh, hh), (wl, hh), (wh, hl))):
                                    last = pe.matmul(ps[:, tile_bank(0, t), 0:UW], mv_[:, k, tile(t)], w[:, u % 2, k, :],
                                                     start=(k == 0 and j == 0), stop=(k == nk - 1 and j == 2))
                        last.then_inc(w_used, 1)
                        pe.wait_ge(w_lo, i * 2 + (u + 2))
                        for t in range(TT):
                            if t >= 3:
                                pe.wait_ge(y_tile_out, i * 10 + (20 * n + 5 + t - 2))
                            for k in range(nk):
                                for j, (w, mv_) in enumerate(((wh, hh), (wl, hh), (wh, hl))):
                                    last = pe.matmul(ps[:, tile_bank(1, t), 0:UW], mv_[:, k, tile(t)], w[:, (u + 1) % 2, k, :],
                                                     start=(k == 0 and j == 0), stop=(k == nk - 1 and j == 2))
                            last.then_inc(w_used if t == TT - 1 else y_tile_full, 1)
                    u, pair = u + 4, pair + pairs

            pe.wait_ge(ident_load, 16)
            pe.wait_ge(rows_loads, 16 * 6)
            pe.transpose(ps[:, 0, 0:ROWS], rows[0:ROWS, :], ident[0:ROWS, 0:ROWS]).then_inc(rows_full, 1)

            def turn(t):
                pe.wait_ge(x_load[t], 16)
                if t >= 2:
                    pe.wait_ge(x0_done, t - 1)
                    pe.wait_ge(xg_done, t - 1)
                for k in range(KB):
                    last = pe.transpose(span(4 + 2 * (t % 2), D)[:, tile(k)], xin[:, t, tile(k)], ident)
                last.then_inc(x0_full, 1)

            def first_unit(h):
                for n, (w, mv_) in enumerate(((wh, xh), (wh, xl), (wl, xh))):
                    if n == 2 and h == 0:
                        pe.wait_ge(w_lo, 1)
                    for k in range(KB):
                        for m in range(2):
                            last = pe.matmul(banks4(0)[:, m, h, :], w[:, 0, k, m * P:(m + 1) * P], mv_[:, k, h * HALF:(h + 1) * HALF],
                                             start=(k == 0 and n == 0), stop=(k == KB - 1 and n == 2))
                return last
            for t in range(TT):
                turn(t)
            pe.wait_ge(rows_done, 1)
            pe.wait_ge(w_hi, 1)
            pe.wait_ge(x0_lo, 3)
            first_unit(0)
            pe.wait_ge(x0_lo, TT)
            first_unit(1).then_inc(w_used, 1)

            pe.wait_ge(x0_done, TT)
            pe.wait_ge(consts_set, 2)
            spread("pre0", 6)
            for u in range(1, 4):
                if u == 2:
                    unit(u, u, xh, xl)
                    continue
                pe.wait_ge(w_lo, u + 1)
                if u == 3:
                    pe.wait_ge(acc_empty, u - 1)
                    pe.wait_ge(small_loads, 16 * SMALL_LOADS)
                    for h in range(4):
                        last = pe.transpose(ps[:, 7, h * P:h * P + STREAMS * HIST], hist[0:STREAMS * HIST, tile(h)], ident[0:STREAMS * HIST, 0:STREAMS * HIST])
                    last.then_inc(hist_full, 1)
                for h in range(2):
                    part(u, banks4(u), xh, xl, 0, h, range(KB), KB)
                if u == 1:
                    pe.wait_ge(rs_done, 1)
                else:
                    pe.wait_ge(hist_done, 1)
                for h in range(2):
                    last = part(u, banks4(u), xh, xl, 1, h, range(KB), KB)
                last.then_inc(w_used, 1)
            pe.wait_ge(acc_empty, 3)

            def v_wait(t):
                if t == 4:
                    pe.wait_ge(acc_empty, 4)
            frames_unit(U_V, range(5), 0, wait=v_wait)
            pe.wait_ge(zeroed, 1)
            for n in range(2):
                for h in range(4):
                    last = pe.transpose(ps[:, 5 + n, tile(h)], wsn[:, n, h, :], ident)
                last.then_inc(ws_full, 1)
            pe.wait_ge(a_last_done, 1)
            pe.wait_ge(ws_done, 1)
            for gr in range(4):
                pe.transpose(ps[0:HIST, 7, tile(gr)], winA[:, gr, 1 + PROMPT:16 + PROMPT], ident)
                last = pe.transpose(ps[:, 5, tile(gr)], a_last[:, gr, :], ident)
            last.then_inc(last_a_full, 1)
            frames_unit(U_V + 1, range(5), 1, event=v_full)
            pe.wait_ge(last_a_done, 2)
            pe.wait_ge(ws_done, 2)
            for gr, b in enumerate((6, 4, 0, 2)):
                pe.wait_ge(pooled_done, 2 * gr + 2)
                pe.wait_ge(v_gelu, (1, 5, 5, 5)[gr])
                res = (winB, winC)[gr % 2]
                pe.matmul(span(b)[:, 0:PROMPT], wpool[:, gr, :], res[:, gr, 16:16 + PROMPT], start=True, stop=True)
                pe.matmul(span(b)[:, PROMPT:T], wpool[:, gr, :],
                          res[:, gr, 16 + PROMPT:].rearrange("p (b s) -> p b s", s=32)[:, :, 16:], start=True, stop=True).then_inc(ya_full, 1)
            for t, b in enumerate((6, 7, 4, 5, 6)):
                pe.wait_ge(v_done, t + 1)
                if t < 4:
                    pe.wait_ge(xl_done, X_OUT0 + (1, 1, 2, 2)[t])
                else:
                    pe.wait_ge(yb_done, 1)
                n = int(t == 4)
                for h in range(4):
                    last = pe.matmul(ps[:, b, tile(h)], v[:, t, tile(h)], wsT[:, n, h, :], start=True, stop=True)
                last.then_inc(yb_full, 1)
            def mixed(k):
                if k == 0:
                    pe.wait_ge(xl_done, X_OUT0 + 4)
                elif k == 4:
                    pe.wait_ge(yb_lo, TT)
            for m in range(3):
                if m == 1:
                    pe.wait_ge(yb_done, TT)
                unit(U_OUT0 + m, G_OUT0 + m, xh, xl, ready=mixed if m == 0 else None)
            last_y_unit(U_OUT0 + 3, BOUNDS[0], xh, xl, KB)
            boundary(BOUNDS[0], U_FF0)
            ffn(U_FF0, G_FF0, 0, BOUNDS[1])

            boundary(BOUNDS[1], U_QK, blocks=1)
            unit(U_QKS[1], G_QKS[1], xh, xl)
            pe.wait_ge(acc_empty, G_G + 1)
            pe.wait_ge(gate_loads, 32)
            for t, b in enumerate((6, 7, 4, 5, 6)):
                if t == 4:
                    pe.wait_ge(gx_done, 1)
                pe.matmul(ps[:, b, :], zf[:, tile(t)], w2[:], start=True, stop=True).then_inc(gate_full, 1)
            pe.wait_ge(gx_done, TT)
            unit(U_QKS[2], G_QKS[2], xh, xl)
            unit(U_QKS[3], G_QKS[3], xh, xl)
            pe.wait_ge(la_done, 1)
            for h, b in enumerate((4, 6, 0, 2)):
                pe.wait_ge(acc_empty, G_QKS[2 if h < 2 else 3] + 1)
                for t in range(TT):
                    last = pe.matmul(span(b)[:, tile(t)], la[:, t, tile(h)], tri[:, 1 if t < 4 else 2, :], start=True, stop=True)
                last.then_inc(cum_full, 1)
            for p, (banks, waits) in enumerate((((4, 5, 6, 7, 2), [(cum_done, 1), (cum_done, 1), (cum_done, 2), (cum_done, 2), (cum_done, 4)]),
                                                ((6, 7, 2, 0, 1), [(vv_done, 3), (vv_done, 4), (vv_done, 5), (cum_done, 4), (cum_done, 4)]))):
                frames_unit(U_VV + 2 * p, banks, 0, wait=lambda t: pe.wait_ge(*waits[t]))
                frames_unit(U_VV + 2 * p + 1, banks, 1, event=vv_full)
            for h, (b, n) in enumerate(((4, 5), (2, 8), (0, 10), (6, 10))):
                pe.wait_ge(vv_done, n)
                pe.wait_ge(head_done, h + 1)
                for t in range(TT):
                    last = pe.transpose(span(b)[:, tile(t)], cum[:, h, tile(t)], ident)
                last.then_inc(kt_full, 1)
            pe.wait_ge(kt_done, 4)

            def scores(t):
                for h in range(HEADS):
                    last = pe.matmul(ps[:, 0, tile(h)], qk[:, 4 + h, tile(t)], qk[:, h, tile(t)], start=True, stop=True)
                last.then_inc(att_full, 1)

            def streams(h):
                if h == 0:
                    scores(4)
                    pe.wait_ge(att_done, 1)
                    pe.wait_ge(cleared, 3)
                    pe.wait_ge(km_done, 2)
                if h >= 2:
                    pe.wait_ge(o_normed, SO_NORMED[0] if h == 2 else O_NORMED[0])
                pe.wait_ge(states_in[h % 2], 16 * (h // 2 + 1))
                out = ps[:, SO_BANK[h % 2], 0:DV]
                pe.matmul(out, att[:, 2, tile(h)], vv[:, 4, h * DV:(h + 1) * DV], start=True, stop=False, skip_group_check=True)
                for b in range(STREAMS):
                    q = slice(32 * (b // 2), 32 * (b // 2) + 32)
                    last = pe.matmul(out[q, :], qm[:, h, b % 2, q], Ss[:, h % 2, b, :], start=False, stop=(b == STREAMS - 1),
                                     skip_group_check=True)
                last.then_inc(so_full, 1)
                for q in range(4):
                    n = 4 * h + q
                    if n == 8:
                        pe.wait_ge(s_done, 2)
                    if n >= 4:
                        pe.wait_ge(ss_done, 2 * (n - 3))
                    rows_ = slice(32 * q, 32 * q + 32)
                    for odd in range(2):
                        last = pe.matmul(ps[:, KV_RING[q], odd * DV:(odd + 1) * DV], km[rows_, odd, tile(h)],
                                         vv[rows_, 4, h * DV:(h + 1) * DV], start=True, stop=True)
                    last.then_inc(skv_full, 1)

            def chunk(c):
                t, odd = divmod(c, 2)
                r0 = CHUNK * odd
                mine = slice(r0, r0 + CHUNK)
                if not odd:
                    pe.wait_ge(att_done, t + 1)
                    scores(t)
                if c == 0:
                    pe.wait_ge(ss_done, 4 * STREAMS // 2)
                    pe.wait_ge(cleared, 3)
                else:
                    pe.wait_ge(s_done, c)
                for h in range(HEADS):
                    last = pe.matmul(span(1, D)[:, h * DV:(h + 1) * DV], kend[mine, t, tile(h)],
                                     vv[mine, t, h * DV:(h + 1) * DV], start=True, stop=True)
                last.then_inc(kv_full, 1)
                pe.wait_ge(att_done, t + 2)
                if not odd:
                    pe.wait_ge(o_normed, O_NORMED[t] - 1)
                for h in range(HEADS):
                    out = span(3, D)[:, h * DV:(h + 1) * DV]
                    if not odd:
                        pe.matmul(out, att[:, t % 2, tile(h)], vv[:, t, h * DV:(h + 1) * DV], start=(h % 2 == 0), stop=False, skip_group_check=True)
                for h in range(HEADS):
                    out = span(3, D)[mine, h * DV:(h + 1) * DV]
                    last = pe.matmul(out, qk[:, h, c * CHUNK:(c + 1) * CHUNK], S[:, c % 2, h, :], start=False, stop=True, skip_group_check=True)
                last.then_inc(o_full, 1)

            def r_tile(p, t):
                n = p * TT + t
                if n == 0:
                    pe.wait_ge(ss_done, HEADS * STREAMS)
                if n >= 2:
                    pe.wait_ge(r_done, n - 1)
                for j in range(2):
                    u = U_R + 2 * p + j
                    pe.wait_ge(w_lo, u + 1)
                    for k in range(KB):
                        for m, (w, mv_) in enumerate(((wh, xh), (wl, xh), (wh, xl))):
                            last = pe.matmul(ps[:, 5 + n % 2, j * UW:(j + 1) * UW], mv_[:, k, tile(t)], w[:, u % 2, k, :],
                                             start=(k == 0 and m == 0), stop=(k == KB - 1 and m == 2))
                    if t == TT - 1:
                        last.then_inc(w_used, 1)
                    elif j:
                        last.then_inc(r_tile_full, 1)

            for what, *n in CORE:
                {"streams": streams, "chunk": chunk, "r": r_tile}[what](*n)
            pe.wait_ge(gated, TT)
            for k in range(KB):
                if k < 2:
                    pe.wait_ge(o_normed, HEADS + 4)
                    pe.wait_ge(s_done, 8)
                else:
                    pe.wait_ge(xl_done, X_OUT1 + k - 1)
                for t in range(TT):
                    last = pe.transpose(span(2 * (k % 2))[:, tile(t)], rg[:, t, tile(k)], ident)
                last.then_inc(gated_full, 1)
            for m in range(3):
                if m == 0:
                    pe.wait_ge(r_done, 2 * TT)
                unit(U_OUT1 + m, G_OUT1 + m, xh, xl, ready=(lambda k: pe.wait_ge(xl_done, X_OUT1 + k + 1)) if m == 0 else None)
            last_y_unit(U_OUT1 + 3, BOUNDS[2], xh, xl, KB)
            boundary(BOUNDS[2], U_FF1)
            last_ffn(U_FF1, G_FF1, sum(n for _, n in FF_PARTS))

        @block.vector
        def _(dve):
            steps = [0]

            def step(ins, n=1):
                steps[0] += n
                ins.then_inc(dve_step, 1)
                dve.wait_ge(dve_step, steps[0])

            def lo(u, di=0):
                dve.wait_ge(w_hi, di + (u + 1))
                s = u % 2
                dve.tensor_tensor(wl[:, s].rearrange("p k c -> p (k c)"), stage[:, s, :],
                                  f32(wh[:, s].rearrange("p k c -> p (k c)")), ALU.subtract).then_inc(w_lo, 1)

            def scaled(dst, u, g, di=0):
                dve.wait_ge(w_used, di + (u + 1))
                dve.tensor_tensor(dst, banks4(g), rs_twice(), ALU.mult).then_inc(acc_empty, 1)

            def norm(name, bank, width=D):
                n = NORM[name]
                if bank is not None:
                    dve.wait_ge(sums_full, n)
                    src = ps[:, bank, 0:TT]
                else:
                    dve.wait_ge(x0_sums, TT)
                    src = ss[:, 0:TT]
                dve.tensor_scalar(ms[:, 0:TT], src, 1.0 / width, EPS, ALU.mult, ALU.add).then_inc(ms_done, 1)
                dve.wait_ge(rstd_done, n + 1)
                dve.tensor_tensor(diag[:], ident.unsqueeze(1).broadcast_to([P, TT, P]),
                                  rstd_of(name).unsqueeze(2).broadcast_to([P, TT, P]), ALU.mult).then_inc(diag_done, 1)

            def x_lo(k, row, n):
                dve.wait_ge(xh_done, n + 1)
                dve.scalar_tensor_tensor(xl[:, k, :], x[:, k, :], gain(row + k), f32(xh[:, k, :]), ALU.mult, ALU.subtract).then_inc(xl_done, 1)

            def y_out(u, g, m, add, di=0):
                dve.wait_ge(w_used, di + (u + 1))
                if add:
                    dve.tensor_tensor(two(y, m), two(y, m), banks4(g), ALU.add).then_inc(acc_empty, 1)
                else:
                    dve.tensor_copy(two(y, m), banks4(g)).then_inc(acc_empty, 1)

            def y_units(u, B, add):
                g = B["g"] - 4
                for m in range(3):
                    y_out(u + m, g + m, 2 * m, add)
                    lo(u + m + 2)
                    if m:
                        dve.wait_ge(squares, 6 * B["n"] + m + 1)
                        if m == 2:
                            dve.wait_ge(squares_added, 4 * B["n"] + 1)
                        dve.tensor_tensor(acc[:], acc[:], sq[:], ALU.add).then_inc(squares_added, 1)
                dve.wait_ge(squares_added, 4 * B["n"] + 2)
                dve.tensor_tensor(acc[:, 0], acc[:, 0], acc[:, 1], ALU.add).then_inc(squares_added, 1)

                def piece(m, h):
                    dst, src = y[:, 6 + m, h], banks4(g + 3)[:, m, :, :] if h.stop - h.start > HALF else banks4(g + 3)[:, m, h.start // HALF, :]
                    if h.stop - h.start > HALF:
                        dst = halved(dst)
                    return dve.tensor_tensor(dst, dst, src, ALU.add) if add else dve.tensor_copy(dst, src)
                dve.wait_ge(y_blocks_full, 2 * B["n"] + 1)
                piece(0, slice(0, T)).then_inc(y_stands, 1)
                dve.wait_ge(y_blocks_full, 2 * B["n"] + 2)
                piece(1, slice(0, HALF)).then_inc(y_stands, 1)
                dve.wait_ge(squares, 6 * B["n"] + 4)
                dve.wait_ge(squares_added, 4 * B["n"] + 3)
                dve.tensor_tensor(acc[:, 0], acc[:, 0], sq[:, 0], ALU.add).then_inc(squares_added, 1)
                dve.wait_ge(w_used, u + 4)
                piece(1, slice(HALF, T)).then_inc(acc_empty, 1)

            def boundary(B):
                behind, ahead, bank = norm_banks(B["g"])
                norm(B["post"], bank)
                dve.wait_ge(r_full, NORM[B["post"]] + 1)
                r = ps[:, behind:behind + 2, 0:HALF]
                for k in range(KB):
                    dve.scalar_tensor_tensor(halved(y[:, k, :]), halved(y[:, k, :]), gain(B["gp"] + k), r, ALU.mult, ALU.mult).then_inc(y_scaled, 1)
                    if k in ADDED_BY_DVE:
                        dve.wait_ge(y_scaled, KB * B["n"] + k + 1)
                        dve.tensor_tensor(x[:, k, :], x[:, k, :], y[:, k, :], ALU.add).then_inc(x_added_dve, 1)
                    if k:
                        x_lo(k - 1, B["gq"], B["x"] + k - 1)
                x_lo(KB - 1, B["gq"], B["x"] + KB - 1)
                for j in range(4):
                    if j < 3:
                        dve.wait_ge(x_squares, KB * B["n"] + 2 * j + 4)
                    if j:
                        dve.wait_ge(x_squares_added, 4 * B["n"] + j)
                    first, second, out = ((y[:, 0:2], y[:, 2:4], acc[:]), (acc[:], y[:, 4:6], acc[:]), (acc[:], y[:, 6:8], acc[:]),
                                          (acc[:, 0], acc[:, 1], acc[:, 0]))[j]
                    dve.tensor_tensor(out, first, second, ALU.add).then_inc(x_squares_added, 1)
                norm(B["pre"], bank)
                dve.wait_ge(rs_done, 2 + B["n"])

            def gate_up(u, g, pair, pairs):
                with dve.Fori(0, pairs) as i:
                    scaled(two(gate, 0), u, g, di=i * 2)
                    lo(u + 2, di=i * 2)
                    scaled(two(up, 0), u + 1, g + 1, di=i * 2)
                    dve.wait_ge(silu_done, i + (pair + 1))
                    dve.wait_ge(acc_empty, i * 2 + (g + 2))
                    dve.tensor_tensor(up[:], up[:], gate[:], ALU.mult).then_inc(hid_done, 1)
                    lo(u + 3, di=i * 2)
                    dve.wait_ge(hid_hi, i + (pair + 1))
                    dve.tensor_tensor(hl[:, bass.ds(i * 2, 2), :], up[:], f32(hh[:, bass.ds(i * 2, 2), :]), ALU.subtract).then_inc(hid_lo, 1)
                    dve.wait_ge(hid_lo, i + (pair + 1))

            def ffn(u, g, pair, B):
                for n, (f, pairs) in enumerate(FF_PARTS):
                    gate_up(u, g, pair, pairs)
                    u, g, pair = u + 2 * pairs, g + 2 * pairs, pair + pairs
                    if n < len(FF_PARTS) - 1:
                        with dve.Fori(0, 2) as i:
                            for j in range(2):
                                if n:
                                    dve.wait_ge(acc_empty, i * 2 + (g + j))
                                y_out(u + j, g + j, i * 4 + 2 * j, n > 0, di=i * 2)
                                lo(u + j + 2, di=i * 2)
                    else:
                        y_units(u, B, True)
                        lo(u + 5)
                    u, g = u + 4, g + 4

            def y_tile(n, t, cols, add, bank):
                dst = yF[:, t, cols]
                ins = dve.tensor_tensor(dst, dst, ps[:, bank, 0:UW], ALU.add) if add else dve.tensor_copy(dst, ps[:, bank, 0:UW])
                ins.then_inc(y_tile_out, 1)

            def last_ffn(u, g, pair):
                for n, (f, pairs) in enumerate(FF_PARTS):
                    gate_up(u, g, pair, pairs)
                    u, g, pair = u + 2 * pairs, g + 2 * pairs, pair + pairs
                    if n < len(FF_PARTS) - 1:
                        with dve.Fori(0, 2) as i:
                            for j in range(2):
                                for t in range(TT):
                                    if j == 0 or t == TT - 1:
                                        if t in (0, TT - 1):
                                            dve.wait_ge(w_used, i * 2 + (u + j + 1))
                                    else:
                                        dve.wait_ge(y_tile_full, i * 4 + (8 * n + t + 1))
                                    y_tile(n, t, bass.ds(i * (2 * UW) + j * UW, UW), n > 0, tile_bank(j, t))
                                lo(u + j + 2, di=i * 2)
                        u += 4
                for m in range(4):
                    for t in range(TT):
                        if m % 2 == 0 or t == TT - 1:
                            dve.wait_ge(w_used, u + m + 1)
                        else:
                            dve.wait_ge(y_tile_full, 8 * n + 4 * (m // 2) + t + 1)
                        y_tile(n, t, slice(m * UW, (m + 1) * UW), True, tile_bank(m % 2, t))
                        if m < 3:
                            continue
                        if t == 0:
                            dve.wait_ge(y_tile_sq, 3 * TT)
                            step(dve.tensor_tensor(ss[:, 0:5], ss[:, 0:5], ss[:, 5:10], ALU.add))
                            step(dve.tensor_tensor(ss[:, 0:5], ss[:, 0:5], ss[:, 10:15], ALU.add))
                            step(dve.tensor_scalar(ss[:, 0:5], ss[:, 0:5], 1.0 / D, EPS, ALU.mult, ALU.add))
                        dve.wait_ge(y_tile_out, 20 * n + 5 * m + t + 1)
                        dve.tensor_tensor(yg[:, t, :], yF[:, t, D - UW:], gF[:, D - UW:], ALU.mult)
                        dve.wait_ge(y_tile_sq, 3 * TT + t + 1)
                        dve.scalar_tensor_tensor(ms[:, t:t + 1], ss[:, 15 + t:16 + t], 1.0 / D, ss[:, t:t + 1], ALU.mult, ALU.add).then_inc(tile_ms, 1)
                        dve.wait_ge(tile_rstd, t + 1)
                        r = rstd[:, t:t + 1]
                        if t == 0:
                            dve.wait_ge(y_gained, 3 * TT)
                            dve.wait_ge(xF_done, TT)
                        rest, last = slice(0, D - UW), slice(D - UW, D)
                        dve.scalar_tensor_tensor(yF[:, t, rest], yF[:, t, rest], r, xF[:, t, rest], ALU.mult, ALU.add).then_inc(out_ready, 1)
                        dve.scalar_tensor_tensor(yF[:, t, last], yg[:, t, :], r, xF[:, t, last], ALU.mult, ALU.add).then_inc(out_ready, 1)
                    if u + m + 2 < UNITS:
                        lo(u + m + 2)

            def rstd_of(name):
                return (rpre if name.startswith("pre") else rstd[:, 0:TT])

            dve.memset(ones[:], 1.0).then_inc(consts_set, 1)
            dve.memset(minus_half, -0.5).then_inc(consts_set, 1)
            dve.wait_ge(rows_full, 1)
            dve.tensor_copy(gains[:], ps[:, 0, 0:ROWS]).then_inc(rows_done, 1)
            dve.wait_ge(rows_done, 1)
            def x0_low(t):
                dve.wait_ge(x0_hi, t + 1)
                dve.tensor_tensor(xl[:, :, tile(t)], xg[:, t % 2], f32(xh[:, :, tile(t)]), ALU.subtract).then_inc(x0_lo, 1)

            for t in range(TT):
                dve.wait_ge(x0_full, t + 1)
                if t >= 2:
                    dve.wait_ge(x0_lo, t - 1)
                dve.tensor_tensor(xg[:, t % 2], span(4 + 2 * (t % 2), D).rearrange("p (k n) -> p k n", n=P),
                                  gains[:, PRE_MIX:PRE_MIX + KB].unsqueeze(2).broadcast_to([P, KB, P]), ALU.mult).then_inc(xg_done, 1)
                if t:
                    x0_low(t - 1)
                if t == 3:
                    lo(0)
            x0_low(TT - 1)
            norm("pre0", None)
            lo(1)

            dve.wait_ge(rs_done, 1)
            stream_r = rs[:, PROMPT:].rearrange("p (b s) -> p b s", s=STEP)
            for u in range(4):
                if u < 2:
                    dve.wait_ge(w_used, u + 1)
                    src = banks4(u)
                    dst = winA[:, 2 * u:2 * u + 2, :]
                    n = PROMPT - HALF
                    dve.tensor_tensor(dst[:, :, 16:16 + HALF], src[:, :, 0, :], rs[:, 0:HALF].unsqueeze(1).broadcast_to([P, 2, HALF]), ALU.mult)
                    dve.tensor_tensor(dst[:, :, 16 + HALF:16 + PROMPT], src[:, :, 1, 0:n],
                                      rs[:, HALF:PROMPT].unsqueeze(1).broadcast_to([P, 2, n]), ALU.mult)
                    for m in range(2):
                        last = dve.tensor_tensor(dst[:, m, 16 + PROMPT:].rearrange("p (b s) -> p b s", s=32)[:, :, 16:],
                                                 src[:, m, 1, n:].rearrange("p (b s) -> p b s", s=STEP), stream_r, ALU.mult)
                    last.then_inc(acc_empty, 1)
                else:
                    scaled(two(uT, 2 * (u - 2)), u, u)
                if u == 2:
                    dve.wait_ge(hist_full, 1)
                    dve.wait_ge(zeroed, 3)
                    dve.tensor_copy(winA[:, :, 16 + PROMPT:].rearrange("p g (b s) -> p g b s", s=32)[:, :, :, 1:16],
                                    ps[:, 7, :].rearrange("p (g n) -> p g n", g=4)[:, :, 0:STREAMS * HIST].rearrange("p g (b s) -> p g b s", s=HIST)).then_inc(hist_done, 1)
                lo(u + 2)
            dve.wait_ge(small_loads, 16 * SMALL_LOADS)
            dve.tensor_copy(bs[:, 1, :].rearrange("p (h b s) -> p h b s", h=4, s=STEP),
                            bs[:, 0, :].rearrange("p (h t) -> p h t", h=4)[:, :, 0:STEP].unsqueeze(2).broadcast_to([P, 4, STREAMS, STEP]))
            for n in range(2):
                dve.wait_ge(ws_full, n + 1)
                dve.tensor_tensor(wsT[:, n], ps[:, 5 + n, :].rearrange("p (h t) -> p h t", h=4),
                                  tri[:, 2 * n:2 * n + 1, :].broadcast_to([P, 4, P]), ALU.mult).then_inc(ws_done, 1)
            dve.wait_ge(windows_done, 1)
            for gr, w in enumerate(WINDOWS):
                s = (winB, winC)[gr % 2][:, gr, :]
                own = winA[:, gr, :]
                dve.scalar_tensor_tensor(s[:, 16:16 + PROMPT], s[:, 16:16 + PROMPT], 1.0 / w, own[:, 16:16 + PROMPT], ALU.mult, ALU.subtract).then_inc(pooled_done, 1)
                s, own = (t_[:, 16 + PROMPT:].rearrange("p (b s) -> p b s", s=32)[:, :, 16:] for t_ in (s, own))
                dve.scalar_tensor_tensor(s, s, 1.0 / w, own, ALU.mult, ALU.subtract).then_inc(pooled_done, 1)
            lo(U_OUT0)
            def v_stats(t):
                m = mv[:, 2 * (t % 2):2 * (t % 2) + 2]
                dve.wait_ge(v_gelu, t + 1)
                step(dve.bn_stats(bn6, gv[:, t % 2, :]))
                step(dve.bn_aggr(m, bn6))
                dve.tensor_scalar(vms[:, t % 2:t % 2 + 1], m[:, 1:2], EPS, None, ALU.add).then_inc(vms_done, 1)
            v_stats(0)
            for t in range(TT):
                if t + 1 < TT:
                    v_stats(t + 1)
                dve.wait_ge(vrstd_done, t + 1)
                dve.tensor_scalar(v[:, t, :], gv[:, t % 2, :], mv[:, 2 * (t % 2):2 * (t % 2) + 1], vrstd[:, t:t + 1], ALU.subtract, ALU.mult).then_inc(v_normed, 1)
                dve.wait_ge(v_normed, t + 1)
                dve.tensor_tensor(v[:, t, :], v[:, t, :], lng[:], ALU.mult).then_inc(v_gained, 1)
            for gr, b in enumerate((6, 4, 0, 2)):
                dve.wait_ge(xh_done, X_OUT0 + gr + 1)
                dve.scalar_tensor_tensor(xl[:, gr, :], span(b), gain(POOL_SCALE + gr), f32(xh[:, gr, :]), ALU.mult, ALU.subtract).then_inc(xl_done, 1)
            dve.wait_ge(u_done, 2)

            def yb_low(t):
                dve.wait_ge(yb_hi, t + 1)
                dve.tensor_tensor(xl[:, 4:8, tile(t)], uT[:, :, tile(t)], f32(xh[:, 4:8, tile(t)]), ALU.subtract).then_inc(yb_lo, 1)
            for t, b in enumerate((6, 7, 4, 5, 6)):
                dve.wait_ge(yb_full, t + 1)
                step(dve.tensor_tensor(ps[:, b, :], ps[:, b, :], bs[:, int(t == 4), :], ALU.add))
                dve.tensor_tensor(uT[:, :, tile(t)], ps[:, b, :].rearrange("p (h t) -> p h t", h=4), uT[:, :, tile(t)], ALU.mult).then_inc(yb_done, 1)
                if t:
                    yb_low(t - 1)
            yb_low(TT - 1)
            lo(U_OUT0 + 1)
            dve.wait_ge(mixer_stores, 16 * MIXER_STORES)
            y_units(U_OUT0, BOUNDS[0], False)
            lo(U_OUT0 + 5)
            boundary(BOUNDS[0])
            ffn(U_FF0, G_FF0, 0, BOUNDS[1])
            boundary(BOUNDS[1])

            for j, u in enumerate(U_QKS):
                scaled(two(qk, 2 * j), u, G_QKS[j])
                lo(u + 2)
                if j == 0:
                    dve.wait_ge(w_used, U_G + 1)
                    dve.tensor_tensor(halved(zf[:]), banks4(G_G)[:, 0], halved(rs[:]), ALU.mult).then_inc(acc_empty, 1)
                    lo(U_G + 2)
                if j == 1:
                    for t, b in enumerate((6, 7, 4, 5, 6)):
                        dve.wait_ge(gate_full, t + 1)
                        dve.tensor_tensor(la[:, t, :], ps[:, b, :], bg[:], ALU.add).then_inc(gx_done, 1)
                    dve.wait_ge(gx_done, TT)
                    step(dve.tensor_scalar(lmin[:], la[:], 0.0, None, ALU.min))
                    dve.scalar_tensor_tensor(la[:], lmin[:], -2.0, la[:], ALU.mult, ALU.add).then_inc(gabs_done, 1)
                if j == 2:
                    dve.wait_ge(gln_done, 1)
                    dve.tensor_tensor(la[:], lmin[:], la[:], ALU.subtract).then_inc(la_done, 1)
            for h in range(HEADS):
                dve.wait_ge(cum_done, h + 1)
                ends = bend.rearrange("p (n c) -> p n c", n=2)
                c = cum[:, h, :]
                prompt = c[:, 0:PROMPT].rearrange("p (c s) -> p c s", s=CHUNK)
                each = c[:, PROMPT:].rearrange("p (b s) -> p b s", s=STEP)
                dve.tensor_copy(ends[:, 0, :].unsqueeze(2), prompt[:, :, CHUNK - 1:])
                dve.tensor_copy(ends[:, 1, :].unsqueeze(2), each[:, :, STEP - 1:]).then_inc(bend_done, 1)
                dve.wait_ge(bend_done, h + 1)
                dve.wait_ge(exps_done, h + 1)
                dve.tensor_tensor(prompt, ends[:, 0, :].unsqueeze(2).broadcast_to([P, 8, CHUNK]), prompt, ALU.subtract)
                dve.tensor_tensor(each, ends[:, 1, :].unsqueeze(2).broadcast_to([P, 8, STEP]), each, ALU.subtract).then_inc(dist_done, 1)
                dve.scalar_tensor_tensor(qk[:, h, :], qk[:, h, :], DK ** -0.5, eq[:], ALU.mult, ALU.mult)
                dve.wait_ge(dist_exp, h + 1)
                dve.tensor_tensor(c, c, qk[:, 4 + h, :], ALU.mult)
                dve.tensor_tensor(qk[:, 4 + h, :], qk[:, 4 + h, :], ek[:], ALU.mult).then_inc(head_done, 1)
                lo(U_VV + h + 2)
            dve.wait_ge(cleared, 3)
            norms, squared = [0], [0]

            def masked(n, slot, mask):
                dve.wait_ge(att_full, n + 1)
                dve.copy_predicated(att[:, slot, :].rearrange("p (h t) -> p h t", h=HEADS),
                                    tri[:, mask:mask + 1, :].bitcast(U32).broadcast_to([P, HEADS, P]),
                                    ps[:, 0, :].rearrange("p (h t) -> p h t", h=HEADS)).then_inc(att_done, 1)

            def normed(t, heads):
                norms[0] += 1
                n, c0 = norms[0], 4 * t + heads[0]
                squared[0] += len(heads)
                dve.wait_ge(o_squared, squared[0])
                cols = slice(c0, c0 + len(heads))
                dve.tensor_scalar(ms[:, cols], ss[:, cols], 1.0 / DV, EPS, ALU.mult, ALU.add).then_inc(o_ms, 1)
                dve.wait_ge(o_rstd, n)
                for h in heads:
                    src = span(3, D)[:, h * DV:(h + 1) * DV] if len(heads) > 1 else ps[:, SO_BANK[h % 2], 0:DV]
                    last = dve.tensor_scalar(qk[:, 2 * h:2 * h + 2, tile(t)], src.rearrange("p (v n) -> p v n", v=2),
                                             rstd[:, 4 * t + h:4 * t + h + 1], None, ALU.mult)
                last.then_inc(o_normed, 1)

            for what, *n in CORE:
                if what == "streams":
                    h, = n
                    if h == 0:
                        masked(0, 2, 2)
                    dve.wait_ge(so_full, h + 1)
                    for q in range(4):
                        dve.wait_ge(skv_full, 4 * h + q + 1)
                        for odd in range(2):
                            b = 2 * q + odd
                            dve.scalar_tensor_tensor(Ss[:, h % 2, b, :], Ss[:, h % 2, b, :], elast[:, h, STREAMS + b:STREAMS + b + 1],
                                                     ps[:, KV_RING[q], odd * DV:(odd + 1) * DV], ALU.mult, ALU.add).then_inc(ss_done, 1)
                    normed(4, [h])
                elif what == "chunk":
                    c, = n
                    t, odd = divmod(c, 2)
                    if not odd:
                        if t >= 2:
                            dve.wait_ge(o_full, 2 * t - 2)
                        masked(t + 1, t % 2, 1)
                    dve.wait_ge(kv_full, c + 1)
                    if c:
                        dve.wait_ge(o_full, c)
                        dve.wait_ge(s_done, c)
                    for h in range(HEADS):
                        last = dve.scalar_tensor_tensor(S[:, 1 - odd, h, :], S[:, odd, h, :], elast[:, h, c:c + 1],
                                                        span(1, D)[:, h * DV:(h + 1) * DV], ALU.mult, ALU.add)
                    last.then_inc(s_done, 1)
                    if odd:
                        normed(t, list(range(HEADS)))
                else:
                    p, t = n
                    if p:
                        dve.wait_ge(r_done, TT + t + 1)
                        dve.wait_ge(o_normed, len(_NORMS) if t > 1 else O_NORMED[t])
                        dve.tensor_tensor(rg[:, t, :].rearrange("p (k n) -> p k n", n=P), rg[:, t, :].rearrange("p (k n) -> p k n", n=P),
                                          qk[:, :, tile(t)], ALU.mult).then_inc(gated, 1)
                    if t == TT - 1:
                        lo(U_R + 2 * p + 2)
                        lo(U_R + 2 * p + 3)
            for k in range(KB):
                dve.wait_ge(xh_done, X_OUT1 + k + 1)
                dve.scalar_tensor_tensor(xl[:, k, :], span(2 * (k % 2)), gain(O_NORM + k), f32(xh[:, k, :]), ALU.mult, ALU.subtract).then_inc(xl_done, 1)
            y_units(U_OUT1, BOUNDS[2], False)
            lo(U_OUT1 + 5)
            boundary(BOUNDS[2])
            dve.wait_ge(prompt_out, 16)
            dve.wait_ge(gain_load, 16)
            last_ffn(U_FF1, G_FF1, sum(n for _, n in FF_PARTS))

        @block.scalar
        def _(act):
            def hi(u, di=0):
                s = u % 2
                n = di * 8 if not isinstance(di, int) else 0
                act.wait_ge(w_loaded[s], n + 16 * (u // 2 + 1))
                if u >= 2:
                    act.wait_ge(w_used, di + (u - 1))
                act.activation(wh[:, s].rearrange("p k c -> p (k c)"), stage[:, s, :], ACT.Copy).then_inc(w_hi, 1)

            def x_hi(k, row):
                act.activation(xh[:, k, :], x[:, k, :], ACT.Copy, scale=gain(row + k)).then_inc(xh_done, 1)

            def y_units(u, B):
                n, g = B["n"], B["g"] - 4
                for m in range(3):
                    hi(u + m + 2)
                    act.wait_ge(acc_empty, g + m + 1)
                    if m == 2:
                        act.wait_ge(squares_added, 4 * n + 1)
                    act.activation((acc, sq, sq)[m][:], y[:, 2 * m:2 * m + 2, :], ACT.Square).then_inc(squares, 1)
                act.wait_ge(y_stands, 2 * n + 1)
                act.wait_ge(squares_added, 4 * n + 2)
                act.activation(sq[:, 0], y[:, 6, :], ACT.Square).then_inc(squares, 1)
                act.wait_ge(y_stands, 2 * n + 2)
                act.activation(sq[:, 1, 0:HALF], y[:, 7, 0:HALF], ACT.Square).then_inc(squares, 1)
                act.wait_ge(acc_empty, g + 4)
                act.activation(sq[:, 1, HALF:], y[:, 7, HALF:], ACT.Square).then_inc(squares, 1)
                hi(u + 5)

            def rs_copy(n, b):
                act.wait_ge(r_full, n + 1)
                act.activation(halved(rs[:]), ps[:, b:b + 2, 0:HALF], ACT.Copy).then_inc(rs_done, 1)

            def boundary(B):
                for k in range(KB):
                    wait_x_added(act, B["n"], k)
                    x_hi(k, B["gq"])
                    act.activation(y[:, k, :], x[:, k, :], ACT.Square).then_inc(x_squares, 1)
                rs_copy(NORM[B["pre"]], norm_banks(B["g"])[1])

            def gate_up(u, g, pair, pairs):
                with act.Fori(0, pairs) as i:
                    hi(u + 2, di=i * 2)
                    act.wait_ge(acc_empty, i * 2 + (g + 1))
                    act.activation(gate[:], gate[:], ACT.Silu).then_inc(silu_done, 1)
                    hi(u + 3, di=i * 2)
                    act.wait_ge(hid_done, i + (pair + 1))
                    act.activation(hh[:, bass.ds(i * 2, 2), :], up[:], ACT.Copy).then_inc(hid_hi, 1)

            def ffn(u, g, pair, B):
                for n, (f, pairs) in enumerate(FF_PARTS):
                    gate_up(u, g, pair, pairs)
                    u, g, pair = u + 2 * pairs, g + 2 * pairs, pair + pairs
                    if n < len(FF_PARTS) - 1:
                        with act.Fori(0, 2) as i:
                            for j in range(2):
                                hi(u + j + 2, di=i * 2)
                    else:
                        y_units(u, B)
                    u, g = u + 4, g + 4

            def last_ffn(u, g, pair):
                for n, (f, pairs) in enumerate(FF_PARTS):
                    gate_up(u, g, pair, pairs)
                    u, g, pair = u + 2 * pairs, g + 2 * pairs, pair + pairs
                    if n < len(FF_PARTS) - 1:
                        with act.Fori(0, 2) as i:
                            for j in range(2):
                                hi(u + j + 2, di=i * 2)
                        u += 4
                for t in range(TT):
                    act.wait_ge(xF_full, t + 1)
                    act.activation(xF[:, t, :], span(xF_bank(t), D), ACT.Copy).then_inc(xF_done, 1)
                for m in range(4):
                    if u + m + 2 < UNITS:
                        hi(u + m + 2)
                    for t in range(TT):
                        act.wait_ge(y_tile_out, 20 * n + 5 * m + t + 1)
                        if m or t:
                            act.wait_ge(y_tile_sq, 5 * m + t)
                        act.activation(rs[:, 0:UW], yF[:, t, m * UW:(m + 1) * UW], ACT.Square,
                                       accum_out=ss[:, 5 * m + t:5 * m + t + 1]).then_inc(y_tile_sq, 1)

            for t in range(TT):
                act.wait_ge(xg_done, t + 1)
                act.activation(xh[:, :, tile(t)], xg[:, t % 2], ACT.Copy).then_inc(x0_hi, 1)
                act.wait_ge(x0_full, t + 1)
                act.activation(x[:, :, tile(t)], span(4 + 2 * (t % 2), D).rearrange("p (k n) -> p k n", n=P), ACT.Copy).then_inc(x0_done, 1)
                if t == 0:
                    hi(0)
            for t in range(TT):
                if t:
                    act.wait_ge(x0_sums, t)
                act.activation(junk[:], xin[:, t, :], ACT.Square, accum_out=ss[:, t:t + 1]).then_inc(x0_sums, 1)
            hi(1)
            rs_copy(0, 6)
            for u in range(4):
                hi(u + 2)
                if u >= 2:
                    act.wait_ge(acc_empty, u + 1)
                    act.activation(uT[:, 2 * (u - 2):2 * (u - 1), :], uT[:, 2 * (u - 2):2 * (u - 1), :], ACT.Gelu_apprx_tanh).then_inc(u_done, 1)
            act.activation(a_last[:].rearrange("p g (b s) -> p g b s", s=STEP),
                           winA[:, :, 16 + PROMPT:].rearrange("p g (b s) -> p g b s", s=32)[:, :, :, 16:], ACT.Copy).then_inc(a_last_done, 1)
            hi(U_OUT0)
            act.wait_ge(last_a_full, 1)
            act.activation(a_out[0:HIST, 0, :], ps[0:HIST, 7, :], ACT.Copy).then_inc(last_a_done, 1)
            act.activation(a_out[:, 1, :], ps[:, 5, :], ACT.Copy).then_inc(last_a_done, 1)
            act.wait_ge(last_a_done, 2)
            act.dma_start(a["pool_prompt"][0, 0], a_out[0:HIST, 0, :]).then_inc(mixer_stores, 16)
            for b in range(STREAMS):
                act.dma_start(a["pool_sample"][0, b], a_out[b * STEP + 1:(b + 1) * STEP, 1, :]).then_inc(mixer_stores, 16)
            for t in range(TT):
                if t < 4:
                    act.wait_ge(v_full, t + 1)
                else:
                    act.wait_ge(w_used, U_V + 2)
                if t >= 2:
                    act.wait_ge(v_normed, t - 1)
                act.activation(gv[:, t % 2, :], ps[:, t, :], ACT.Gelu_apprx_tanh, scale=rpre[:, t:t + 1]).then_inc(v_gelu, 1)
            hi(U_OUT0 + 1)
            for gr, b in enumerate((6, 4, 0, 2)):
                act.wait_ge(ya_full, gr + 1)
                act.activation(xh[:, gr, :], span(b), ACT.Copy, scale=gain(POOL_SCALE + gr)).then_inc(xh_done, 1)
            for t in range(TT):
                act.wait_ge(yb_done, t + 1)
                act.activation(xh[:, 4:8, tile(t)], uT[:, :, tile(t)], ACT.Copy).then_inc(yb_hi, 1)
            act.wait_ge(v_done, TT)
            act.dma_start(a["sg_v_sample"][0].rearrange("b s d -> (b s) d"), v[:, 4, :]).then_inc(mixer_stores, 16)
            act.wait_ge(mixer_stores, 16 * MIXER_STORES)
            y_units(U_OUT0, BOUNDS[0])
            boundary(BOUNDS[0])
            ffn(U_FF0, G_FF0, 0, BOUNDS[1])
            boundary(BOUNDS[1])
            hi(U_QK + 2)
            hi(U_QK + 3)
            hi(U_QK + 4)
            act.wait_ge(gabs_done, 1)
            act.activation(la[:], la[:], ACT.Exp, scale=-1.0).then_inc(act_step, 1)
            act.wait_ge(act_step, 1)
            act.activation(la[:], la[:], ACT.Ln, bias=1.0).then_inc(gln_done, 1)
            hi(U_QK + 5)
            hi(U_QK + 6)
            for h, b in enumerate((4, 6, 0, 2)):
                act.wait_ge(cum_full, h + 1)
                act.activation(cum[:, h, :], span(b), ACT.Copy, scale=1.0 / TAU).then_inc(cum_done, 1)

            def exps(h):
                act.wait_ge(cum_done, h + 1)
                if h:
                    act.wait_ge(head_done, h)
                act.activation(eq[:], cum[:, h, :], ACT.Exp)
                act.activation(ek[:], cum[:, h, :], ACT.Exp, scale=-1.0)
                act.wait_ge(bend_done, h + 1)
                act.activation(elast[:, h, :], bend, ACT.Exp).then_inc(exps_done, 1)
                act.wait_ge(dist_done, h + 1)
                act.activation(cum[:, h, :], cum[:, h, :], ACT.Exp).then_inc(dist_exp, 1)

            def v_copy(p, banks):
                for t, b in enumerate(banks):
                    if t < 4:
                        act.wait_ge(vv_full, 4 * p + t + 1)
                    else:
                        act.wait_ge(w_used, U_VV + 2 * p + 2)
                    act.activation(vv[:, t, p * 512:(p + 1) * 512], ps[:, b, :], ACT.Copy, scale=rpre[:, t:t + 1]).then_inc(vv_done, 1)
            exps(0)
            hi(U_VV + 2)
            exps(1)
            v_copy(0, (4, 5, 6, 7, 2))
            hi(U_VV + 3)
            exps(2)
            hi(U_VV + 4)
            exps(3)
            v_copy(1, (6, 7, 2, 0, 1))
            hi(U_VV + 5)
            for h, b in enumerate((4, 2, 0, 6)):
                act.wait_ge(kt_full, h + 1)
                act.activation(kend[:, :, tile(h)], span(b).rearrange("p (t n) -> p t n", n=P), ACT.Copy).then_inc(kt_done, 1)
            norms = [0]
            for what, *n in CORE:
                if what == "r":
                    p, t = n
                    if t < 4:
                        act.wait_ge(r_tile_full, 4 * p + t + 1)
                    else:
                        act.wait_ge(w_used, U_R + 2 * p + 2)
                    if (p, t) == (0, 0):
                        for sem_ in states_out:
                            act.wait_ge(sem_, 16 * HEADS // 2)
                    act.activation(rg[:, t, p * 512:(p + 1) * 512], ps[:, 5 + (p * TT + t) % 2, :], ACT.Silu, scale=rpre[:, t:t + 1]).then_inc(r_done, 1)
                    if t == 4:
                        hi(U_R + 2 * p + 2)
                        hi(U_R + 2 * p + 3)
                    continue
                if what == "streams":
                    heads, t = n, 4
                    act.wait_ge(so_full, n[0] + 1)
                elif n[0] % 2:
                    heads, t = range(HEADS), n[0] // 2
                    act.wait_ge(o_full, n[0] + 1)
                else:
                    continue
                for h in heads:
                    src = ps[:, SO_BANK[h % 2], 0:DV] if what == "streams" else span(3, D)[:, h * DV:(h + 1) * DV]
                    if norms[0]:
                        act.wait_ge(o_squared, norms[0])
                    norms[0] += 1
                    act.activation(rs[:, 0:DV], src, ACT.Square, accum_out=ss[:, 4 * t + h:4 * t + h + 1]).then_inc(o_squared, 1)
            for k in range(KB):
                act.wait_ge(gated_full, k + 1)
                act.activation(xh[:, k, :], span(2 * (k % 2)), ACT.Copy, scale=gain(O_NORM + k)).then_inc(xh_done, 1)
            y_units(U_OUT1, BOUNDS[2])
            boundary(BOUNDS[2])
            last_ffn(U_FF1, G_FF1, sum(n for _, n in FF_PARTS))

        @block.gpsimd
        def _(pool):
            steps = [0]

            def step(ins):
                steps[0] += 1
                ins.then_inc(pool_step, 1)
                pool.wait_ge(pool_step, steps[0])

            def norm(name):
                n = NORM[name]
                pool.wait_ge(ms_done, n + 1)
                dst = rpre if name.startswith("pre") else rstd[:, 0:TT]
                pool.tensor_tensor(dst, ms[:, 0:TT], minus_half[:, 0:TT], ALU.pow).then_inc(rstd_done, 1)

            def boundary(B):
                norm(B["post"])
                for k in range(KB):
                    if k not in ADDED_BY_DVE:
                        pool.wait_ge(y_scaled, KB * B["n"] + k + 1)
                        pool.tensor_tensor(x[:, k, :], x[:, k, :], y[:, k, :], ALU.add).then_inc(x_added_pool, 1)
                norm(B["pre"])

            pool.memset(wsn[:, 1], 0.0).then_inc(zeroed, 1)
            pool.memset(winA[:, :, 0:16], 0.0).then_inc(zeroed, 1)
            pool.memset(winA[:, :, 16 + PROMPT:].rearrange("p g (b s) -> p g b s", s=32)[:, :, :, 0:1], 0.0).then_inc(zeroed, 1)
            pool.dma_start(cst[:, P:], a["consts"][:, P:]).then_inc(small_loads, 16)
            w_s = a["w_s"][0].rearrange("h t s -> t h s")
            pool.dma_start(wsn[:, 0], w_s).then_inc(small_loads, 16)
            pool.dma_start(hist[0:STREAMS * HIST, :], a["state_pool"][0].rearrange("b s d -> (b s) d")).then_inc(small_loads, 16)
            pool.wait_ge(zeroed, 1)
            for b in range(STREAMS):
                pool.dma_start(wsn[b * STEP:(b + 1) * STEP, 1, :, b * STEP:(b + 1) * STEP], w_s[0:STEP, :, 0:STEP]).then_inc(small_loads, 16)
            pool.dma_start(bs[:, 0, :], a["b_s"][0].rearrange("h t -> (h t)").partition_broadcast(P)).then_inc(small_loads, 16)
            pool.dma_start(wpool[:], a["w_pool"][0].rearrange("g c d -> c g d")).then_inc(small_loads, 16)
            pool.dma_start(lng[:], a["ln_v_g"][0].partition_broadcast(P)).then_inc(small_loads, 16)
            pool.dma_start(lnb[:], a["ln_v_b"][0].partition_broadcast(P)).then_inc(small_loads, 16)
            pool.wait_ge(consts_set, 2)
            norm("pre0")
            pool.wait_ge(acc_empty, 2)
            pool.wait_ge(hist_done, 1)
            for n, (src, dst) in enumerate(((winA, winB), (winB, winC), (winC, winB), (winB, winC))):
                w, s0 = 1 << n, (2 << n) - 1
                step(pool.tensor_tensor(dst[:, n:4, s0:], src[:, n:4, s0:], src[:, n:4, s0 - w:AW - w], ALU.add))
            for gr in range(4):
                s = (winB, winC)[gr % 2][:, gr, 16:32]
                last = pool.tensor_tensor(s, s, fix[:, gr, :], ALU.mult)
            last.then_inc(windows_done, 1)
            for t in range(TT):
                pool.wait_ge(vms_done, t + 1)
                pool.tensor_tensor(vrstd[:, t:t + 1], vms[:, t % 2:t % 2 + 1], minus_half[:, 0:1], ALU.pow).then_inc(vrstd_done, 1)
                if t:
                    pool.wait_ge(v_gained, t)
                    pool.tensor_tensor(v[:, t - 1, :], v[:, t - 1, :], lnb[:], ALU.add).then_inc(v_done, 1)
            pool.wait_ge(v_gained, TT)
            pool.tensor_tensor(v[:, TT - 1, :], v[:, TT - 1, :], lnb[:], ALU.add).then_inc(v_done, 1)
            pool.wait_ge(yb_full, TT)
            pool.wait_ge(v_done, TT)
            pool.memset(w2[:], 0.0).then_inc(w2_zeroed, 1)
            pool.wait_ge(w2_zeroed, 1)
            pool.dma_start(w2[P - 16:P, :], a["w_gate2"][0]).then_inc(gate_loads, 16)
            pool.dma_start(bg[:], a["b_gate"][0].partition_broadcast(P)).then_inc(gate_loads, 16)
            boundary(BOUNDS[0])
            boundary(BOUNDS[1])
            def states_load(h):
                pool.dma_start(Ss[:, h % 2], a["state_gla"][0, :, h].rearrange("b k v -> k b v")).then_inc(states_in[h % 2], 16)

            pool.wait_ge(cum_full, HEADS)
            states_load(0)
            states_load(1)
            pool.wait_ge(head_done, HEADS)
            pool.memset(att[:], 0.0).then_inc(cleared, 1)
            step(pool.memset(qm[:], 0.0))
            q4 = qk[:, 0:HEADS, tile(4)].rearrange("p h (q two s) -> p h q two s", two=2, s=STEP)
            m4 = qm[:].rearrange("p h o (q two s) -> p h o q two s", two=2, s=STEP)
            for n in range(2):
                for h in range(HEADS):
                    last = pool.tensor_copy(m4[:, h, n, :, n, :], q4[:, h, :, n, :])
            last.then_inc(cleared, 1)
            pool.wait_ge(kt_full, HEADS)
            pool.memset(S[:, 0], 0.0).then_inc(cleared, 1)
            pool.wait_ge(kt_done, HEADS)
            for n in range(2):
                pool.tensor_scalar(km[:, n, :], kend[:, 4, :], par[:, n:n + 1], None, ALU.mult).then_inc(km_done, 1)
            norms = 0
            for what, *n in CORE:
                if what == "r" or (what == "chunk" and n[0] % 2 == 0):
                    continue
                norms += 1
                c0, heads = (16 + n[0], 1) if what == "streams" else (4 * (n[0] // 2), HEADS)
                pool.wait_ge(o_ms, norms)
                pool.tensor_tensor(rstd[:, c0:c0 + heads], ms[:, c0:c0 + heads], minus_half[:, 0:heads], ALU.pow).then_inc(o_rstd, 1)
                if what == "streams":
                    h = n[0]
                    pool.wait_ge(ss_done, STREAMS * (h + 1))
                    pool.dma_start(a["gla_sample"][0, :, h].rearrange("b k v -> k b v"), Ss[:, h % 2]).then_inc(states_out[h % 2], 16)
                    if h == 1:
                        for g in range(2):
                            pool.wait_ge(states_out[g], 16)
                            states_load(2 + g)
            pool.wait_ge(s_done, 8)
            pool.dma_start(a["gla_prompt"][0, 0].rearrange("h k v -> k h v"), S[:, 0]).then_inc(prompt_out, 16)
            pool.dma_start(gF[:], a["post_ffn_g"][1].partition_broadcast(P)).then_inc(gain_load, 16)
            boundary(BOUNDS[2])
            pool.wait_ge(gain_load, 16)
            for m in range(3):
                for t in range(TT):
                    pool.wait_ge(y_tile_sq, 5 * m + t + 1)
                    cols = slice(m * UW, (m + 1) * UW)
                    pool.tensor_tensor(yF[:, t, cols], yF[:, t, cols], gF[:, cols], ALU.mult).then_inc(y_gained, 1)
            for t in range(TT):
                pool.wait_ge(tile_ms, t + 1)
                pool.tensor_tensor(rstd[:, t:t + 1], ms[:, t:t + 1], minus_half[:, 0:1], ALU.pow).then_inc(tile_rstd, 1)


def constants():
    s, t = np.indices((P, P))
    masks = [(s <= t) & (s // n == t // n) for n in (P, CHUNK, STEP)]
    frames = np.arange(16)
    fix = [w / np.minimum(w, frames + 1) for w in WINDOWS]
    odd = (np.arange(P) // STEP) % 2
    parts = [np.eye(P), *masks, np.broadcast_to(np.concatenate(fix), (P, 64)), np.stack([1 - odd, odd], 1)]
    return np.concatenate([np.asarray(x, np.float32) for x in parts], 1)


_OUTS = {
    "y_prompt": (1, PROMPT, D), "y_sample": (STREAMS, STEP, D),
    "pool_prompt": (1, 1, HIST, SG), "pool_sample": (1, STREAMS, HIST, SG),
    "sg_v_sample": (1, STREAMS, STEP, SG),
    "gla_prompt": (1, 1, HEADS, DK, DV), "gla_sample": (1, STREAMS, HEADS, DK, DV),
}


def kernel(**inputs):
    import concourse.bacc as bacc
    from concourse.bass_utils import run_bass_kernel_spmd

    nc = bacc.Bacc("TRN2", target_bir_lowering=False, num_devices=1)
    arrays = {name: np.ascontiguousarray(x) for name, x in inputs.items()}
    arrays["consts"] = constants()
    aps = {name: nc.dram_tensor(name, x.shape, mybir.dt.from_np(x.dtype), kind="ExternalInput").ap() for name, x in arrays.items()}
    for name, shape in _OUTS.items():
        aps[name] = nc.dram_tensor(name, shape, F32, kind="ExternalOutput").ap()
    encoder(nc, aps)
    r = run_bass_kernel_spmd(nc, [arrays], core_ids=[0])
    return tuple(r.results[0][name] for name in _OUTS)
```

```python
from contextlib import ExitStack

import concourse.bass as bass
import numpy as np
from concourse import mybir

F32 = mybir.dt.float32
F32R = mybir.dt.float32r
U32 = mybir.dt.uint32
ACT = mybir.ActivationFunctionType
ALU = mybir.AluOpType

P = 128
D = 1024
KB = D // P
PROMPT, STREAMS, STEP = 512, 8, 16
T = PROMPT + STREAMS * STEP
TT = T // P
HALF = T // 2
EPS = 1e-6
WINDOWS = (2, 4, 8, 16)
HIST = 15
SG = 512
HEADS, DK, DV = 4, 128, 256
TAU = 16.0
CHUNK = 64
D_FF = 2816
FF_PARTS = ((0, 4), (8, 4), (16, 3))
UW = 2 * P
CONSTS = 4 * P + 66

PRE_MIX, POST_MIX, PRE_FFN, POST_FFN, POOL_SCALE, O_NORM, ROWS = 0, 16, 32, 48, 64, 68, 76

U_AU, U_V, U_OUT0, U_FF0 = 0, 4, 6, 10
FF_UNITS = sum(2 * n + 4 for _, n in FF_PARTS)
U_QK = U_FF0 + FF_UNITS
U_G = U_QK + 1
U_VV = U_QK + 5
U_R = U_VV + 4
U_OUT1 = U_R + 4
U_FF1 = U_OUT1 + 4
UNITS = U_FF1 + FF_UNITS

G_AU, G_OUT0, G_FF0 = 0, 4, 8
G_QK = G_FF0 + FF_UNITS
G_G = G_QK + 1
G_OUT1 = G_QK + 5
G_FF1 = G_OUT1 + 4

CORE = (("streams", 0), ("streams", 1), ("chunk", 0), ("chunk", 1), ("streams", 2), ("streams", 3),
        ("r", 0, 0), ("chunk", 2), ("r", 0, 1), ("chunk", 3), ("r", 0, 2), ("r", 0, 3), ("chunk", 4),
        ("r", 0, 4), ("chunk", 5), ("r", 1, 0), ("chunk", 6), ("r", 1, 1), ("chunk", 7),
        ("r", 1, 2), ("r", 1, 3), ("r", 1, 4))


_NORMS = [(what, n[0]) for what, *n in CORE if what == "streams" or (what == "chunk" and n[0] % 2)]
SO_NORMED = [_NORMS.index(("streams", h)) + 1 for h in range(HEADS)]
O_NORMED = [_NORMS.index(("chunk", 2 * t + 1)) + 1 for t in range(PROMPT // P)]


def encoder(nc, a):
    with ExitStack() as ctx:
        base, end = nc.sbuf_base, nc.sbuf_usable_end
        base = (base + 63) // 64 * 64

        def at(name, offset, shape, dt=F32, parts=P):
            size = 4 * int(np.prod(shape))
            assert base + offset + size <= end, (name, base + offset + size, end)
            return nc.alloc_sbuf_tensor_at(name, [parts, *shape], dt, offset=base + offset)

        K20, K10, K5 = 20480, 10240, 5120
        o_x, o_xh, o_xl, o_y, o_hh, o_hl = (i * K20 for i in range(6))
        o_stage = 6 * K20
        o_wh, o_wl = o_stage + 16384, o_stage + 2 * 16384
        o_rs = o_wl + 16384
        o_sq = o_rs + 2560
        o_acc = o_sq + K5
        o_gate = o_acc + K5
        o_up = o_gate + K5
        o_diag = o_up + K5
        o_late = o_diag + 2560
        o_const = o_late + K10

        x = at("x", o_x, [KB, T])
        xh = at("xh", o_xh, [KB, T], F32R)
        xl = at("xl", o_xl, [KB, T], F32R)
        y = at("y", o_y, [KB, T])
        hh = at("hh", o_hh, [KB, T], F32R)
        hl = at("hl", o_hl, [KB, T], F32R)
        stage = at("stage", o_stage, [2, KB * UW])
        wh = at("wh", o_wh, [2, KB, UW], F32R)
        wl = at("wl", o_wl, [2, KB, UW], F32R)
        rs = at("rs", o_rs, [T])
        sq = at("sq", o_sq, [2, T])
        acc = at("acc", o_acc, [2, T])
        gate = at("gate", o_gate, [2, T])
        up = at("up", o_up, [2, T])
        diag = at("diag", o_diag, [TT, P])
        HG = 64
        GROUPS = HALF // HG
        diag64 = diag[:].rearrange("p t n -> p (t n)")[0:HG, 0:HALF].rearrange("p (t n) -> p t n", n=HG)
        cst = at("cst", o_const, [CONSTS])
        ident = cst[:, 0:P]
        tri = cst[:, P:4 * P].rearrange("p (m t) -> p m t", m=3)
        fix = cst[:, 4 * P:4 * P + 64].rearrange("p (g t) -> p g t", g=4)
        par = cst[:, 4 * P + 64:4 * P + 66]
        ones = at("ones", o_const + 2368, [P])
        gains = at("gains", o_const + 2880, [ROWS])
        small = at("small", o_const + 3200, [130])
        elast = at("elast", o_const + 3744, [HEADS, 2 * STREAMS])
        ss, ms, rstd = small[:, 0:20], small[:, 20:40], small[:, 40:60]
        minus_half = small[:, 60:80]
        rpre = small[:, 80:85]
        bn6, vms, vrstd, mv = small[:, 90:96], small[:, 96:98], small[:, 100:105], small[:, 105:109]
        bend = small[:, 110:126]

        uT = at("uT", o_y, [4, T])
        v = at("v", o_y + K10, [TT, SG])
        xin = at("xin", o_y, [TT, D])
        junk = at("junk", o_hl + 6016, [D])
        xg = at("xg", o_hl + 6016 + 4 * D, [2, KB, P])
        AW = 16 + PROMPT + STREAMS * 32
        winA = at("winA", o_hh, [4, AW])
        winB = at("winB", o_hh + 4 * 4 * AW, [4, AW])
        winC = at("winC", o_hh + 8 * 4 * AW, [4, AW])
        wsT = at("wsT", o_late, [2, 4, P])
        wpool = at("wpool", o_late + 4096, [4, P])
        lng = at("lng", o_late + 6144, [SG])
        lnb = at("lnb", o_late + 8192, [SG])
        gv = at("gv", o_gate, [2, SG])
        bs = at("bs", o_gate + 4096, [2, 4 * P])
        hist = at("hist", o_sq, [SG])
        a_last = at("a_last", o_sq + 2048, [4, P])
        wsn = at("wsn", o_acc, [2, 4, P])
        a_out = at("a_out", o_acc, [2, SG])
        rows = at("rows", o_diag, [P])

        qk = at("qk", o_hh, [8, T])
        vv = at("vv", o_hl, [TT, D])
        la = at("la", o_y, [TT, SG])
        Ss = at("Ss", o_y, [2, STREAMS, DV])
        rg = at("rg", o_y, [TT, D])
        lmin = at("lmin", o_gate, [TT, SG])
        cum = at("cum", o_gate, [HEADS, T])
        zf = at("zf", o_diag, [T])
        w2 = at("w2", o_late, [SG])
        bg = at("bg", o_late + 2048, [SG])
        kend = at("kend", o_late, [TT, SG])
        eq = at("eq", o_sq, [T])
        ek = at("ek", o_sq + 2560, [T])
        att = at("att", o_sq, [3, 4 * P])
        qm = at("qm", o_sq + 6144, [HEADS, 2, P])
        S = at("S", o_gate, [2, HEADS, DV])
        km = (kend[:, 4], at("km_odd", o_diag, [SG])[:])

        yF = at("yF", o_y, [TT, D])
        xF = at("xF", o_xh, [TT, D])
        gF = at("gF", o_late, [D])
        yg = at("yg", o_late + 4 * D, [TT, UW])

        ps = ctx.enter_context(nc.psum_tensor("ps", [P, 8, 512], F32))
        flat = ps[:].rearrange("p b n -> p (b n)")

        def sem(name):
            return ctx.enter_context(nc.semaphore(name))

        w_loaded = [sem("w_loaded0"), sem("w_loaded1")]
        w_hi, w_lo, w_used = sem("w_hi"), sem("w_lo"), sem("w_used")
        acc_empty = sem("acc_empty")
        ident_load, rows_loads, small_loads = sem("ident_load"), sem("rows_loads"), sem("small_loads")
        x_load = [sem(f"x_load{t}") for t in range(TT)]
        consts_set, zeroed = sem("consts_set"), sem("zeroed")
        dve_step, act_step, pool_step = sem("dve_step"), sem("act_step"), sem("pool_step")
        xh_done, xl_done = sem("xh_done"), sem("xl_done")
        squares, squares_added = sem("squares"), sem("squares_added")
        sums_full, ms_done, rstd_done = sem("sums_full"), sem("ms_done"), sem("rstd_done")
        diag_done, r_full, rs_done = sem("diag_done"), sem("r_full"), sem("rs_done")
        y_blocks_full, y_stands, y_scaled = sem("y_blocks_full"), sem("y_stands"), sem("y_scaled")
        x_added_dve, x_added_pool = sem("x_added_dve"), sem("x_added_pool")
        x_squares, x_squares_first, x_squares_added = sem("x_squares"), sem("x_squares_first"), sem("x_squares_added")
        rows_full, rows_done, x0_full, x0_done = sem("rows_full"), sem("rows_done"), sem("x0_full"), sem("x0_done")
        xg_done, x0_hi, x0_lo = sem("xg_done"), sem("x0_hi"), sem("x0_lo")
        ws_full, ws_done, hist_full, hist_done = sem("ws_full"), sem("ws_done"), sem("hist_full"), sem("hist_done")
        x0_sums = sem("x0_sums")
        a_last_done, windows_done, pooled_done, ya_full = sem("a_last_done"), sem("windows_done"), sem("pooled_done"), sem("ya_full")
        u_done, v_full, v_gelu, vms_done = sem("u_done"), sem("v_full"), sem("v_gelu"), sem("vms_done")
        vrstd_done, v_normed, v_gained, v_done = sem("vrstd_done"), sem("v_normed"), sem("v_gained"), sem("v_done")
        yb_full, yb_done, yb_hi, yb_lo = sem("yb_full"), sem("yb_done"), sem("yb_hi"), sem("yb_lo")
        last_a_full, last_a_done, mixer_stores = sem("last_a_full"), sem("last_a_done"), sem("mixer_stores")
        silu_done, hid_done, hid_hi, hid_lo = sem("silu_done"), sem("hid_done"), sem("hid_hi"), sem("hid_lo")
        w2_zeroed, gate_loads = sem("w2_zeroed"), sem("gate_loads")
        vv_full, vv_done = sem("vv_full"), sem("vv_done")
        gate_full, gx_done, gabs_done, gln_done, la_done = (sem(n) for n in ("gate_full", "gx_done", "gabs_done", "gln_done", "la_done"))
        states_in = [sem("states_in0"), sem("states_in1")]
        states_out = [sem("states_out0"), sem("states_out1")]
        cum_full, cum_done, bend_done, exps_done = sem("cum_full"), sem("cum_done"), sem("bend_done"), sem("exps_done")
        dist_done, dist_exp, head_done = sem("dist_done"), sem("dist_exp"), sem("head_done")
        kt_full, kt_done, km_done, cleared = (sem(n) for n in ("kt_full", "kt_done", "km_done", "cleared"))
        att_full, att_done, kv_full, s_done = sem("att_full"), sem("att_done"), sem("kv_full"), sem("s_done")
        o_full, skv_full, ss_done = sem("o_full"), sem("skv_full"), sem("ss_done")
        so_full, o_squared, o_ms, o_rstd, o_normed = (sem(n) for n in ("so_full", "o_squared", "o_ms", "o_rstd", "o_normed"))
        r_tile_full, r_done, gated, gated_full = (sem(n) for n in ("r_tile_full", "r_done", "gated", "gated_full"))
        prompt_out = sem("prompt_out")
        gain_load, xF_full, xF_done = sem("gain_load"), sem("xF_full"), sem("xF_done")
        y_tile_full, y_tile_out, y_tile_sq = sem("y_tile_full"), sem("y_tile_out"), sem("y_tile_sq")
        y_gained, tile_ms, tile_rstd = sem("y_gained"), sem("tile_ms"), sem("tile_rstd")
        first_scaled, first_ready = sem("first_scaled"), sem("first_ready")
        out_ready, stores = sem("out_ready"), sem("stores")

        SMALL_LOADS = 1 + 2 + STREAMS + 4
        MIXER_STORES = 1 + STREAMS + 1
        U_QKS = (U_QK, U_QK + 2, U_QK + 3, U_QK + 4)
        G_QKS = (G_QK, G_QK + 2, G_QK + 3, G_QK + 4)
        GATED_BANK = (0, 2, 4, 6, 0, 2, 0, 2)
        KT_BANK = (4, 6, 2, 0)
        SO_BANK = (7, 3)
        KV_RING = (1, 2, 5, 6)

        PRE0 = 0

        def post_norm(n, h):
            return 3 * n + 1 + h

        def pre_norm(n):
            return 3 * n + 3

        X_OUT0, X_FF0, X_IN1, X_OUT1, X_FF1 = 0, 4, 20, 36, 44
        BOUNDS = (
            dict(n=0, gp=POST_MIX, gq=PRE_FFN, g=G_FF0, x=X_FF0),
            dict(n=1, gp=POST_FFN, gq=PRE_MIX + 8, g=G_QK, x=X_IN1),
            dict(n=2, gp=POST_MIX + 8, gq=PRE_FFN + 8, g=G_FF1, x=X_FF1),
        )

        def f32(t):
            return t.bitcast(F32)

        def banks4(g):
            b = 4 * (g % 2)
            return ps[:, b:b + 4, 0:HALF].rearrange("p (m h) n -> p m h n", m=2)

        def span(b, n=T):
            return flat[:, 512 * b:512 * b + n]

        def halved(t):
            return t.rearrange("p (h n) -> p h n", h=2)

        def two(t, k):
            return t[:, bass.ds(k, 2), :].rearrange("p m (h n) -> p m h n", h=2)

        def rs_twice():
            return halved(rs[:]).unsqueeze(1).broadcast_to([P, 2, 2, HALF])

        def tile(t):
            return slice(t * P, (t + 1) * P)

        def norm_banks(g):
            own, other = 4 * (g % 2), 4 * ((g + 1) % 2)
            return (own + 1, other + 2), (own + 3, other + 3), other + 2, other + 3

        def tile_bank(odd, t):
            return (4 * (G_FF1 % 2) + (5 + t % 3 if odd else t)) % 8

        def gain(row):
            return gains[:, row:row + 1]

        def half(t, i):
            h, k = divmod(i, KB)
            return t[:, k, h * HALF:(h + 1) * HALF]

        PIECES = 2 * KB
        LAG = 2
        ADDED_BY_DVE = (0, 6)

        def wait_x_added(engine, n, i):
            if i in ADDED_BY_DVE:
                engine.wait_ge(x_added_dve, len(ADDED_BY_DVE) * n + ADDED_BY_DVE.index(i) + 1)
            else:
                done = sum(j not in ADDED_BY_DVE for j in range(i + 1))
                engine.wait_ge(x_added_pool, (PIECES - len(ADDED_BY_DVE)) * n + done)

        block = ctx.enter_context(nc.Block())

        @block.sync
        def _(sp):
            def load(u, src, wait=True):
                if wait:
                    sp.wait_ge(w_lo, u - 1)
                src = src.rearrange("(k p) c -> p k c", p=P)
                nk, width = src.shape[1:]
                dst = stage[:, u % 2, 0:nk * width].rearrange("p (k c) -> p k c", c=width)
                sp.dma_start(dst, src).then_inc(w_loaded[u % 2], 16)

            def load_loop(u0, pairs, src):
                with sp.Fori(0, pairs) as i:
                    for j in range(2):
                        u = u0 + j
                        sp.wait_ge(w_lo, i * 2 + (u - 1))
                        dst = stage[:, u % 2, :].rearrange("p (k c) -> p k c", c=UW)
                        s = src(i, j).rearrange("(k p) c -> p k c", p=P)
                        sp.dma_start(dst[:, 0:s.shape[1], :], s).then_inc(w_loaded[u % 2], 16)

            def load_ffn(layer, u):
                for f, pairs in FF_PARTS:
                    load_loop(u, pairs, lambda i, j: (a["w_ffn_gate"], a["w_ffn_up"])[j][layer, :, bass.ds(i * UW + f * P, UW)])
                    u += 2 * pairs
                    load_loop(u, 2, lambda i, j: a["w_ffn_down"][layer, f * P:(f + 2 * pairs) * P, bass.ds(i * (2 * UW) + j * UW, UW)])
                    u += 4

            sp.dma_start(ident, a["consts"][:, 0:P]).then_inc(ident_load, 16)
            r0 = 0
            for name in ("pre_mix_g", "post_mix_g", "pre_ffn_g", "post_ffn_g", "pool_scale", "g_onorm"):
                src = a[name].rearrange("l (k p) -> (l k) p", p=P)
                sp.dma_start(rows[r0:r0 + src.shape[0], :], src).then_inc(rows_loads, 16)
                r0 += src.shape[0]
            assert r0 == ROWS
            for t in range(TT):
                src = a["x_prompt"][0, tile(t), :] if t < 4 else a["x_sample"].rearrange("b s d -> (b s) d")
                sp.dma_start(xin[:, t, :], src).then_inc(x_load[t], 16)
                if t == 0:
                    load(0, a["w_in_even"][0, :, 0:UW], wait=False)
            for u in range(1, U_OUT0):
                load(u, a["w_in_even"][0, :, u * UW:(u + 1) * UW], wait=u >= 2)
            for m in range(4):
                load(U_OUT0 + m, a["w_out_even"][0, :, m * UW:(m + 1) * UW])
            load_ffn(0, U_FF0)
            w_in = a["w_in_odd"][0]
            for j, u in enumerate(U_QKS):
                load(u, w_in[:, j * UW:(j + 1) * UW])
                if j == 0:
                    load(U_G, w_in[:, w_in.shape[1] - P:])
            for j in range(8):
                load(U_VV + j, w_in[:, D + j * UW:D + (j + 1) * UW])
            for m in range(4):
                load(U_OUT1 + m, a["w_out_odd"][0, :, m * UW:(m + 1) * UW])
            load_ffn(1, U_FF1)

            for t in range(TT):
                dst = a["y_prompt"][0, tile(t), :] if t < 4 else a["y_sample"].rearrange("b s d -> (b s) d")
                for ready, cols in ((first_ready, slice(0, UW)), (out_ready, slice(UW, D))):
                    sp.wait_ge(ready, t + 1)
                    sp.dma_start(dst[:, cols], yF[:, t, cols]).then_inc(stores, 16)
            sp.wait_ge(stores, 16 * 2 * TT)
            sp.wait_ge(mixer_stores, 16 * MIXER_STORES)
            for sem_ in states_out:
                sp.wait_ge(sem_, 16 * HEADS // 2)
            sp.wait_ge(prompt_out, 16)

        @block.tensor
        def _(pe):
            def unit(u, g, mh, ml, nk=KB, ready=None, di=0):
                pe.wait_ge(w_lo, di + (u + 1))
                if g >= 2:
                    pe.wait_ge(acc_empty, di + (g - 1))
                out = banks4(g)
                for k in range(nk):
                    if ready is not None:
                        ready(k)
                    for m in range(2):
                        for n, (w, mv_) in enumerate(((wh, mh), (wh, ml), (wl, mh))):
                            wt = w[:, u % 2, k, m * P:(m + 1) * P]
                            for h in range(2):
                                last = pe.matmul(out[:, m, h, :], wt, mv_[:, k, h * HALF:(h + 1) * HALF],
                                                 start=(k == 0 and n == 0), stop=(k == nk - 1 and n == 2))
                last.then_inc(w_used, 1)

            def frames_unit(u, bank, half, wait=None, event=None):
                pe.wait_ge(w_lo, u + 1)
                for t in range(TT):
                    if wait is not None:
                        wait(t)
                    for k in range(KB):
                        for n, (w, mv_) in enumerate(((wh, xh), (wl, xh), (wh, xl))):
                            last = pe.matmul(ps[:, bank[t], half * UW:(half + 1) * UW], mv_[:, k, tile(t)], w[:, u % 2, k, :],
                                             start=(k == 0 and n == 0), stop=(k == KB - 1 and n == 2))
                    if t == TT - 1:
                        last.then_inc(w_used, 1)
                    elif event is not None:
                        last.then_inc(event, 1)

            def sum_tiles(bank, src, tiles, first=False):
                for t in tiles:
                    last = pe.matmul(ps[:, bank, t:t + 1], src[:, tile(t)], ones[:, 0:1], start=(first and t == 0), stop=True,
                                     skip_group_check=True)
                return last

            def spread(n, b):
                pe.wait_ge(diag_done, n + 1)
                for h in range(2):
                    last = pe.matmul(ps[:, b + h, 0:HALF], ones[:], diag[:].rearrange("p t n -> p (t n)")[:, h * HALF:(h + 1) * HALF],
                                     start=True, stop=True)
                last.then_inc(r_full, 1)

            def sum_half(B, h):
                bank = norm_banks(B["g"])[1][h]
                pe.wait_ge(squares_added, 5 * B["n"] + 4 + h)
                pe.wait_ge(squares, 7 * B["n"] + 5 + 2 * h)
                for n, src in enumerate((acc[:, 0], sq[:, 1])):
                    for t in range(GROUPS):
                        c = h * HALF + t * HG
                        last = pe.matmul(ps[0:HG, bank, t:t + 1], src[:, c:c + HG], ones[:, 0:1], start=(n == 0 and t == 0), stop=True,
                                         skip_group_check=True)
                last.then_inc(sums_full, 1)

            def spread_half(B, h):
                pe.wait_ge(diag_done, post_norm(B["n"], h) + 1)
                pe.matmul(ps[:, norm_banks(B["g"])[0][h], 0:HALF], ones[0:HG, :], diag64.rearrange("p t n -> p (t n)"),
                          start=True, stop=True).then_inc(r_full, 1)

            def part(u, out, mh, ml, m, h, ks, nk):
                for k in ks:
                    for n, (w, mv_) in enumerate(((wh, mh), (wh, ml), (wl, mh))):
                        last = pe.matmul(out[:, m, h, :], w[:, u % 2, k, m * P:(m + 1) * P], mv_[:, k, h * HALF:(h + 1) * HALF],
                                         start=(k == 0 and n == 0), stop=(k == nk - 1 and n == 2))
                return last

            def last_y_unit(u, B, mh, ml, nk):
                g, out = B["g"] - 1, banks4(B["g"] - 1)
                pe.wait_ge(w_lo, u + 1)
                pe.wait_ge(acc_empty, g - 1)
                for m, h in ((0, 0), (1, 0), (0, 1)):
                    part(u, out, mh, ml, m, h, range(nk), nk).then_inc(y_blocks_full, 1)
                pe.wait_ge(acc_empty, g)
                sum_half(B, 0)
                now = min(nk, 6)
                last = part(u, out, mh, ml, 1, 1, range(now), nk)
                if now == nk:
                    last.then_inc(w_used, 1)
                spread_half(B, 0)
                if now < nk:
                    part(u, out, mh, ml, 1, 1, range(now, nk), nk).then_inc(w_used, 1)

            def boundary(B, u, blocks=2):
                _, _, ahead, bank = norm_banks(B["g"])
                g = B["g"]
                out = banks4(g)
                pe.wait_ge(w_lo, u + 1)
                for i in range(PIECES):
                    h, k = divmod(i, KB)
                    for n, (w, mv_, ready) in enumerate(((wh, xh, xh_done), (wl, xh, None), (wh, xl, xl_done))):
                        if ready is not None:
                            pe.wait_ge(ready, B["x"] + i + 1)
                        for m in range(2):
                            last = pe.matmul(out[:, m, h, :], w[:, u % 2, k, m * P:(m + 1) * P], half(mv_, i),
                                             start=(k == 0 and n == 0), stop=(k == KB - 1 and n == 2))
                    if i == 1:
                        pe.wait_ge(acc_empty, g)
                        sum_half(B, 1)
                    elif i == 4:
                        spread_half(B, 1)
                last.then_inc(w_used, 1)
                out, v = banks4(g + 1), u + 1
                pe.wait_ge(w_hi, u + 2)

                def first(passes):
                    for n, (w, mv_) in passes:
                        for k in range(KB):
                            wt = w[:, v % 2, k, 0:P] if blocks == 2 else w[:, v % 2, k // 2, (k % 2) * P:(k % 2 + 1) * P]
                            for h in range(2):
                                last = pe.matmul(out[:, 0, h, :], wt, mv_[:, k, h * HALF:(h + 1) * HALF],
                                                 start=(k == 0 and n == 0), stop=(k == KB - 1 and n == 2))
                    return last
                first(((0, (wh, xh)), (1, (wh, xl))))
                pe.wait_ge(x_squares_added, 3 * (B["n"] + 1))
                sum_tiles(bank, acc[:, 0], range(TT), first=True).then_inc(sums_full, 1)
                pe.wait_ge(w_lo, u + 2)
                last = first(((2, (wl, xh)),))
                if blocks == 1:
                    last.then_inc(w_used, 1)
                spread(pre_norm(B["n"]), ahead)
                pe.wait_ge(rs_done, 2 + B["n"])
                if blocks == 2:
                    part(v, out, xh, xl, 1, 0, range(KB), KB)
                    part(v, out, xh, xl, 1, 1, range(KB), KB).then_inc(w_used, 1)

            def gate_up(u, g, pairs, first):
                with pe.Fori(first, pairs) as i:
                    for j in range(2):
                        unit(u + j, g + j, xh, xl, di=i * 2)

            def hid_ready(pair, k):
                if k % 2 == 0:
                    pe.wait_ge(hid_lo, pair + k // 2 + 1)

            def ffn(u, g, pair, B):
                for n, (f, pairs) in enumerate(FF_PARTS):
                    gate_up(u, g, pairs, int(n == 0))
                    u, g = u + 2 * pairs, g + 2 * pairs
                    ready = lambda k: hid_ready(pair, k)
                    if n < len(FF_PARTS) - 1:
                        with pe.Fori(0, 2) as i:
                            for j in range(2):
                                unit(u + j, g + j, hh, hl, nk=2 * pairs, ready=ready, di=i * 2)
                    else:
                        for m in range(3):
                            unit(u + m, g + m, hh, hl, nk=2 * pairs, ready=ready)
                        last_y_unit(u + 3, B, hh, hl, 2 * pairs)
                    u, g, pair = u + 4, g + 4, pair + pairs

            def last_ffn(u, g, pair):
                for n, (f, pairs) in enumerate(FF_PARTS):
                    gate_up(u, g, pairs, int(n == 0))
                    u, g = u + 2 * pairs, g + 2 * pairs
                    nk = 2 * pairs

                    def even(di, turning=False):
                        pe.wait_ge(w_lo, di + (u + 1))
                        for k in range(nk):
                            hid_ready(pair, k)
                            for t in range(TT):
                                if k == 0 and t == 4:
                                    pe.wait_ge(acc_empty, g)
                                for j, (w, mv_) in enumerate(((wh, hh), (wl, hh), (wh, hl))):
                                    last = pe.matmul(ps[:, tile_bank(0, t), 0:UW], mv_[:, k, tile(t)], w[:, u % 2, k, :],
                                                     start=(k == 0 and j == 0), stop=(k == nk - 1 and j == 2))
                            if turning and k < TT:
                                if k:
                                    pe.wait_ge(xF_done, k)
                                for j in range(KB):
                                    turned = pe.transpose(span(tile_bank(1, 0), D)[:, tile(j)], x[:, j, tile(k)], ident)
                                turned.then_inc(xF_full, 1)
                        last.then_inc(w_used, 1)

                    def odd(di):
                        pe.wait_ge(w_lo, di + (u + 2))
                        for t in range(TT):
                            if t >= 3:
                                pe.wait_ge(y_tile_out, di * 5 + (20 * n + 5 + t - 2))
                            for k in range(nk):
                                for j, (w, mv_) in enumerate(((wh, hh), (wl, hh), (wh, hl))):
                                    last = pe.matmul(ps[:, tile_bank(1, t), 0:UW], mv_[:, k, tile(t)], w[:, (u + 1) % 2, k, :],
                                                     start=(k == 0 and j == 0), stop=(k == nk - 1 and j == 2))
                            last.then_inc(w_used if t == TT - 1 else y_tile_full, 1)
                    if n < len(FF_PARTS) - 1:
                        with pe.Fori(0, 2) as i:
                            even(i * 2)
                            odd(i * 2)
                    else:
                        assert nk > TT
                        even(0, turning=True)
                        pe.wait_ge(xF_done, TT)
                        odd(0)
                        even(2)
                        odd(2)
                    u, pair = u + 4, pair + pairs

            pe.wait_ge(ident_load, 16)
            pe.wait_ge(rows_loads, 16 * 6)
            pe.transpose(ps[:, 0, 0:ROWS], rows[0:ROWS, :], ident[0:ROWS, 0:ROWS]).then_inc(rows_full, 1)

            def turn(t):
                pe.wait_ge(x_load[t], 16)
                if t >= 2:
                    pe.wait_ge(x0_done, t - 1)
                    pe.wait_ge(xg_done, t - 1)
                for k in range(KB):
                    last = pe.transpose(span(4 + 2 * (t % 2), D)[:, tile(k)], xin[:, t, tile(k)], ident)
                last.then_inc(x0_full, 1)

            def first_unit(h):
                for n, (w, mv_) in enumerate(((wh, xh), (wh, xl), (wl, xh))):
                    if n == 2 and h == 0:
                        pe.wait_ge(w_lo, 1)
                    for k in range(KB):
                        for m in range(2):
                            last = pe.matmul(banks4(0)[:, m, h, :], w[:, 0, k, m * P:(m + 1) * P], mv_[:, k, h * HALF:(h + 1) * HALF],
                                             start=(k == 0 and n == 0), stop=(k == KB - 1 and n == 2))
                return last
            for t in range(TT):
                turn(t)
            pe.wait_ge(rows_done, 1)
            pe.wait_ge(w_hi, 1)
            pe.wait_ge(x0_lo, 3)
            first_unit(0)
            pe.wait_ge(x0_lo, TT)
            first_unit(1).then_inc(w_used, 1)

            pe.wait_ge(x0_done, TT)
            pe.wait_ge(consts_set, 2)
            spread(PRE0, 6)
            for u in range(1, 4):
                if u == 2:
                    unit(u, u, xh, xl)
                    continue
                pe.wait_ge(w_lo, u + 1)
                if u == 3:
                    pe.wait_ge(acc_empty, u - 1)
                    pe.wait_ge(small_loads, 16 * SMALL_LOADS)
                    for h in range(4):
                        last = pe.transpose(ps[:, 7, h * P:h * P + STREAMS * HIST], hist[0:STREAMS * HIST, tile(h)], ident[0:STREAMS * HIST, 0:STREAMS * HIST])
                    last.then_inc(hist_full, 1)
                for h in range(2):
                    part(u, banks4(u), xh, xl, 0, h, range(KB), KB)
                if u == 1:
                    pe.wait_ge(rs_done, 1)
                else:
                    pe.wait_ge(hist_done, 1)
                for h in range(2):
                    last = part(u, banks4(u), xh, xl, 1, h, range(KB), KB)
                last.then_inc(w_used, 1)
            pe.wait_ge(acc_empty, 3)

            def v_wait(t):
                if t == 4:
                    pe.wait_ge(acc_empty, 4)
            frames_unit(U_V, range(5), 0, wait=v_wait)
            pe.wait_ge(zeroed, 1)
            for n in range(2):
                for h in range(4):
                    last = pe.transpose(ps[:, 5 + n, tile(h)], wsn[:, n, h, :], ident)
                last.then_inc(ws_full, 1)
            pe.wait_ge(a_last_done, 1)
            pe.wait_ge(ws_done, 1)
            for gr in range(4):
                pe.transpose(ps[0:HIST, 7, tile(gr)], winA[:, gr, 1 + PROMPT:16 + PROMPT], ident)
                last = pe.transpose(ps[:, 5, tile(gr)], a_last[:, gr, :], ident)
            last.then_inc(last_a_full, 1)
            frames_unit(U_V + 1, range(5), 1, event=v_full)
            pe.wait_ge(last_a_done, 2)
            pe.wait_ge(ws_done, 2)
            for gr, b in enumerate((6, 4, 0, 2)):
                pe.wait_ge(pooled_done, 2 * gr + 2)
                pe.wait_ge(v_gelu, (1, 5, 5, 5)[gr])
                res = (winB, winC)[gr % 2]
                pe.matmul(span(b)[:, 0:PROMPT], wpool[:, gr, :], res[:, gr, 16:16 + PROMPT], start=True, stop=True)
                pe.matmul(span(b)[:, PROMPT:T], wpool[:, gr, :],
                          res[:, gr, 16 + PROMPT:].rearrange("p (b s) -> p b s", s=32)[:, :, 16:], start=True, stop=True).then_inc(ya_full, 1)
            for t, b in enumerate((6, 7, 4, 5, 6)):
                pe.wait_ge(v_done, t + 1)
                if t < 4:
                    pe.wait_ge(xl_done, X_OUT0 + (1, 1, 2, 2)[t])
                else:
                    pe.wait_ge(yb_done, 1)
                n = int(t == 4)
                for h in range(4):
                    last = pe.matmul(ps[:, b, tile(h)], v[:, t, tile(h)], wsT[:, n, h, :], start=True, stop=True)
                last.then_inc(yb_full, 1)
            def mixed(k):
                if k == 0:
                    pe.wait_ge(xl_done, X_OUT0 + 4)
                elif k == 4:
                    pe.wait_ge(yb_lo, TT)
            for m in range(3):
                if m == 1:
                    pe.wait_ge(yb_done, TT)
                unit(U_OUT0 + m, G_OUT0 + m, xh, xl, ready=mixed if m == 0 else None)
            last_y_unit(U_OUT0 + 3, BOUNDS[0], xh, xl, KB)
            boundary(BOUNDS[0], U_FF0)
            ffn(U_FF0, G_FF0, 0, BOUNDS[1])

            boundary(BOUNDS[1], U_QK, blocks=1)
            unit(U_QKS[1], G_QKS[1], xh, xl)
            pe.wait_ge(acc_empty, G_G + 1)
            pe.wait_ge(gate_loads, 32)
            for t, b in enumerate((6, 7, 4, 5, 6)):
                if t == 4:
                    pe.wait_ge(gx_done, 1)
                pe.matmul(ps[:, b, :], zf[:, tile(t)], w2[:], start=True, stop=True).then_inc(gate_full, 1)
            pe.wait_ge(gx_done, TT)
            unit(U_QKS[2], G_QKS[2], xh, xl)
            unit(U_QKS[3], G_QKS[3], xh, xl)
            pe.wait_ge(la_done, 1)
            for h, b in enumerate((4, 6, 0, 2)):
                pe.wait_ge(acc_empty, G_QKS[2 if h < 2 else 3] + 1)
                for t in range(TT):
                    last = pe.matmul(span(b)[:, tile(t)], la[:, t, tile(h)], tri[:, 1 if t < 4 else 2, :], start=True, stop=True)
                last.then_inc(cum_full, 1)
            for p, (banks, waits) in enumerate((((4, 5, 6, 7, 2), [(cum_done, 1), (cum_done, 1), (cum_done, 2), (cum_done, 2), (cum_done, 4)]),
                                                ((6, 7, 2, 0, 1), [(vv_done, 3), (vv_done, 4), (vv_done, 5), (cum_done, 4), (cum_done, 4)]))):
                frames_unit(U_VV + 2 * p, banks, 0, wait=lambda t: pe.wait_ge(*waits[t]))
                frames_unit(U_VV + 2 * p + 1, banks, 1, event=vv_full)
            for h, (b, n) in enumerate(zip(KT_BANK, (5, 7, 8, 10))):
                pe.wait_ge(vv_done, n)
                pe.wait_ge(head_done, h + 1)
                for t in range(TT):
                    last = pe.transpose(span(b)[:, tile(t)], cum[:, h, tile(t)], ident)
                last.then_inc(kt_full, 1)
            pe.wait_ge(kt_done, HEADS)
            pe.wait_ge(km_done, HEADS)

            def scores(t):
                for h in range(HEADS):
                    last = pe.matmul(ps[:, 0, tile(h)], qk[:, 4 + h, tile(t)], qk[:, h, tile(t)], start=True, stop=True)
                last.then_inc(att_full, 1)

            def streams(h):
                if h == 0:
                    scores(4)
                    pe.wait_ge(att_done, 1)
                    pe.wait_ge(cleared, 3)
                if h >= 2:
                    pe.wait_ge(o_normed, SO_NORMED[0] if h == 2 else O_NORMED[0])
                pe.wait_ge(states_in[h % 2], 16 * (h // 2 + 1))
                out = ps[:, SO_BANK[h % 2], 0:DV]
                pe.matmul(out, att[:, 2, tile(h)], vv[:, 4, h * DV:(h + 1) * DV], start=True, stop=False, skip_group_check=True)
                for b in range(STREAMS):
                    q = slice(32 * (b // 2), 32 * (b // 2) + 32)
                    last = pe.matmul(out[q, :], qm[:, h, b % 2, q], Ss[:, h % 2, b, :], start=False, stop=(b == STREAMS - 1),
                                     skip_group_check=True)
                last.then_inc(so_full, 1)
                for q in range(4):
                    n = 4 * h + q
                    if n == 8:
                        pe.wait_ge(s_done, 2)
                    if n >= 4:
                        pe.wait_ge(ss_done, 2 * (n - 3))
                    rows_ = slice(32 * q, 32 * q + 32)
                    for odd in range(2):
                        last = pe.matmul(ps[:, KV_RING[q], odd * DV:(odd + 1) * DV], km[odd][rows_, tile(h)],
                                         vv[rows_, 4, h * DV:(h + 1) * DV], start=True, stop=True)
                    last.then_inc(skv_full, 1)

            def chunk(c):
                t, odd = divmod(c, 2)
                r0 = CHUNK * odd
                mine = slice(r0, r0 + CHUNK)
                if not odd:
                    pe.wait_ge(att_done, t + 1)
                    scores(t)
                if c == 0:
                    pe.wait_ge(ss_done, 4 * STREAMS // 2)
                    pe.wait_ge(cleared, 3)
                else:
                    pe.wait_ge(s_done, c)
                for h in range(HEADS):
                    last = pe.matmul(span(1, D)[:, h * DV:(h + 1) * DV], kend[mine, t, tile(h)],
                                     vv[mine, t, h * DV:(h + 1) * DV], start=True, stop=True)
                last.then_inc(kv_full, 1)
                pe.wait_ge(att_done, t + 2)
                if not odd:
                    pe.wait_ge(o_normed, O_NORMED[t] - 1)
                for h in range(HEADS):
                    out = span(3, D)[:, h * DV:(h + 1) * DV]
                    if not odd:
                        pe.matmul(out, att[:, t % 2, tile(h)], vv[:, t, h * DV:(h + 1) * DV], start=(h % 2 == 0), stop=False, skip_group_check=True)
                for h in range(HEADS):
                    out = span(3, D)[mine, h * DV:(h + 1) * DV]
                    last = pe.matmul(out, qk[:, h, c * CHUNK:(c + 1) * CHUNK], S[:, c % 2, h, :], start=False, stop=True, skip_group_check=True)
                last.then_inc(o_full, 1)

            def r_part(p, t, j):
                n, u = p * TT + t, U_R + 2 * p + j
                if j == 0:
                    if n < 2:
                        pe.wait_ge(ss_done, HEADS * STREAMS)
                    else:
                        pe.wait_ge(r_done, n - 1)
                pe.wait_ge(w_lo, u + 1)
                for k in range(KB):
                    for m, (w, mv_) in enumerate(((wh, xh), (wl, xh), (wh, xl))):
                        last = pe.matmul(ps[:, 5 + n % 2, j * UW:(j + 1) * UW], mv_[:, k, tile(t)], w[:, u % 2, k, :],
                                         start=(k == 0 and m == 0), stop=(k == KB - 1 and m == 2))
                if t == TT - 1:
                    last.then_inc(w_used, 1)
                elif j:
                    last.then_inc(r_tile_full, 1)

            def r_tile(p, t):
                for t_, j in {3: ((3, 0), (4, 0)), 4: ((3, 1), (4, 1))}.get(t, ((t, 0), (t, 1))):
                    r_part(p, t_, j)

            for what, *n in CORE:
                {"streams": streams, "chunk": chunk, "r": r_tile}[what](*n)
            pe.wait_ge(gated, TT)
            pe.wait_ge(o_normed, HEADS + 4)
            pe.wait_ge(s_done, 8)
            pe.wait_ge(r_done, 2 * TT)
            for k in range(KB):
                if k >= 4:
                    pe.wait_ge(xl_done, X_OUT1 + (1, 2, 5, 6)[k - 4])
                for t in range(TT):
                    last = pe.transpose(span(GATED_BANK[k])[:, tile(t)], rg[:, t, tile(k)], ident)
                last.then_inc(gated_full, 1)
            pe.wait_ge(xl_done, X_OUT1 + 4)
            for m in range(3):
                if m == 1:
                    pe.wait_ge(xl_done, X_OUT1 + KB)
                unit(U_OUT1 + m, G_OUT1 + m, xh, xl, ready=(lambda k: pe.wait_ge(xl_done, X_OUT1 + k + 1)) if m == 0 else None)
            last_y_unit(U_OUT1 + 3, BOUNDS[2], xh, xl, KB)
            boundary(BOUNDS[2], U_FF1)
            last_ffn(U_FF1, G_FF1, sum(n for _, n in FF_PARTS))

        @block.vector
        def _(dve):
            steps = [0]

            def step(ins, n=1):
                steps[0] += n
                ins.then_inc(dve_step, 1)
                dve.wait_ge(dve_step, steps[0])

            def lo(u, di=0):
                dve.wait_ge(w_hi, di + (u + 1))
                s = u % 2
                dve.tensor_tensor(wl[:, s].rearrange("p k c -> p (k c)"), stage[:, s, :],
                                  f32(wh[:, s].rearrange("p k c -> p (k c)")), ALU.subtract).then_inc(w_lo, 1)

            def scaled(dst, u, g, di=0):
                dve.wait_ge(w_used, di + (u + 1))
                dve.tensor_tensor(dst, banks4(g), rs_twice(), ALU.mult).then_inc(acc_empty, 1)

            def norm(n, src, dst, eyes, out):
                norm_ms(n, src, dst[0])
                norm_diag(n, dst[1], eyes, out)

            def norm_ms(n, src, dst):
                if n == PRE0:
                    dve.wait_ge(x0_sums, TT)
                else:
                    dve.wait_ge(sums_full, n)
                dve.tensor_scalar(dst, src, 1.0 / D, EPS, ALU.mult, ALU.add).then_inc(ms_done, 1)

            def norm_diag(n, r, eyes, out):
                dve.wait_ge(rstd_done, n + 1)
                shape = list(out.shape)
                dve.tensor_tensor(out, eyes.unsqueeze(1).broadcast_to(shape), r.unsqueeze(2).broadcast_to(shape), ALU.mult).then_inc(diag_done, 1)

            def norm_ahead(n, src):
                norm(n, src, (ms[:, 0:TT], rpre), ident, diag[:])

            def half_ms(B, h):
                cols = slice(h * GROUPS, (h + 1) * GROUPS)
                norm_ms(post_norm(B["n"], h), ps[0:HG, norm_banks(B["g"])[1][h], 0:GROUPS], ms[0:HG, cols])

            def half_diag(B, h):
                cols = slice(h * GROUPS, (h + 1) * GROUPS)
                norm_diag(post_norm(B["n"], h), rstd[0:HG, cols], ident[0:HG, 0:HG], diag64)

            def x_lo(B, i):
                dve.wait_ge(xh_done, B["x"] + i + 1)
                dve.scalar_tensor_tensor(half(xl, i), half(x, i), gain(B["gq"] + i % KB), f32(half(xh, i)), ALU.mult, ALU.subtract).then_inc(xl_done, 1)

            def y_out(u, g, m, add, di=0):
                dve.wait_ge(w_used, di + (u + 1))
                if add:
                    dve.tensor_tensor(two(y, m), two(y, m), banks4(g), ALU.add).then_inc(acc_empty, 1)
                else:
                    dve.tensor_copy(two(y, m), banks4(g)).then_inc(acc_empty, 1)

            def last_piece(B, add, m, h):
                dst, src = y[:, 6 + m, h * HALF:(h + 1) * HALF], banks4(B["g"] - 1)[:, m, h, :]
                return dve.tensor_tensor(dst, dst, src, ALU.add) if add else dve.tensor_copy(dst, src)

            def y_units(u, B, add):
                g, n = B["g"] - 4, B["n"]
                for m in range(3):
                    y_out(u + m, g + m, 2 * m, add)
                    lo(u + m + 2)
                    if m:
                        dve.wait_ge(squares, 7 * n + m + 1)
                        if m == 2:
                            dve.wait_ge(squares_added, 5 * n + 1)
                        dve.tensor_tensor(acc[:], acc[:], sq[:], ALU.add).then_inc(squares_added, 1)
                dve.wait_ge(squares_added, 5 * n + 2)
                dve.tensor_tensor(acc[:, 0], acc[:, 0], acc[:, 1], ALU.add).then_inc(squares_added, 1)
                for i, (m, h) in enumerate(((0, 0), (1, 0), (0, 1))):
                    dve.wait_ge(y_blocks_full, 3 * n + i + 1)
                    last_piece(B, add, m, h).then_inc(y_stands, 1)
                    if i:
                        cols = slice((i - 1) * HALF, i * HALF)
                        dve.wait_ge(squares, 7 * n + (4, 6)[i - 1])
                        dve.wait_ge(squares_added, 5 * n + 2 + i)
                        dve.tensor_tensor(acc[:, 0, cols], acc[:, 0, cols], sq[:, 0, cols], ALU.add).then_inc(squares_added, 1)
                half_ms(B, 0)
                half_diag(B, 0)

            def boundary(B, u, add):
                n = B["n"]
                for i in range(PIECES):
                    h, k = divmod(i, KB)
                    if k == 0:
                        dve.wait_ge(r_full, post_norm(n, h) + 1)
                    dve.scalar_tensor_tensor(half(y, i), half(y, i), gain(B["gp"] + k), ps[:, norm_banks(B["g"])[0][h], 0:HALF],
                                             ALU.mult, ALU.mult).then_inc(y_scaled, 1)
                    if i in ADDED_BY_DVE:
                        dve.wait_ge(y_scaled, PIECES * n + i + 1)
                        dve.tensor_tensor(half(x, i), half(x, i), half(y, i), ALU.add).then_inc(x_added_dve, 1)
                    if i == 0:
                        dve.wait_ge(w_used, u)
                        last_piece(B, add, 1, 1).then_inc(acc_empty, 1)
                    if i >= LAG:
                        x_lo(B, i - LAG)
                    if i == 4:
                        half_ms(B, 1)
                    elif i == 6:
                        half_diag(B, 1)
                    elif i == 9:
                        lo(u + 1)
                for i in range(PIECES - LAG, PIECES):
                    x_lo(B, i)
                dve.wait_ge(x_squares_first, n + 1)
                dve.wait_ge(x_squares, PIECES * n + 14)
                dve.tensor_tensor(acc[:], acc[:], y[:, 4:6], ALU.add).then_inc(x_squares_added, 1)
                dve.wait_ge(x_squares, PIECES * n + 16)
                dve.wait_ge(x_squares_added, 3 * n + 1)
                dve.tensor_tensor(acc[:], acc[:], y[:, 6:8], ALU.add).then_inc(x_squares_added, 1)
                dve.wait_ge(x_squares_added, 3 * n + 2)
                dve.tensor_tensor(acc[:, 0], acc[:, 0], acc[:, 1], ALU.add).then_inc(x_squares_added, 1)
                norm_ahead(pre_norm(n), ps[:, norm_banks(B["g"])[3], 0:TT])
                if n == 1:
                    lo(u + 2)
                dve.wait_ge(rs_done, 2 + n)

            def gate_up(u, g, pair, pairs):
                with dve.Fori(0, pairs) as i:
                    scaled(two(gate, 0), u, g, di=i * 2)
                    lo(u + 2, di=i * 2)
                    scaled(two(up, 0), u + 1, g + 1, di=i * 2)
                    dve.wait_ge(silu_done, i + (pair + 1))
                    dve.wait_ge(acc_empty, i * 2 + (g + 2))
                    dve.tensor_tensor(up[:], up[:], gate[:], ALU.mult).then_inc(hid_done, 1)
                    lo(u + 3, di=i * 2)
                    dve.wait_ge(hid_hi, i + (pair + 1))
                    dve.tensor_tensor(hl[:, bass.ds(i * 2, 2), :], up[:], f32(hh[:, bass.ds(i * 2, 2), :]), ALU.subtract).then_inc(hid_lo, 1)
                    dve.wait_ge(hid_lo, i + (pair + 1))

            def ffn(u, g, pair, B):
                for n, (f, pairs) in enumerate(FF_PARTS):
                    gate_up(u, g, pair, pairs)
                    u, g, pair = u + 2 * pairs, g + 2 * pairs, pair + pairs
                    if n < len(FF_PARTS) - 1:
                        with dve.Fori(0, 2) as i:
                            for j in range(2):
                                if n:
                                    dve.wait_ge(acc_empty, i * 2 + (g + j))
                                y_out(u + j, g + j, i * 4 + 2 * j, n > 0, di=i * 2)
                                lo(u + j + 2, di=i * 2)
                    else:
                        y_units(u, B, True)
                    u, g = u + 4, g + 4

            def y_tile(n, t, cols, add, bank):
                dst = yF[:, t, cols]
                ins = dve.tensor_tensor(dst, dst, ps[:, bank, 0:UW], ALU.add) if add else dve.tensor_copy(dst, ps[:, bank, 0:UW])
                ins.then_inc(y_tile_out, 1)

            def last_ffn(u, g, pair):
                for n, (f, pairs) in enumerate(FF_PARTS):
                    gate_up(u, g, pair, pairs)
                    u, g, pair = u + 2 * pairs, g + 2 * pairs, pair + pairs
                    if n < len(FF_PARTS) - 1:
                        with dve.Fori(0, 2) as i:
                            for j in range(2):
                                for t in range(TT):
                                    if j == 0 or t == TT - 1:
                                        if t in (0, TT - 1):
                                            dve.wait_ge(w_used, i * 2 + (u + j + 1))
                                    else:
                                        dve.wait_ge(y_tile_full, i * 4 + (8 * n + t + 1))
                                    y_tile(n, t, bass.ds(i * (2 * UW) + j * UW, UW), n > 0, tile_bank(j, t))
                                lo(u + j + 2, di=i * 2)
                        u += 4
                def final(t):
                    dve.wait_ge(tile_rstd, t + 1)
                    r = rstd[:, t:t + 1]
                    if t == 0:
                        dve.wait_ge(y_gained, 3 * TT)
                        dve.wait_ge(xF_done, TT)
                    rest, last = slice(UW, D - UW), slice(D - UW, D)
                    dve.scalar_tensor_tensor(yF[:, t, rest], yF[:, t, rest], r, xF[:, t, rest], ALU.mult, ALU.add)
                    dve.scalar_tensor_tensor(yF[:, t, last], yg[:, t, :], r, xF[:, t, last], ALU.mult, ALU.add).then_inc(out_ready, 1)

                for m in range(4):
                    for t in range(TT):
                        if m % 2 == 0 or t == TT - 1:
                            dve.wait_ge(w_used, u + m + 1)
                        else:
                            dve.wait_ge(y_tile_full, 8 * n + 4 * (m // 2) + t + 1)
                        y_tile(n, t, slice(m * UW, (m + 1) * UW), True, tile_bank(m % 2, t))
                        if m < 3:
                            continue
                        dve.wait_ge(y_tile_out, 20 * n + 5 * m + t + 1)
                        dve.tensor_tensor(yg[:, t, :], yF[:, t, D - UW:], gF[:, D - UW:], ALU.mult)
                        if t == 0:
                            dve.wait_ge(y_tile_sq, 3 * TT)
                            step(dve.tensor_tensor(ss[:, 0:5], ss[:, 0:5], ss[:, 5:10], ALU.add))
                            step(dve.tensor_tensor(ss[:, 0:5], ss[:, 0:5], ss[:, 10:15], ALU.add))
                            step(dve.tensor_scalar(ss[:, 0:5], ss[:, 0:5], 1.0 / D, EPS, ALU.mult, ALU.add))
                        else:
                            final(t - 1)
                        dve.wait_ge(y_tile_sq, 3 * TT + t + 1)
                        dve.scalar_tensor_tensor(ms[:, t:t + 1], ss[:, 15 + t:16 + t], 1.0 / D, ss[:, t:t + 1], ALU.mult, ALU.add).then_inc(tile_ms, 1)
                    if m == 3:
                        final(TT - 1)
                    if u + m + 2 < UNITS:
                        lo(u + m + 2)

            dve.memset(ones[:], 1.0).then_inc(consts_set, 1)
            dve.memset(minus_half, -0.5).then_inc(consts_set, 1)
            dve.wait_ge(rows_full, 1)
            dve.tensor_copy(gains[:], ps[:, 0, 0:ROWS]).then_inc(rows_done, 1)
            dve.wait_ge(rows_done, 1)
            def x0_low(t):
                dve.wait_ge(x0_hi, t + 1)
                dve.tensor_tensor(xl[:, :, tile(t)], xg[:, t % 2], f32(xh[:, :, tile(t)]), ALU.subtract).then_inc(x0_lo, 1)

            for t in range(TT):
                dve.wait_ge(x0_full, t + 1)
                if t >= 2:
                    dve.wait_ge(x0_lo, t - 1)
                dve.tensor_tensor(xg[:, t % 2], span(4 + 2 * (t % 2), D).rearrange("p (k n) -> p k n", n=P),
                                  gains[:, PRE_MIX:PRE_MIX + KB].unsqueeze(2).broadcast_to([P, KB, P]), ALU.mult).then_inc(xg_done, 1)
                if t:
                    x0_low(t - 1)
                if t == 3:
                    lo(0)
            x0_low(TT - 1)
            norm_ahead(PRE0, ss[:, 0:TT])
            lo(1)

            dve.wait_ge(rs_done, 1)
            stream_r = rs[:, PROMPT:].rearrange("p (b s) -> p b s", s=STEP)
            for u in range(4):
                if u < 2:
                    dve.wait_ge(w_used, u + 1)
                    src = banks4(u)
                    dst = winA[:, 2 * u:2 * u + 2, :]
                    n = PROMPT - HALF
                    dve.tensor_tensor(dst[:, :, 16:16 + HALF], src[:, :, 0, :], rs[:, 0:HALF].unsqueeze(1).broadcast_to([P, 2, HALF]), ALU.mult)
                    dve.tensor_tensor(dst[:, :, 16 + HALF:16 + PROMPT], src[:, :, 1, 0:n],
                                      rs[:, HALF:PROMPT].unsqueeze(1).broadcast_to([P, 2, n]), ALU.mult)
                    for m in range(2):
                        last = dve.tensor_tensor(dst[:, m, 16 + PROMPT:].rearrange("p (b s) -> p b s", s=32)[:, :, 16:],
                                                 src[:, m, 1, n:].rearrange("p (b s) -> p b s", s=STEP), stream_r, ALU.mult)
                    last.then_inc(acc_empty, 1)
                else:
                    scaled(two(uT, 2 * (u - 2)), u, u)
                if u == 2:
                    dve.wait_ge(hist_full, 1)
                    dve.wait_ge(zeroed, 3)
                    dve.tensor_copy(winA[:, :, 16 + PROMPT:].rearrange("p g (b s) -> p g b s", s=32)[:, :, :, 1:16],
                                    ps[:, 7, :].rearrange("p (g n) -> p g n", g=4)[:, :, 0:STREAMS * HIST].rearrange("p g (b s) -> p g b s", s=HIST)).then_inc(hist_done, 1)
                lo(u + 2)
            dve.wait_ge(small_loads, 16 * SMALL_LOADS)
            dve.tensor_copy(bs[:, 1, :].rearrange("p (h b s) -> p h b s", h=4, s=STEP),
                            bs[:, 0, :].rearrange("p (h t) -> p h t", h=4)[:, :, 0:STEP].unsqueeze(2).broadcast_to([P, 4, STREAMS, STEP]))
            for n in range(2):
                dve.wait_ge(ws_full, n + 1)
                dve.tensor_tensor(wsT[:, n], ps[:, 5 + n, :].rearrange("p (h t) -> p h t", h=4),
                                  tri[:, 2 * n:2 * n + 1, :].broadcast_to([P, 4, P]), ALU.mult).then_inc(ws_done, 1)
            dve.wait_ge(windows_done, 1)
            for gr, w in enumerate(WINDOWS):
                s = (winB, winC)[gr % 2][:, gr, :]
                own = winA[:, gr, :]
                dve.scalar_tensor_tensor(s[:, 16:16 + PROMPT], s[:, 16:16 + PROMPT], 1.0 / w, own[:, 16:16 + PROMPT], ALU.mult, ALU.subtract).then_inc(pooled_done, 1)
                s, own = (t_[:, 16 + PROMPT:].rearrange("p (b s) -> p b s", s=32)[:, :, 16:] for t_ in (s, own))
                dve.scalar_tensor_tensor(s, s, 1.0 / w, own, ALU.mult, ALU.subtract).then_inc(pooled_done, 1)
            lo(U_OUT0)
            def v_stats(t):
                m = mv[:, 2 * (t % 2):2 * (t % 2) + 2]
                dve.wait_ge(v_gelu, t + 1)
                step(dve.bn_stats(bn6, gv[:, t % 2, :]))
                step(dve.bn_aggr(m, bn6))
                dve.tensor_scalar(vms[:, t % 2:t % 2 + 1], m[:, 1:2], EPS, None, ALU.add).then_inc(vms_done, 1)
            v_stats(0)
            for t in range(TT):
                if t + 1 < TT:
                    v_stats(t + 1)
                dve.wait_ge(vrstd_done, t + 1)
                dve.tensor_scalar(v[:, t, :], gv[:, t % 2, :], mv[:, 2 * (t % 2):2 * (t % 2) + 1], vrstd[:, t:t + 1], ALU.subtract, ALU.mult).then_inc(v_normed, 1)
                dve.wait_ge(v_normed, t + 1)
                dve.tensor_tensor(v[:, t, :], v[:, t, :], lng[:], ALU.mult).then_inc(v_gained, 1)
            for gr, b in enumerate((6, 4, 0, 2)):
                dve.wait_ge(xh_done, X_OUT0 + gr + 1)
                dve.scalar_tensor_tensor(xl[:, gr, :], span(b), gain(POOL_SCALE + gr), f32(xh[:, gr, :]), ALU.mult, ALU.subtract).then_inc(xl_done, 1)
            dve.wait_ge(u_done, 2)

            def yb_low(t):
                dve.wait_ge(yb_hi, t + 1)
                dve.tensor_tensor(xl[:, 4:8, tile(t)], uT[:, :, tile(t)], f32(xh[:, 4:8, tile(t)]), ALU.subtract).then_inc(yb_lo, 1)
            for t, b in enumerate((6, 7, 4, 5, 6)):
                dve.wait_ge(yb_full, t + 1)
                step(dve.tensor_tensor(ps[:, b, :], ps[:, b, :], bs[:, int(t == 4), :], ALU.add))
                dve.tensor_tensor(uT[:, :, tile(t)], ps[:, b, :].rearrange("p (h t) -> p h t", h=4), uT[:, :, tile(t)], ALU.mult).then_inc(yb_done, 1)
                if t:
                    yb_low(t - 1)
            yb_low(TT - 1)
            lo(U_OUT0 + 1)
            dve.wait_ge(mixer_stores, 16 * MIXER_STORES)
            y_units(U_OUT0, BOUNDS[0], False)
            boundary(BOUNDS[0], U_FF0, False)
            ffn(U_FF0, G_FF0, 0, BOUNDS[1])
            boundary(BOUNDS[1], U_QK, True)

            for j, u in enumerate(U_QKS):
                scaled(two(qk, 2 * j), u, G_QKS[j])
                if j:
                    lo(u + 2)
                else:
                    dve.wait_ge(w_used, U_G + 1)
                    dve.tensor_tensor(halved(zf[:]), banks4(G_G)[:, 0], halved(rs[:]), ALU.mult).then_inc(acc_empty, 1)
                    lo(U_G + 2)
                if j == 1:
                    for t, b in enumerate((6, 7, 4, 5, 6)):
                        dve.wait_ge(gate_full, t + 1)
                        dve.tensor_tensor(la[:, t, :], ps[:, b, :], bg[:], ALU.add).then_inc(gx_done, 1)
                    dve.wait_ge(gx_done, TT)
                    step(dve.tensor_scalar(lmin[:], la[:], 0.0, None, ALU.min))
                    dve.scalar_tensor_tensor(la[:], lmin[:], -2.0, la[:], ALU.mult, ALU.add).then_inc(gabs_done, 1)
                if j == 2:
                    dve.wait_ge(gln_done, 1)
                    dve.tensor_tensor(la[:], lmin[:], la[:], ALU.subtract).then_inc(la_done, 1)
            for h in range(HEADS):
                dve.wait_ge(cum_done, h + 1)
                ends = bend.rearrange("p (n c) -> p n c", n=2)
                c = cum[:, h, :]
                prompt = c[:, 0:PROMPT].rearrange("p (c s) -> p c s", s=CHUNK)
                each = c[:, PROMPT:].rearrange("p (b s) -> p b s", s=STEP)
                dve.tensor_copy(ends[:, 0, :].unsqueeze(2), prompt[:, :, CHUNK - 1:])
                dve.tensor_copy(ends[:, 1, :].unsqueeze(2), each[:, :, STEP - 1:]).then_inc(bend_done, 1)
                dve.wait_ge(bend_done, h + 1)
                dve.wait_ge(exps_done, h + 1)
                dve.tensor_tensor(prompt, ends[:, 0, :].unsqueeze(2).broadcast_to([P, 8, CHUNK]), prompt, ALU.subtract)
                dve.tensor_tensor(each, ends[:, 1, :].unsqueeze(2).broadcast_to([P, 8, STEP]), each, ALU.subtract).then_inc(dist_done, 1)
                dve.scalar_tensor_tensor(qk[:, h, :], qk[:, h, :], DK ** -0.5, eq[:], ALU.mult, ALU.mult)
                dve.wait_ge(dist_exp, h + 1)
                dve.tensor_tensor(c, c, qk[:, 4 + h, :], ALU.mult)
                dve.tensor_tensor(qk[:, 4 + h, :], qk[:, 4 + h, :], ek[:], ALU.mult).then_inc(head_done, 1)
                if h < 3:
                    lo(U_VV + h + 2)
            for h, b in enumerate(KT_BANK):
                dve.wait_ge(kt_full, h + 1)
                for n in range(2):
                    last = dve.tensor_scalar(km[n][:, tile(h)], span(b)[:, tile(4)], par[:, n:n + 1], None, ALU.mult)
                last.then_inc(km_done, 1)
            dve.wait_ge(cleared, 3)
            norms, squared = [0], [0]

            def masked(n, slot, mask):
                dve.wait_ge(att_full, n + 1)
                dve.copy_predicated(att[:, slot, :].rearrange("p (h t) -> p h t", h=HEADS),
                                    tri[:, mask:mask + 1, :].bitcast(U32).broadcast_to([P, HEADS, P]),
                                    ps[:, 0, :].rearrange("p (h t) -> p h t", h=HEADS)).then_inc(att_done, 1)

            def normed(t, heads):
                norms[0] += 1
                n, c0 = norms[0], 4 * t + heads[0]
                squared[0] += len(heads)
                dve.wait_ge(o_squared, squared[0])
                cols = slice(c0, c0 + len(heads))
                dve.tensor_scalar(ms[:, cols], ss[:, cols], 1.0 / DV, EPS, ALU.mult, ALU.add).then_inc(o_ms, 1)
                dve.wait_ge(o_rstd, n)
                for h in heads:
                    src = span(3, D)[:, h * DV:(h + 1) * DV] if len(heads) > 1 else ps[:, SO_BANK[h % 2], 0:DV]
                    last = dve.tensor_scalar(qk[:, 2 * h:2 * h + 2, tile(t)], src.rearrange("p (v n) -> p v n", v=2),
                                             rstd[:, 4 * t + h:4 * t + h + 1], None, ALU.mult)
                last.then_inc(o_normed, 1)

            for what, *n in CORE:
                if what == "streams":
                    h, = n
                    if h == 0:
                        masked(0, 2, 2)
                        lo(U_R + 1)
                    dve.wait_ge(so_full, h + 1)
                    for q in range(4):
                        dve.wait_ge(skv_full, 4 * h + q + 1)
                        for odd in range(2):
                            b = 2 * q + odd
                            dve.scalar_tensor_tensor(Ss[:, h % 2, b, :], Ss[:, h % 2, b, :], elast[:, h, STREAMS + b:STREAMS + b + 1],
                                                     ps[:, KV_RING[q], odd * DV:(odd + 1) * DV], ALU.mult, ALU.add).then_inc(ss_done, 1)
                    normed(4, [h])
                elif what == "chunk":
                    c, = n
                    t, odd = divmod(c, 2)
                    if not odd:
                        if t >= 2:
                            dve.wait_ge(o_full, 2 * t - 2)
                        masked(t + 1, t % 2, 1)
                    dve.wait_ge(kv_full, c + 1)
                    if c:
                        dve.wait_ge(o_full, c)
                        dve.wait_ge(s_done, c)
                    for h in range(HEADS):
                        last = dve.scalar_tensor_tensor(S[:, 1 - odd, h, :], S[:, odd, h, :], elast[:, h, c:c + 1],
                                                        span(1, D)[:, h * DV:(h + 1) * DV], ALU.mult, ALU.add)
                    last.then_inc(s_done, 1)
                    if odd:
                        normed(t, list(range(HEADS)))
                    if c == 4:
                        lo(U_R + 2)
                else:
                    p, t = n
                    for tt in {3: (), 4: (3, 4)}.get(t, (t,)) if p else ():
                        dve.wait_ge(r_done, TT + tt + 1)
                        dve.wait_ge(o_normed, len(_NORMS) if tt > 1 else O_NORMED[tt])
                        dve.tensor_tensor(rg[:, tt, :].rearrange("p (k n) -> p k n", n=P), rg[:, tt, :].rearrange("p (k n) -> p k n", n=P),
                                          qk[:, :, tile(tt)], ALU.mult).then_inc(gated, 1)
                    if (p, t) == (1, 3):
                        lo(U_OUT1)
                    elif (p, t) == (0, 4):
                        lo(U_R + 3)
            for k in range(KB):
                dve.wait_ge(xh_done, X_OUT1 + k + 1)
                dve.scalar_tensor_tensor(xl[:, k, :], span(GATED_BANK[k]), gain(O_NORM + k), f32(xh[:, k, :]), ALU.mult, ALU.subtract).then_inc(xl_done, 1)
            lo(U_OUT1 + 1)
            y_units(U_OUT1, BOUNDS[2], False)
            boundary(BOUNDS[2], U_FF1, False)
            dve.wait_ge(prompt_out, 16)
            dve.wait_ge(gain_load, 16)
            last_ffn(U_FF1, G_FF1, sum(n for _, n in FF_PARTS))

        @block.scalar
        def _(act):
            def hi(u, di=0):
                s = u % 2
                n = di * 8 if not isinstance(di, int) else 0
                act.wait_ge(w_loaded[s], n + 16 * (u // 2 + 1))
                if u >= 2:
                    act.wait_ge(w_used, di + (u - 1))
                act.activation(wh[:, s].rearrange("p k c -> p (k c)"), stage[:, s, :], ACT.Copy).then_inc(w_hi, 1)

            def y_units(u, B):
                n, g = B["n"], B["g"] - 4
                for m in range(3):
                    hi(u + m + 2)
                    act.wait_ge(acc_empty, g + m + 1)
                    if m == 2:
                        act.wait_ge(squares_added, 5 * n + 1)
                    act.activation((acc, sq, sq)[m][:], y[:, 2 * m:2 * m + 2, :], ACT.Square).then_inc(squares, 1)
                act.wait_ge(squares_added, 5 * n + 2)
                for i, (m, h) in enumerate(((0, 0), (1, 0), (0, 1))):
                    act.wait_ge(y_stands, 3 * n + i + 1)
                    square_piece(m, h)

            def square_piece(m, h):
                cols = slice(h * HALF, (h + 1) * HALF)
                act.activation(sq[:, m, cols], y[:, 6 + m, cols], ACT.Square).then_inc(squares, 1)

            def rs_copy(n, b):
                act.wait_ge(r_full, n + 1)
                act.activation(halved(rs[:]), ps[:, b:b + 2, 0:HALF], ACT.Copy).then_inc(rs_done, 1)

            def boundary(B, u):
                n, squared = B["n"], 0
                for i in range(PIECES):
                    wait_x_added(act, n, i)
                    act.activation(half(xh, i), half(x, i), ACT.Copy, scale=gain(B["gq"] + i % KB)).then_inc(xh_done, 1)
                    if i == 0:
                        act.wait_ge(acc_empty, B["g"])
                        square_piece(1, 1)
                    elif i == 3:
                        hi(u + 1)
                    target = i - 3 if i < 12 else 2 * i - 15 if i < PIECES - 1 else PIECES
                    while squared < target:
                        act.activation(half(y, squared), half(x, squared), ACT.Square).then_inc(x_squares, 1)
                        squared += 1
                if n == 1:
                    hi(u + 2)
                rs_copy(pre_norm(n), norm_banks(B["g"])[2])

            def gate_up(u, g, pair, pairs):
                with act.Fori(0, pairs) as i:
                    hi(u + 2, di=i * 2)
                    act.wait_ge(acc_empty, i * 2 + (g + 1))
                    act.activation(gate[:], gate[:], ACT.Silu).then_inc(silu_done, 1)
                    hi(u + 3, di=i * 2)
                    act.wait_ge(hid_done, i + (pair + 1))
                    act.activation(hh[:, bass.ds(i * 2, 2), :], up[:], ACT.Copy).then_inc(hid_hi, 1)

            def ffn(u, g, pair, B):
                for n, (f, pairs) in enumerate(FF_PARTS):
                    gate_up(u, g, pair, pairs)
                    u, g, pair = u + 2 * pairs, g + 2 * pairs, pair + pairs
                    if n < len(FF_PARTS) - 1:
                        with act.Fori(0, 2) as i:
                            for j in range(2):
                                hi(u + j + 2, di=i * 2)
                    else:
                        y_units(u, B)
                    u, g = u + 4, g + 4

            def first_columns(t):
                act.wait_ge(tile_rstd, t + 1)
                act.activation(yF[:, t, 0:UW], yF[:, t, 0:UW], ACT.Copy, scale=rstd[:, t:t + 1]).then_inc(first_scaled, 1)

            def last_ffn(u, g, pair):
                for n, (f, pairs) in enumerate(FF_PARTS):
                    gate_up(u, g, pair, pairs)
                    u, g, pair = u + 2 * pairs, g + 2 * pairs, pair + pairs
                    if n < len(FF_PARTS) - 1:
                        with act.Fori(0, 2) as i:
                            for j in range(2):
                                hi(u + j + 2, di=i * 2)
                        u += 4
                for t in range(TT):
                    act.wait_ge(xF_full, t + 1)
                    act.activation(xF[:, t, :], span(tile_bank(1, 0), D), ACT.Copy).then_inc(xF_done, 1)
                for m in range(4):
                    if u + m + 2 < UNITS:
                        hi(u + m + 2)
                    for t in range(TT):
                        act.wait_ge(y_tile_out, 20 * n + 5 * m + t + 1)
                        if m or t:
                            act.wait_ge(y_tile_sq, 5 * m + t)
                        act.activation(rs[:, 0:UW], yF[:, t, m * UW:(m + 1) * UW], ACT.Square,
                                       accum_out=ss[:, 5 * m + t:5 * m + t + 1]).then_inc(y_tile_sq, 1)
                        if m == 3 and t:
                            first_columns(t - 1)
                first_columns(TT - 1)

            for t in range(TT):
                act.wait_ge(xg_done, t + 1)
                act.activation(xh[:, :, tile(t)], xg[:, t % 2], ACT.Copy).then_inc(x0_hi, 1)
                act.wait_ge(x0_full, t + 1)
                act.activation(x[:, :, tile(t)], span(4 + 2 * (t % 2), D).rearrange("p (k n) -> p k n", n=P), ACT.Copy).then_inc(x0_done, 1)
                if t == 0:
                    hi(0)
            for t in range(TT):
                if t:
                    act.wait_ge(x0_sums, t)
                act.activation(junk[:], xin[:, t, :], ACT.Square, accum_out=ss[:, t:t + 1]).then_inc(x0_sums, 1)
            hi(1)
            rs_copy(0, 6)
            for u in range(4):
                hi(u + 2)
                if u >= 2:
                    act.wait_ge(acc_empty, u + 1)
                    act.activation(uT[:, 2 * (u - 2):2 * (u - 1), :], uT[:, 2 * (u - 2):2 * (u - 1), :], ACT.Gelu_apprx_tanh).then_inc(u_done, 1)
            act.activation(a_last[:].rearrange("p g (b s) -> p g b s", s=STEP),
                           winA[:, :, 16 + PROMPT:].rearrange("p g (b s) -> p g b s", s=32)[:, :, :, 16:], ACT.Copy).then_inc(a_last_done, 1)
            hi(U_OUT0)
            act.wait_ge(last_a_full, 1)
            act.activation(a_out[0:HIST, 0, :], ps[0:HIST, 7, :], ACT.Copy).then_inc(last_a_done, 1)
            act.activation(a_out[:, 1, :], ps[:, 5, :], ACT.Copy).then_inc(last_a_done, 1)
            act.wait_ge(last_a_done, 2)
            act.dma_start(a["pool_prompt"][0, 0], a_out[0:HIST, 0, :]).then_inc(mixer_stores, 16)
            for b in range(STREAMS):
                act.dma_start(a["pool_sample"][0, b], a_out[b * STEP + 1:(b + 1) * STEP, 1, :]).then_inc(mixer_stores, 16)
            for t in range(TT):
                if t < 4:
                    act.wait_ge(v_full, t + 1)
                else:
                    act.wait_ge(w_used, U_V + 2)
                if t >= 2:
                    act.wait_ge(v_normed, t - 1)
                act.activation(gv[:, t % 2, :], ps[:, t, :], ACT.Gelu_apprx_tanh, scale=rpre[:, t:t + 1]).then_inc(v_gelu, 1)
            hi(U_OUT0 + 1)
            for gr, b in enumerate((6, 4, 0, 2)):
                act.wait_ge(ya_full, gr + 1)
                act.activation(xh[:, gr, :], span(b), ACT.Copy, scale=gain(POOL_SCALE + gr)).then_inc(xh_done, 1)
            for t in range(TT):
                act.wait_ge(yb_done, t + 1)
                act.activation(xh[:, 4:8, tile(t)], uT[:, :, tile(t)], ACT.Copy).then_inc(yb_hi, 1)
            act.wait_ge(v_done, TT)
            act.dma_start(a["sg_v_sample"][0].rearrange("b s d -> (b s) d"), v[:, 4, :]).then_inc(mixer_stores, 16)
            act.wait_ge(mixer_stores, 16 * MIXER_STORES)
            y_units(U_OUT0, BOUNDS[0])
            boundary(BOUNDS[0], U_FF0)
            ffn(U_FF0, G_FF0, 0, BOUNDS[1])
            boundary(BOUNDS[1], U_QK)
            hi(U_QK + 3)
            hi(U_QK + 4)
            act.wait_ge(gabs_done, 1)
            act.activation(la[:], la[:], ACT.Exp, scale=-1.0).then_inc(act_step, 1)
            act.wait_ge(act_step, 1)
            act.activation(la[:], la[:], ACT.Ln, bias=1.0).then_inc(gln_done, 1)
            hi(U_QK + 5)
            hi(U_QK + 6)
            for h, b in enumerate((4, 6, 0, 2)):
                act.wait_ge(cum_full, h + 1)
                act.activation(cum[:, h, :], span(b), ACT.Copy, scale=1.0 / TAU).then_inc(cum_done, 1)

            def exps(h):
                act.wait_ge(cum_done, h + 1)
                if h:
                    act.wait_ge(head_done, h)
                act.activation(eq[:], cum[:, h, :], ACT.Exp)
                act.activation(ek[:], cum[:, h, :], ACT.Exp, scale=-1.0)
                act.wait_ge(bend_done, h + 1)
                act.activation(elast[:, h, :], bend, ACT.Exp).then_inc(exps_done, 1)
                act.wait_ge(dist_done, h + 1)
                act.activation(cum[:, h, :], cum[:, h, :], ACT.Exp).then_inc(dist_exp, 1)

            def v_copy(p, banks):
                for t, b in enumerate(banks):
                    if t < 4:
                        act.wait_ge(vv_full, 4 * p + t + 1)
                    else:
                        act.wait_ge(w_used, U_VV + 2 * p + 2)
                    act.activation(vv[:, t, p * 512:(p + 1) * 512], ps[:, b, :], ACT.Copy, scale=rpre[:, t:t + 1]).then_inc(vv_done, 1)
            exps(0)
            hi(U_VV + 2)
            exps(1)
            v_copy(0, (4, 5, 6, 7, 2))
            hi(U_VV + 3)
            exps(2)
            hi(U_VV + 4)
            exps(3)
            v_copy(1, (6, 7, 2, 0, 1))
            for h, b in enumerate(KT_BANK):
                act.wait_ge(kt_full, h + 1)
                act.activation(kend[:, 0:4, tile(h)], span(b)[:, 0:PROMPT].rearrange("p (t n) -> p t n", n=P), ACT.Copy).then_inc(kt_done, 1)
            hi(U_R + 1)
            norms = [0]
            for what, *n in CORE:
                if what == "r":
                    p, t = n
                    if (p, t) == (0, 0):
                        for sem_ in states_out:
                            act.wait_ge(sem_, 16 * HEADS // 2)
                    for tt in {3: (), 4: (3, 4)}.get(t, (t,)):
                        if tt < 4:
                            act.wait_ge(r_tile_full, 4 * p + tt + 1)
                        else:
                            act.wait_ge(w_used, U_R + 2 * p + 2)
                        act.activation(rg[:, tt, p * 512:(p + 1) * 512], ps[:, 5 + (p * TT + tt) % 2, :], ACT.Silu, scale=rpre[:, tt:tt + 1]).then_inc(r_done, 1)
                    if t == 3:
                        hi(U_R + 2 * p + 2)
                    elif t == 4 and p == 0:
                        hi(U_R + 3)
                    continue
                if what == "streams":
                    heads, t = n, 4
                    act.wait_ge(so_full, n[0] + 1)
                elif n[0] % 2:
                    heads, t = range(HEADS), n[0] // 2
                    act.wait_ge(o_full, n[0] + 1)
                else:
                    continue
                for h in heads:
                    src = ps[:, SO_BANK[h % 2], 0:DV] if what == "streams" else span(3, D)[:, h * DV:(h + 1) * DV]
                    if norms[0]:
                        act.wait_ge(o_squared, norms[0])
                    norms[0] += 1
                    act.activation(rs[:, 0:DV], src, ACT.Square, accum_out=ss[:, 4 * t + h:4 * t + h + 1]).then_inc(o_squared, 1)
            for k in range(KB):
                act.wait_ge(gated_full, k + 1)
                act.activation(xh[:, k, :], span(GATED_BANK[k]), ACT.Copy, scale=gain(O_NORM + k)).then_inc(xh_done, 1)
            hi(U_OUT1 + 1)
            y_units(U_OUT1, BOUNDS[2])
            boundary(BOUNDS[2], U_FF1)
            last_ffn(U_FF1, G_FF1, sum(n for _, n in FF_PARTS))

        @block.gpsimd
        def _(pool):
            steps = [0]

            def step(ins):
                steps[0] += 1
                ins.then_inc(pool_step, 1)
                pool.wait_ge(pool_step, steps[0])

            def norm(n, dst, src):
                pool.wait_ge(ms_done, n + 1)
                pool.tensor_tensor(dst, src, minus_half[0:src.shape[0], 0:src.shape[1]], ALU.pow).then_inc(rstd_done, 1)

            def norm_ahead(n):
                norm(n, rpre, ms[:, 0:TT])

            def norm_half(B, h):
                cols = slice(h * GROUPS, (h + 1) * GROUPS)
                norm(post_norm(B["n"], h), rstd[0:HG, cols], ms[0:HG, cols])

            def boundary(B):
                n = B["n"]
                norm_half(B, 0)
                for i in range(PIECES):
                    if i not in ADDED_BY_DVE:
                        pool.wait_ge(y_scaled, PIECES * n + i + 1)
                        pool.tensor_tensor(half(x, i), half(x, i), half(y, i), ALU.add).then_inc(x_added_pool, 1)
                    if i == 4:
                        norm_half(B, 1)
                pool.wait_ge(x_squares, PIECES * n + 12)
                pool.tensor_tensor(acc[:], y[:, 0:2], y[:, 2:4], ALU.add).then_inc(x_squares_first, 1)
                norm_ahead(pre_norm(n))

            pool.memset(wsn[:, 1], 0.0).then_inc(zeroed, 1)
            pool.memset(winA[:, :, 0:16], 0.0).then_inc(zeroed, 1)
            pool.memset(winA[:, :, 16 + PROMPT:].rearrange("p g (b s) -> p g b s", s=32)[:, :, :, 0:1], 0.0).then_inc(zeroed, 1)
            pool.dma_start(cst[:, P:], a["consts"][:, P:]).then_inc(small_loads, 16)
            w_s = a["w_s"][0].rearrange("h t s -> t h s")
            pool.dma_start(wsn[:, 0], w_s).then_inc(small_loads, 16)
            pool.dma_start(hist[0:STREAMS * HIST, :], a["state_pool"][0].rearrange("b s d -> (b s) d")).then_inc(small_loads, 16)
            pool.wait_ge(zeroed, 1)
            for b in range(STREAMS):
                pool.dma_start(wsn[b * STEP:(b + 1) * STEP, 1, :, b * STEP:(b + 1) * STEP], w_s[0:STEP, :, 0:STEP]).then_inc(small_loads, 16)
            pool.dma_start(bs[:, 0, :], a["b_s"][0].rearrange("h t -> (h t)").partition_broadcast(P)).then_inc(small_loads, 16)
            pool.dma_start(wpool[:], a["w_pool"][0].rearrange("g c d -> c g d")).then_inc(small_loads, 16)
            pool.dma_start(lng[:], a["ln_v_g"][0].partition_broadcast(P)).then_inc(small_loads, 16)
            pool.dma_start(lnb[:], a["ln_v_b"][0].partition_broadcast(P)).then_inc(small_loads, 16)
            pool.wait_ge(consts_set, 2)
            norm_ahead(PRE0)
            pool.wait_ge(acc_empty, 2)
            pool.wait_ge(hist_done, 1)
            for n, (src, dst) in enumerate(((winA, winB), (winB, winC), (winC, winB), (winB, winC))):
                w, s0 = 1 << n, (2 << n) - 1
                step(pool.tensor_tensor(dst[:, n:4, s0:], src[:, n:4, s0:], src[:, n:4, s0 - w:AW - w], ALU.add))
            for gr in range(4):
                s = (winB, winC)[gr % 2][:, gr, 16:32]
                last = pool.tensor_tensor(s, s, fix[:, gr, :], ALU.mult)
            last.then_inc(windows_done, 1)
            for t in range(TT):
                pool.wait_ge(vms_done, t + 1)
                pool.tensor_tensor(vrstd[:, t:t + 1], vms[:, t % 2:t % 2 + 1], minus_half[:, 0:1], ALU.pow).then_inc(vrstd_done, 1)
                if t:
                    pool.wait_ge(v_gained, t)
                    pool.tensor_tensor(v[:, t - 1, :], v[:, t - 1, :], lnb[:], ALU.add).then_inc(v_done, 1)
            pool.wait_ge(v_gained, TT)
            pool.tensor_tensor(v[:, TT - 1, :], v[:, TT - 1, :], lnb[:], ALU.add).then_inc(v_done, 1)
            pool.wait_ge(yb_full, TT)
            pool.wait_ge(v_done, TT)
            pool.memset(w2[:], 0.0).then_inc(w2_zeroed, 1)
            pool.wait_ge(w2_zeroed, 1)
            pool.dma_start(w2[P - 16:P, :], a["w_gate2"][0]).then_inc(gate_loads, 16)
            pool.dma_start(bg[:], a["b_gate"][0].partition_broadcast(P)).then_inc(gate_loads, 16)
            boundary(BOUNDS[0])
            boundary(BOUNDS[1])
            def states_load(h):
                pool.dma_start(Ss[:, h % 2], a["state_gla"][0, :, h].rearrange("b k v -> k b v")).then_inc(states_in[h % 2], 16)

            pool.wait_ge(cum_full, HEADS)
            states_load(0)
            states_load(1)
            pool.wait_ge(head_done, HEADS)
            pool.memset(att[:], 0.0).then_inc(cleared, 1)
            step(pool.memset(qm[:], 0.0))
            q4 = qk[:, 0:HEADS, tile(4)].rearrange("p h (q two s) -> p h q two s", two=2, s=STEP)
            m4 = qm[:].rearrange("p h o (q two s) -> p h o q two s", two=2, s=STEP)
            for n in range(2):
                for h in range(HEADS):
                    last = pool.tensor_copy(m4[:, h, n, :, n, :], q4[:, h, :, n, :])
            last.then_inc(cleared, 1)
            pool.wait_ge(kt_full, HEADS)
            pool.memset(S[:, 0], 0.0).then_inc(cleared, 1)
            norms = 0
            for what, *n in CORE:
                if what == "r" or (what == "chunk" and n[0] % 2 == 0):
                    continue
                norms += 1
                c0, heads = (16 + n[0], 1) if what == "streams" else (4 * (n[0] // 2), HEADS)
                pool.wait_ge(o_ms, norms)
                pool.tensor_tensor(rstd[:, c0:c0 + heads], ms[:, c0:c0 + heads], minus_half[:, 0:heads], ALU.pow).then_inc(o_rstd, 1)
                if what == "streams":
                    h = n[0]
                    pool.wait_ge(ss_done, STREAMS * (h + 1))
                    pool.dma_start(a["gla_sample"][0, :, h].rearrange("b k v -> k b v"), Ss[:, h % 2]).then_inc(states_out[h % 2], 16)
                    if h == 1:
                        for g in range(2):
                            pool.wait_ge(states_out[g], 16)
                            states_load(2 + g)
            pool.wait_ge(s_done, 8)
            pool.dma_start(a["gla_prompt"][0, 0].rearrange("h k v -> k h v"), S[:, 0]).then_inc(prompt_out, 16)
            pool.dma_start(gF[:], a["post_ffn_g"][1].partition_broadcast(P)).then_inc(gain_load, 16)
            boundary(BOUNDS[2])
            def first_columns(t):
                pool.wait_ge(first_scaled, t + 1)
                pool.tensor_tensor(yF[:, t, 0:UW], yF[:, t, 0:UW], xF[:, t, 0:UW], ALU.add).then_inc(first_ready, 1)

            pool.wait_ge(gain_load, 16)
            for m in range(3):
                for t in range(TT):
                    pool.wait_ge(y_tile_sq, 5 * m + t + 1)
                    cols = slice(m * UW, (m + 1) * UW)
                    pool.tensor_tensor(yF[:, t, cols], yF[:, t, cols], gF[:, cols], ALU.mult).then_inc(y_gained, 1)
            for t in range(TT):
                pool.wait_ge(tile_ms, t + 1)
                pool.tensor_tensor(rstd[:, t:t + 1], ms[:, t:t + 1], minus_half[:, 0:1], ALU.pow).then_inc(tile_rstd, 1)
                if t:
                    first_columns(t - 1)
            first_columns(TT - 1)


def constants():
    s, t = np.indices((P, P))
    masks = [(s <= t) & (s // n == t // n) for n in (P, CHUNK, STEP)]
    frames = np.arange(16)
    fix = [w / np.minimum(w, frames + 1) for w in WINDOWS]
    odd = (np.arange(P) // STEP) % 2
    parts = [np.eye(P), *masks, np.broadcast_to(np.concatenate(fix), (P, 64)), np.stack([1 - odd, odd], 1)]
    return np.concatenate([np.asarray(x, np.float32) for x in parts], 1)


_OUTS = {
    "y_prompt": (1, PROMPT, D), "y_sample": (STREAMS, STEP, D),
    "pool_prompt": (1, 1, HIST, SG), "pool_sample": (1, STREAMS, HIST, SG),
    "sg_v_sample": (1, STREAMS, STEP, SG),
    "gla_prompt": (1, 1, HEADS, DK, DV), "gla_sample": (1, STREAMS, HEADS, DK, DV),
}


def kernel(**inputs):
    import concourse.bacc as bacc
    from concourse.bass_utils import run_bass_kernel_spmd

    nc = bacc.Bacc("TRN2", target_bir_lowering=False, num_devices=1)
    arrays = {name: np.ascontiguousarray(x) for name, x in inputs.items()}
    arrays["consts"] = constants()
    aps = {name: nc.dram_tensor(name, x.shape, mybir.dt.from_np(x.dtype), kind="ExternalInput").ap() for name, x in arrays.items()}
    for name, shape in _OUTS.items():
        aps[name] = nc.dram_tensor(name, shape, F32, kind="ExternalOutput").ap()
    encoder(nc, aps)
    r = run_bass_kernel_spmd(nc, [arrays], core_ids=[0])
    return tuple(r.results[0][name] for name in _OUTS)
```
